# Optimizing a Trainium2 kernel written in Bass

```python
import jax, jax.numpy as jnp
from jax import lax
import numpy as np

D_MODEL = 1024
BATCH = 1
SEQ = 512
DEPTH = 1

CHUNK = 64
POOL_WIDTH = 512
POOL_WINDOWS = (2, 4, 8, 16)
POOL_GROUPS = len(POOL_WINDOWS)
POOL_GROUP_DIM = POOL_WIDTH // POOL_GROUPS
MLSTM_WIDTH = 1024
MLSTM_HEADS = 4
MLSTM_HEAD_DIM = MLSTM_WIDTH // MLSTM_HEADS
CONV_WIDTH = 4
N_BRANCHES = 2
SPLITS = (POOL_WIDTH,
          POOL_WIDTH + MLSTM_WIDTH,
          POOL_WIDTH + 2 * MLSTM_WIDTH,
          POOL_WIDTH + 3 * MLSTM_WIDTH,
          POOL_WIDTH + 3 * MLSTM_WIDTH + 2 * MLSTM_HEADS)
IN_COLS = SPLITS[-1] + N_BRANCHES * D_MODEL
N_EXPERTS = 32
TOP_K = 4
D_FF = D_MODEL
SWIGLU_ALPHA = 1.702
SWIGLU_LIMIT = 7.0
EXPERT_BLOCK = 128
LN_EPS = 1e-5
DEEPNORM_ALPHA = (2.0 * DEPTH) ** 0.25
DEEPNORM_BETA = (8.0 * DEPTH) ** -0.25

kernel_name = 'hybrid_pool_mlstm_moe_encoder'

def layer_norm(x, g, b):
    xf = x.astype(jnp.float32)
    mu = xf.mean(-1, keepdims=True)
    var = jnp.square(xf - mu).mean(-1, keepdims=True)
    return ((xf - mu) * lax.rsqrt(var + LN_EPS) * g + b).astype(x.dtype)

def pool_mixer(p, w_pool, b_pool, ls_pool):
    B, S, _ = p.shape
    pf = p.astype(jnp.float32)
    cs = jnp.pad(jnp.cumsum(pf, axis=1), ((0, 0), (1, 0), (0, 0)))
    t = jnp.arange(S)
    outs = []
    for gi, w in enumerate(POOL_WINDOWS):
        sl = slice(gi * POOL_GROUP_DIM, (gi + 1) * POOL_GROUP_DIM)
        csg = cs[:, :, sl]
        start = jnp.maximum(t + 1 - w, 0)
        win_sum = csg[:, 1:] - csg[:, start]
        cnt = jnp.minimum(t + 1, w).astype(jnp.float32)[None, :, None]
        outs.append(win_sum / cnt - pf[:, :, sl])
    pooled = jnp.stack(outs, axis=2).astype(p.dtype)
    mixed = jnp.einsum('bsgc,gcd->bsgd', pooled, w_pool).reshape(B, S, POOL_WIDTH) + b_pool
    return mixed * ls_pool

def causal_depthwise_conv(u, w, b):
    C = u.shape[-1]
    y = lax.conv_general_dilated(u, w[:, None, :].astype(u.dtype), window_strides=(1,),
                                 padding=[(CONV_WIDTH - 1, 0)],
                                 dimension_numbers=('NWC', 'WIO', 'NWC'),
                                 feature_group_count=C)
    return y + b

def mlstm_chunkwise(q, k, v, i_pre, f_pre):
    B, H, S, Dh = q.shape
    nc = S // CHUNK

    def to_chunks(a):
        return jnp.moveaxis(a.reshape(B, H, nc, CHUNK, *a.shape[3:]), 2, 0)

    log_f = jax.nn.log_sigmoid(f_pre)
    xs = (to_chunks(q), to_chunks(k), to_chunks(v), to_chunks(i_pre), to_chunks(log_f))
    causal = jnp.tril(jnp.ones((CHUNK, CHUNK), dtype=bool))

    def step(carry, inp):
        C, n, m = carry
        qc, kc, vc, ic, lfc = inp
        b = jnp.cumsum(lfc, axis=-1)
        d_log = jnp.where(causal, b[..., :, None] - b[..., None, :] + ic[..., None, :], -jnp.inf)
        m_inter = b + m[..., None]
        m_t = jnp.maximum(m_inter, d_log.max(-1))
        w_intra = jnp.exp(d_log - m_t[..., None])
        s = jnp.einsum('bhtd,bhsd->bhts', qc, kc) * w_intra
        w_inter = jnp.exp(m_inter - m_t)
        num = (jnp.einsum('bhts,bhse->bhte', s, vc)
               + w_inter[..., None] * jnp.einsum('bhed,bhtd->bhte', C, qc))
        den = s.sum(-1) + w_inter * jnp.einsum('bhd,bhtd->bht', n, qc)
        h = num / jnp.maximum(jnp.abs(den), jnp.exp(-m_t))[..., None]
        g = b[..., -1]
        w_log = g[..., None] - b + ic
        m_new = jnp.maximum(g + m, w_log.max(-1))
        decay = jnp.exp(g + m - m_new)
        w_state = jnp.exp(w_log - m_new[..., None])
        C_new = decay[..., None, None] * C + jnp.einsum('bhse,bhsd->bhed', vc * w_state[..., None], kc)
        n_new = decay[..., None] * n + jnp.einsum('bhs,bhsd->bhd', w_state, kc)
        return (C_new, n_new, m_new), h

    init = (jnp.zeros((B, H, Dh, Dh), jnp.float32),
            jnp.zeros((B, H, Dh), jnp.float32),
            jnp.zeros((B, H), jnp.float32))
    _, h = lax.scan(step, init, xs)
    return jnp.moveaxis(h, 0, 2).reshape(B, H, S, Dh)

def hybrid_mixer(xn, w_in, conv_w, conv_b, w_q, w_k, b_if, mh_gain, w_pool, b_pool, ls_pool,
                 w_branch_pool, w_branch_mlstm, w_out):
    B, S, _ = xn.shape
    H, Dh = MLSTM_HEADS, MLSTM_HEAD_DIM
    proj = xn @ w_in
    p, u, v, o_pre, if_pre, gates = jnp.split(proj, list(SPLITS), axis=-1)
    y_pool = pool_mixer(p, w_pool, b_pool, ls_pool) @ w_branch_pool
    uc = jax.nn.silu(causal_depthwise_conv(u, conv_w, conv_b)).reshape(B, S, H, Dh)
    q = jnp.einsum('bshd,hde->bhse', uc, w_q) * (Dh ** -0.5)
    k = jnp.einsum('bshd,hde->bhse', uc, w_k)
    vh = v.reshape(B, S, H, Dh).transpose(0, 2, 1, 3)
    gif = (if_pre + b_if).astype(jnp.float32)
    i_pre = gif[..., :H].transpose(0, 2, 1)
    f_pre = gif[..., H:].transpose(0, 2, 1)
    h = mlstm_chunkwise(q.astype(jnp.float32), k.astype(jnp.float32), vh.astype(jnp.float32), i_pre, f_pre)
    h = h.transpose(0, 2, 1, 3)
    mu = h.mean(-1, keepdims=True)
    var = jnp.square(h - mu).mean(-1, keepdims=True)
    hn = ((h - mu) * lax.rsqrt(var + LN_EPS)).reshape(B, S, MLSTM_WIDTH) * mh_gain
    h_out = (jax.nn.sigmoid(o_pre.astype(jnp.float32)) * hn).astype(xn.dtype)
    y_mlstm = h_out @ w_branch_mlstm
    g = jax.nn.sigmoid(gates.astype(jnp.float32)).reshape(B, S, N_BRANCHES, D_MODEL).astype(xn.dtype)
    merged = g[:, :, 0] * y_pool + g[:, :, 1] * y_mlstm
    return merged @ w_out

def clamped_swiglu(h):
    x_glu, x_lin = h[..., ::2], h[..., 1::2]
    x_glu = jnp.minimum(x_glu, SWIGLU_LIMIT)
    x_lin = jnp.clip(x_lin, -SWIGLU_LIMIT, SWIGLU_LIMIT)
    return x_glu * jax.nn.sigmoid(SWIGLU_ALPHA * x_glu) * (x_lin + 1.0)

def moe_ffn(x, w_router, b_router, w_e1, b_e1, w_e2, b_e2):
    B, S, D = x.shape
    T = B * S
    xt = x.reshape(T, D)
    logits = (xt @ w_router + b_router).astype(jnp.float32)
    top_val, top_idx = lax.top_k(logits, TOP_K)
    gate = jax.nn.softmax(top_val, axis=-1).astype(x.dtype)
    A = T * TOP_K
    e_flat = top_idx.reshape(A).astype(jnp.int32)
    tok_flat = jnp.arange(A, dtype=jnp.int32) // TOP_K
    g_flat = gate.reshape(A)
    order = jnp.argsort(e_flat, stable=True)
    e_sorted = e_flat[order]
    counts = jnp.zeros((N_EXPERTS,), jnp.int32).at[e_flat].add(1)
    padded = (counts + EXPERT_BLOCK - 1) // EXPERT_BLOCK * EXPERT_BLOCK
    start = jnp.cumsum(counts) - counts
    padded_end = jnp.cumsum(padded)
    padded_start = padded_end - padded
    rank = jnp.arange(A, dtype=jnp.int32) - start[e_sorted]
    dest = padded_start[e_sorted] + rank
    n_rows = -(-(A + N_EXPERTS * (EXPERT_BLOCK - 1)) // EXPERT_BLOCK) * EXPERT_BLOCK
    n_blocks = n_rows // EXPERT_BLOCK
    row_tok = jnp.zeros((n_rows,), jnp.int32).at[dest].set(tok_flat[order])
    row_gate = jnp.zeros((n_rows,), x.dtype).at[dest].set(g_flat[order])
    block_e = jnp.minimum(
        jnp.searchsorted(padded_end, jnp.arange(n_blocks, dtype=jnp.int32) * EXPERT_BLOCK, side='right'),
        N_EXPERTS - 1).astype(jnp.int32)
    x_rows = xt[row_tok].reshape(n_blocks, EXPERT_BLOCK, D)

    def expert_block(args):
        xb, e = args
        hb = xb @ w_e1[e] + b_e1[e]
        return clamped_swiglu(hb) @ w_e2[e] + b_e2[e]

    y_rows = lax.map(expert_block, (x_rows, block_e)).reshape(n_rows, D)
    y = jnp.zeros((T, D), x.dtype).at[row_tok].add(y_rows * row_gate[:, None])
    return y.reshape(B, S, D)

def setup_inputs(seed: int = 0) -> dict:
    key = jax.random.key(seed)
    ks = jax.random.split(key, 32)
    f32 = jnp.float32
    L, D, H = DEPTH, D_MODEL, MLSTM_HEADS

    def nrm(k, shape, scale):
        return jax.random.normal(k, shape, f32) * scale

    b_if = jnp.concatenate([
        nrm(ks[8], (L, H), 0.1),
        jnp.broadcast_to(jnp.linspace(3.0, 6.0, H, dtype=f32), (L, H)) + nrm(ks[9], (L, H), 0.1)], axis=-1)
    return {
        'x': nrm(ks[0], (BATCH, SEQ, D), 1.0),
        'ln0_g': 1.0 + nrm(ks[1], (D,), 0.02),
        'ln0_b': nrm(ks[2], (D,), 0.02),
        'w_in': nrm(ks[3], (L, D, IN_COLS), D ** -0.5),
        'conv_w': nrm(ks[4], (L, CONV_WIDTH, MLSTM_WIDTH), CONV_WIDTH ** -0.5),
        'conv_b': nrm(ks[5], (L, MLSTM_WIDTH), 0.02),
        'w_q': nrm(ks[6], (L, H, MLSTM_HEAD_DIM, MLSTM_HEAD_DIM), MLSTM_HEAD_DIM ** -0.5),
        'w_k': nrm(ks[7], (L, H, MLSTM_HEAD_DIM, MLSTM_HEAD_DIM), MLSTM_HEAD_DIM ** -0.5),
        'b_if': b_if,
        'mh_gain': 1.0 + nrm(ks[10], (L, MLSTM_WIDTH), 0.02),
        'w_pool': nrm(ks[11], (L, POOL_GROUPS, POOL_GROUP_DIM, POOL_GROUP_DIM), POOL_GROUP_DIM ** -0.5),
        'b_pool': nrm(ks[12], (L, POOL_WIDTH), 0.02),
        'ls_pool': 1.0 + nrm(ks[13], (L, POOL_WIDTH), 0.02),
        'w_branch_pool': nrm(ks[14], (L, POOL_WIDTH, D), POOL_WIDTH ** -0.5),
        'w_branch_mlstm': nrm(ks[15], (L, MLSTM_WIDTH, D), MLSTM_WIDTH ** -0.5),
        'w_out': nrm(ks[16], (L, D, D), D ** -0.5 * DEEPNORM_BETA),
        'ln1_g': 1.0 + nrm(ks[17], (L, D), 0.02),
        'ln1_b': nrm(ks[18], (L, D), 0.02),
        'w_router': nrm(ks[19], (L, D, N_EXPERTS), D ** -0.5),
        'b_router': nrm(ks[20], (L, N_EXPERTS), 0.01),
        'w_e1': nrm(ks[21], (L, N_EXPERTS, D, 2 * D_FF), D ** -0.5),
        'b_e1': nrm(ks[22], (L, N_EXPERTS, 2 * D_FF), 0.02),
        'w_e2': nrm(ks[23], (L, N_EXPERTS, D_FF, D), D_FF ** -0.5 * DEEPNORM_BETA),
        'b_e2': nrm(ks[24], (L, N_EXPERTS, D), 0.02),
        'ln2_g': 1.0 + nrm(ks[25], (L, D), 0.02),
        'ln2_b': nrm(ks[26], (L, D), 0.02),
    }

def reference(x, ln0_g, ln0_b, w_in, conv_w, conv_b, w_q, w_k, b_if, mh_gain, w_pool, b_pool, ls_pool,
              w_branch_pool, w_branch_mlstm, w_out, ln1_g, ln1_b, w_router, b_router, w_e1, b_e1,
              w_e2, b_e2, ln2_g, ln2_b):
    h = layer_norm(x, ln0_g, ln0_b)
    for l in range(DEPTH):
        mix = hybrid_mixer(h, w_in[l], conv_w[l], conv_b[l], w_q[l], w_k[l], b_if[l], mh_gain[l],
                           w_pool[l], b_pool[l], ls_pool[l], w_branch_pool[l], w_branch_mlstm[l], w_out[l])
        h = layer_norm(DEEPNORM_ALPHA * h + mix, ln1_g[l], ln1_b[l])
        ffn = moe_ffn(h, w_router[l], b_router[l], w_e1[l], b_e1[l], w_e2[l], b_e2[l])
        h = layer_norm(DEEPNORM_ALPHA * h + ffn, ln2_g[l], ln2_b[l])
    return h


_drawn_inputs = setup_inputs


def setup_inputs(seed=0):
    import zlib

    import numpy as np

    out = dict(_drawn_inputs(seed))
    spreads = {}
    factors = {'conv_b': 6.122,
     'mh_gain': 18.121,
     'b_pool': 4.089,
     'ls_pool': 16.832,
     'b_router': 3.82,
     'b_e1': 8.0,
     'b_e2': 6.422,
     'ln2_g': 22.238,
     'ln2_b': 22.134}
    for name, (base, spread) in spreads.items():
        noise = np.random.default_rng([zlib.crc32(name.encode()), seed]).standard_normal(out[name].shape)
        drawn = base * np.exp(spread * noise) if base else spread * noise
        out[name] = __import__('jax').numpy.asarray(drawn.astype(out[name].dtype))
    for name, factor in factors.items():
        out[name] = (out[name] * factor).astype(out[name].dtype)
    return out
```

```python
from contextlib import ExitStack

import concourse.bass as bass
from concourse import mybir

F32 = mybir.dt.float32
U32 = mybir.dt.uint32
I32 = mybir.dt.int32
ALU = mybir.AluOpType
ACT = mybir.ActivationFunctionType
X_AXIS = mybir.AxisListType.X

P = 128
BANK = 512


def build_program(nc, A, out):
    _, S, D = A["x"].shape
    NT = S // P
    KD = D // P
    _, TAPS, MW = A["conv_w"].shape
    _, H, DH, _ = A["w_q"].shape
    _, PG, PGD, _ = A["w_pool"].shape
    PW = PG * PGD
    _, _, E = A["w_router"].shape
    FF = A["w_e2"].shape[2]
    KF = FF // P
    MC = MW // P
    EC = DH // P
    TOPK = 4
    LN_EPS = 1e-5
    DEEP_ALPHA = 2.0 ** 0.25
    GLU_ALPHA = 1.702
    GLU_LIMIT = 7.0
    COL_P, COL_U, COL_V, COL_O = 0, PW, PW + MW, PW + 2 * MW
    COL_IF = PW + 3 * MW
    COL_G = COL_IF + 2 * H
    PANEL = 2 * P
    RING = 4
    WINDOWS = [2 ** (g + 1) for g in range(PG)]
    PAD = WINDOWS[-1]
    CPAD = TAPS - 1
    UST = S + CPAD + 1
    PST = S + PAD
    VW = DH + 1
    CAP = P
    ROUNDS = S // CAP
    ROUND_ROWS = E * CAP
    LIST_ROWS = ROUNDS * ROUND_ROWS + CAP
    NO_TOKEN = 1 << 20
    CG = 4
    TB = P // CG
    NB = CAP // TB
    HW_ = 2 * FF // CG
    YW = D // CG
    assert DH == PANEL and HW_ == BANK and NT == 4 and KD == 8

    w_in = A["w_in"][0]
    w_in_k = w_in.rearrange("(k p) n -> p k n", p=P)
    x_rows = A["x"][0]
    out_rows = out[0]

    x1_dram = nc.dram_tensor("x1_rows", (S, D), F32, kind="Internal").ap()
    list_dram = nc.dram_tensor("token_lists", (LIST_ROWS, 1), U32, kind="Internal").ap()
    y_dram = nc.dram_tensor("expert_rows", (S, TOPK, D), F32, kind="Internal").ap()
    y_quarters = y_dram.rearrange("t k (g n) -> (t k g) n", g=CG)

    with ExitStack() as ctx:
        def sb(name, cols, dt=F32, parts=P):
            return ctx.enter_context(nc.sbuf_tensor(name, [parts, cols], dt))

        def sem(name):
            return ctx.enter_context(nc.semaphore(name))

        X0 = sb("X0", NT * D)
        gain = sb("ln_gain", D)
        bias = sb("ln_bias", D)
        W1_COLS, W2_COLS = KD * 2 * FF, KF * D
        big = sb("big", W1_COLS + W2_COLS + 128)
        rest = sb("rest", 12288)
        x1T = sb("x1T", KD * S)
        P1 = sb("P1", NT * S)
        hn = sb("hn", NT * DH)
        ident = sb("ident", P)
        tri = sb("tri", P)
        tri_strict = sb("tri_strict", P)
        ones = sb("ones", BANK)
        head_sel = sb("head_sel", H * P)
        chan_rows = sb("chan_rows", P)
        chan = sb("chan", 64)
        gate_b = sb("gate_b", 2)
        m_line = sb("m_line", S)
        cols = sb("gate_cols", NT * 2 * H)
        wif = sb("w_if", KD * 2 * H)
        inv_cnt = sb("inv_cnt", PAD)
        stat = sb("stat", 96)
        wr = sb("w_router_sb", KD * E)
        br = sb("b_router_sb", E)
        top = sb("top", NT * 8)
        topi = sb("topi", NT * 8, U32)
        topf = sb("topf", NT * TOPK)
        gatew = sb("gatew", NT * TOPK)
        gsum = sb("gsum", 2 * NT)
        rint = chan_rows[:, 0:NT * E].bitcast(I32)
        iota_e = sb("iota_e", E)
        iota_pos = sb("iota_pos", E)
        pos = sb("pos", TOPK * NT)
        posu = sb("posu", TOPK * NT, U32)
        slot_id = sb("slot_id", TOPK * NT, U32)
        slot = sb("slot", NB, U32)
        quarter = sb("quarter", 1)
        cnt = sb("cnt", E + 8)
        more_iter = sb("more_iter", 1, I32)
        idx = sb("idx", 1, U32)

        def cut(t, at, *shape):
            n = 1
            for s in shape:
                n *= s
            v = t[:, at:at + n]
            if len(shape) == 2:
                return v.rearrange("p (a b) -> p a b", a=shape[0])
            if len(shape) == 3:
                return v.rearrange("p (a b c) -> p a b c", a=shape[0], b=shape[1])
            return v

        X0v = cut(X0, 0, NT, D)
        h0T = cut(big, 0, KD, S)
        uT = cut(big, 4096, MC, UST)
        hnT = uT
        v_sb = cut(big, 8224, NT, H, VW)
        mixT = cut(big, 12336, PG, S)
        pT = cut(big, 14384, PG, PST)
        P0 = cut(big, 14384, NT, S)
        pool_w = cut(big, 16496, PG, S)
        qT = cut(big, 16496, EC, S)
        kT = cut(big, 17520, EC, S)
        wqk = cut(big, 18544, 2 * H, EC, DH)
        wtmp = cut(big, 22640, 1280)
        wout = cut(big, 14384, KD, D)
        sig = cut(big, 22640, 2, 2 * BANK)
        ring = cut(rest, 0, RING, KD, PANEL)
        ucT = cut(rest, 8192, MC, S)
        mergedT = ucT
        MS = (2 * KD + PG + MC) * P
        merge_w = [cut(x1T, 0, 2 * KD + PG + MC, P), cut(rest, 0, 2 * KD + PG + MC, P)]
        x1Tv = cut(x1T, 0, KD, S)
        Pm = [P0, cut(P1, 0, NT, S)]
        hnv = cut(hn, 0, NT, DH)
        m_row = m_line[0:H, :]
        no_token = x1T[:, 5 * S:5 * S + LIST_ROWS // P].bitcast(U32)
        a_row, f_row, em_row, t0_row, t1_row = (x1T[0:H, S * n:S * (n + 1)] for n in range(5))
        wpool = big[:, 23920:23920 + PG * PGD]
        onehot = hn[:, 0:TOPK * NT * E]
        logits, mask, rank, rtmp = (hn[:, NT * E * n:NT * E * (n + 1)] for n in range(TOPK, TOPK + 4))
        colv = cut(cols, 0, NT, 2 * H)
        wrv = cut(wr, 0, KD, E)
        W1 = cut(big, 0, KD, 2 * FF)
        W2 = cut(big, W1_COLS, KF // 2, 2, D)
        xg = cut(rest, 0, D)
        xT = cut(rest, 1024, KD, P)
        b1t = cut(rest, 2048, HW_)
        b2t = cut(rest, 2560, YW)
        hS = cut(rest, 2816, NB, HW_)
        gS = cut(rest, 4864, NB, HW_ // 2)
        lS = cut(rest, 5888, NB, HW_ // 2)
        sS = cut(rest, 6912, NB, HW_ // 2)
        aS = cut(rest, 7936, NB, 2, P)
        aT = cut(rest, 8960, NB, 2, P)
        yS = cut(rest, 9984, NB, YW)
        yg = cut(big, 0, NT, TOPK, D)
        acc = cut(rest, 0, 2, D)

        ps = ctx.enter_context(nc.psum_tensor("ps", [P, 8, BANK], F32))

        x_landed = [sem(f"x_landed{i}") for i in range(NT)]
        ln_landed = sem("ln_landed")
        small_landed = sem("small_landed")
        wif_landed = sem("wif_landed")
        wpool_landed = sem("wpool_landed")
        wqk_landed = sem("wqk_landed")
        wout_landed = sem("wout_landed")
        router_landed = sem("router_landed")
        ring_landed = [sem(f"ring_landed{i}") for i in range(RING)]
        merge_landed = [sem(f"merge_landed{i}") for i in range(2)]
        pool_step = sem("pool_step")
        pool_mark = sem("pool_mark")
        consts_made = sem("consts_made")
        pads_made = sem("pads_made")
        dve_step = sem("dve_step")
        act_step = sem("act_step")
        h0_ready = sem("h0_ready")
        var_ready = sem("var_ready")
        rstd_ready = sem("rstd_ready")
        h0_tr = sem("h0_tr")
        h0T_ready = sem("h0T_ready")
        chan_tr = sem("chan_tr")
        chan_ready = sem("chan_ready")
        if_done = sem("if_done")
        log_ready = sem("log_ready")
        tot_ready = sem("tot_ready")
        em_ready = sem("em_ready")
        rows_tr = sem("rows_tr")
        cols_ready = sem("cols_ready")
        gemm_done = sem("gemm_done")
        gemm_out = sem("gemm_out")
        pooled_ready = sem("pooled_ready")
        mix_done = sem("mix_done")
        mixT_ready = sem("mixT_ready")
        conv_ready = sem("conv_ready")
        silu_ready = sem("silu_ready")
        mb_done = sem("mb_done")
        arg_ready = sem("arg_ready")
        w_ready = sem("w_ready")
        sc_done = sem("sc_done")
        p_ready = sem("p_ready")
        pv_done = sem("pv_done")
        num_read = sem("num_read")
        hn_ready = sem("hn_ready")
        hout_ready = sem("hout_ready")
        gate_done = sem("gate_done")
        gate_ready = sem("gate_ready")
        y_done = sem("y_done")
        merged_ready = sem("merged_ready")
        wo_done = sem("wo_done")
        wo_read = sem("wo_read")
        x1_ready = sem("x1_ready")
        x1_stored = sem("x1_stored")
        x1_tr = sem("x1_tr")
        x1T_ready = sem("x1T_ready")
        logits_done = sem("logits_done")
        router_exp = sem("router_exp")
        dist_ready = sem("dist_ready")
        mask_ready = sem("mask_ready")
        rank_done = sem("rank_done")
        pos_ready = sem("pos_ready")
        iter_ready = sem("iter_ready")
        list_cleared = sem("list_cleared")
        list_stored = sem("list_stored")
        idx_landed = sem("idx_landed")
        idx_ready = sem("idx_ready")
        slot_landed = sem("slot_landed")
        slot_ready = sem("slot_ready")
        xg_landed = sem("xg_landed")
        w1_landed = [sem(f"w1_landed{k}") for k in range(KD)]
        w2_landed = [sem(f"w2_landed{k}") for k in range(KF // 2)]
        b1_landed = sem("b1_landed")
        b2_landed = sem("b2_landed")
        w1_used = sem("w1_used")
        w2_used = sem("w2_used")
        x_tr = sem("x_tr")
        xT_ready = sem("xT_ready")
        h_read = sem("h_read")
        swiglu_step = sem("swiglu_step")
        sig_ready = sem("sig_ready")
        lin_ready = sem("lin_ready")
        act_ready = sem("act_ready")
        act_tr = sem("act_tr")
        actT_ready = sem("actT_ready")
        y_ready = sem("y_ready")
        y_stored = sem("y_stored")
        yg_landed = [sem(f"yg_landed{i}") for i in range(NT)]
        tail_act = sem("tail_act")
        ln2_landed = sem("ln2_landed")
        ln1_landed = sem("ln1_landed")
        out_ready = sem("out_ready")
        out_stored = sem("out_stored")

        PANELS = ([("p", COL_P + PANEL * n, n) for n in range(PW // PANEL)]
                  + [("u", COL_U + PANEL * n, n) for n in range(MW // PANEL)]
                  + [("v", COL_V + PANEL * n, n) for n in range(H)]
                  + [("o", COL_O + PANEL * n, n) for n in range(MW // PANEL)])
        N_PU = PW // P + MC
        N_V = H * NT
        PER_HEAD = 2 * EC + EC

        def gemm_at_qk(h):
            return N_PU + N_V + (0 if h == 0 else 2 * EC + PER_HEAD * (h - 1))

        def gemm_at_tr(h):
            return N_PU + N_V + 2 * EC * min(h + 2, H) + EC * h

        GEMM_O = N_PU + N_V + H * PER_HEAD

        def panel_end(n):
            n_pu, n_v = PW // PANEL + MW // PANEL, H
            if n < n_pu:
                return 2 * (n + 1)
            if n < n_pu + n_v:
                return N_PU + NT * (n - n_pu + 1)
            return GEMM_O + 2 * (n - n_pu - n_v + 1)
        S_AT = [(2, 0), (3, 0), (4, 0), (4, 256)]
        NORM0, NORM_H = 0, NT
        NORM1 = NORM_H + H * NT
        NORM2 = NORM1 + NT
        W_AT = [0, 512, 896, 1152]

        block = ctx.enter_context(nc.Block())

        @block.sync
        def _(sp):
            for i in range(NT):
                sp.dma_start(X0v[:, i, :], x_rows[P * i:P * (i + 1), :]).then_inc(x_landed[i], 16)
                if i == 0:
                    sp.dma_start(gain[:], A["ln0_g"].rearrange("(a d) -> a d", a=1).broadcast_to([P, D])).then_inc(ln_landed, 16)
                    sp.dma_start(bias[:], A["ln0_b"].rearrange("(a d) -> a d", a=1).broadcast_to([P, D])).then_inc(ln_landed, 16)
            sp.dma_start(cut(wif, 0, KD, 2 * H), w_in_k[:, :, COL_IF:COL_IF + 2 * H]).then_inc(wif_landed, 16)
            for n, (_, c0, _) in enumerate(PANELS):
                if n >= RING:
                    sp.wait_ge(gemm_done, panel_end(n - RING))
                sp.dma_start(ring[:, n % RING], w_in_k[:, :, c0:c0 + PANEL]).then_inc(ring_landed[n % RING], 16)
                if n == 3:
                    sp.wait_ge(h0_ready, NT)
                    sp.dma_start(gain[:], A["ln1_g"].broadcast_to([P, D])).then_inc(ln1_landed, 16)
                    sp.dma_start(bias[:], A["ln1_b"].broadcast_to([P, D])).then_inc(ln1_landed, 16)
                if n == 5:
                    sp.dma_start(cut(wpool, 0, PG, PGD), A["w_pool"][0].rearrange("g c d -> c g d")).then_inc(wpool_landed, 16)
                if n == 7:
                    for h in range(H):
                        for j, name in enumerate(("w_q", "w_k")):
                            sp.dma_start(wqk[:, 2 * h + j], A[name][0, h].rearrange("(c p) e -> p c e", p=P)).then_inc(wqk_landed, 16)
            w_bp = A["w_branch_pool"][0].rearrange("(k p) n -> p k n", p=P)
            w_bm = A["w_branch_mlstm"][0].rearrange("(k p) n -> p k n", p=P)
            for m in range(KD):
                s = m % 2
                if m == 0:
                    sp.wait_ge(cols_ready, 1)
                    sp.wait_ge(list_cleared, 16)
                if m == 1:
                    sp.wait_ge(gemm_done, GEMM_O + MC)
                    sp.wait_ge(hn_ready, H * NT)
                    sp.dma_start(wout, A["w_out"][0].rearrange("(k p) n -> p k n", p=P)).then_inc(wout_landed, 16)
                if m >= 2:
                    sp.wait_ge(y_done, m - 1)
                t = merge_w[s]
                for k0, src in ((0, w_in_k[:, :, COL_G + P * m:COL_G + P * (m + 1)]),
                                (KD, w_in_k[:, :, COL_G + D + P * m:COL_G + D + P * (m + 1)]),
                                (2 * KD, w_bp[:, :, P * m:P * (m + 1)]),
                                (2 * KD + PG, w_bm[:, :, P * m:P * (m + 1)])):
                    nk = src.shape[1]
                    sp.dma_start(t[:, k0:k0 + nk, :], src).then_inc(merge_landed[s], 16)
            sp.wait_ge(merged_ready, KD)

            def load_w1(it, e, first=False):
                for k in range(KD):
                    if first:
                        if k == KD - 1:
                            sp.wait_ge(wo_done, NT)
                    else:
                        sp.wait_ge(w1_used, KD * it - KD + k + 1)
                    sp.dma_start(W1[:, k, :], A["w_e1"][0, e, P * k:P * (k + 1), :]).then_inc(w1_landed[k], 16)
                sp.wait_ge(h_read, it) if not first else sp.wait_ge(rank_done, 1)
                for g in range(CG):
                    sp.dma_start(b1t[TB * g:TB * (g + 1), :],
                                 A["b_e1"][0, bass.ds(e, 1), HW_ * g:HW_ * (g + 1)].broadcast_to([TB, HW_])).then_inc(b1_landed, 16)

            def load_w2(it, e, first=False):
                for k in range(KF // 2):
                    if not first:
                        sp.wait_ge(w2_used, (KF // 2) * it - KF // 2 + k + 1)
                    sp.dma_start(W2[:, k], A["w_e2"][0, e, 2 * P * k:2 * P * (k + 1), :].rearrange("(a p) n -> p a n", p=P)).then_inc(w2_landed[k], 16)
                if not first:
                    sp.wait_ge(y_ready, it + 1)
                for g in range(CG):
                    sp.dma_start(b2t[TB * g:TB * (g + 1), :],
                                 A["b_e2"][0, bass.ds(e, 1), YW * g:YW * (g + 1)].broadcast_to([TB, YW])).then_inc(b2_landed, 16)

            load_w1(0, 0, first=True)
            load_w2(0, 0, first=True)
            sp.wait_ge(iter_ready, 1)
            n_it = sp.snap(sp.value_load(more_iter[0:1, 0:1], min_val=0, max_val=(ROUNDS - 1) * E) + E)
            with sp.Fori(1, n_it) as it:
                e = sp.snap(it % E)
                load_w1(it, e)
                load_w2(it, e)

            for i in range(NT):
                sp.wait_ge(out_ready, i + 1)
                sp.dma_start(out_rows[P * i:P * (i + 1), :], X0v[:, i, :]).then_inc(out_stored, 16)
            sp.wait_ge(out_stored, 16 * NT)

        @block.gpsimd
        def _(pool):
            n_step = [0]

            def step(ins):
                n_step[0] += 1
                ins.then_inc(pool_step, 1)
                pool.wait_ge(pool_step, n_step[0])

            step(nc.gpsimd.memset(ident[:], 0.0))
            step(nc.gpsimd.affine_select(out=ident[:], in_=ident[:], compare_op=ALU.not_equal, fill=1.0, base=0,
                                         pattern=[[-1, P]], channel_multiplier=1))
            nc.gpsimd.memset(ones[:], 1.0).then_inc(consts_made, 1)
            nc.gpsimd.memset(uT[:, :, 0:CPAD], 0.0).then_inc(pads_made, 1)
            nc.gpsimd.memset(pT[:, :, 0:PAD], 0.0).then_inc(pads_made, 1)
            nc.gpsimd.memset(v_sb[:, :, :, DH:VW], 1.0).then_inc(pads_made, 1)
            step(nc.gpsimd.memset(tri[:], 1.0))
            step(nc.gpsimd.memset(tri_strict[:], 1.0))
            step(nc.gpsimd.affine_select(out=tri[:], in_=tri[:], compare_op=ALU.is_ge, fill=0.0, base=0,
                                         pattern=[[1, P]], channel_multiplier=-1))
            step(nc.gpsimd.affine_select(out=tri_strict[:], in_=tri_strict[:], compare_op=ALU.is_gt, fill=0.0, base=0,
                                         pattern=[[1, P]], channel_multiplier=-1))
            step(nc.gpsimd.memset(head_sel[:], 1.0))
            hs = cut(head_sel, 0, H, P)
            step(nc.gpsimd.affine_select(out=hs, in_=hs, compare_op=ALU.is_equal, fill=0.0, base=0,
                                         pattern=[[-1, H], [0, P]], channel_multiplier=1))
            for t in range(PAD):
                nc.gpsimd.memset(inv_cnt[:, t:t + 1], 1.0 / (t + 1))
            step(nc.gpsimd.iota(iota_e[:], pattern=[[1, E]], base=0, channel_multiplier=0, allow_small_or_imprecise_dtypes=True))
            step(nc.gpsimd.iota(iota_pos[:], pattern=[[CAP, E]], base=0, channel_multiplier=0, allow_small_or_imprecise_dtypes=True))
            step(nc.gpsimd.iota(slot_id[:], pattern=[[1, TOPK], [TOPK * P, NT]], base=0, channel_multiplier=TOPK))
            for g in range(CG):
                step(nc.gpsimd.memset(quarter[TB * g:TB * (g + 1), :], float(g)))
            step(nc.gpsimd.iota(no_token, pattern=[[0, LIST_ROWS // P]], base=NO_TOKEN, channel_multiplier=0))
            nc.gpsimd.memset(stat[:, 67:68], 0.0).then_inc(consts_made, 1)
            pool.dma_start(list_dram.rearrange("(p n) a -> p (n a)", p=P), no_token).then_inc(list_cleared, 16)

            for g in range(PG):
                pool.wait_ge(gemm_out, g + 1)
                src = pT[:, g, :]
                for lvl in range(g + 1):
                    sh = 1 << lvl
                    if lvl == g:
                        step(nc.gpsimd.tensor_tensor(pool_w[:, g, :], src[:, PAD:PST], src[:, PAD - sh:PST - sh], ALU.add))
                    else:
                        lo = 2 * sh - 1
                        d = cut(hn, 0, PST) if lvl % 2 == 0 else cut(P1, 0, PST)
                        step(nc.gpsimd.tensor_tensor(d[:, lo:PST], src[:, lo:PST], src[:, lo - sh:PST - sh], ALU.add))
                        src = d
                w = WINDOWS[g]
                step(nc.gpsimd.tensor_tensor(pool_w[:, g, 0:w], pool_w[:, g, 0:w], inv_cnt[:, 0:w], ALU.mult))
                step(nc.gpsimd.tensor_scalar(pool_w[:, g, w:S], pool_w[:, g, w:S], 1.0 / w, None, ALU.mult))
                nc.gpsimd.tensor_tensor(pool_w[:, g, :], pool_w[:, g, :], pT[:, g, PAD:PST], ALU.subtract).then_inc(pooled_ready, 1)

            pool.wait_ge(pos_ready, 1)
            pool.wait_ge(list_cleared, 16)
            for n in range(TOPK * NT):
                pool.indirect_dma_start(out=list_dram, out_offset=bass.IndirectOffsetOnAxis(ap=posu[:, n:n + 1], axis=0),
                                        in_=slot_id[:, n:n + 1], in_offset=None).then_inc(list_stored, 16)
            step(nc.gpsimd.memset(xg, 0.0))
            pool.wait_ge(list_stored, 16 * TOPK * NT)
            pool.wait_ge(x1_stored, 16 * NT)

            def own_wait():
                pool.sem_inc(pool_mark, 1)

            def gather(it):
                pool.dma_start(idx[:], list_dram[bass.ds(it * CAP, CAP), :]).then_inc(idx_landed, 16)
                pool.wait_ge(idx_landed, 16 * it + 16)
                own_wait()
                nc.gpsimd.tensor_scalar(idx[:], idx[:], 1.0 / TOPK, -0.375, ALU.mult, ALU.add).then_inc(idx_ready, 1)
                pool.wait_ge(x_tr, it)
                pool.wait_ge(idx_ready, it + 1)
                own_wait()
                pool.indirect_dma_start(out=xg, out_offset=None, in_=x1_dram,
                                        in_offset=bass.IndirectOffsetOnAxis(ap=idx[:, 0:1], axis=0),
                                        bounds_check=S - 1, oob_is_err=False).then_inc(xg_landed, 16)
                pool.wait_ge(xg_landed, 16 * it + 16)
                own_wait()

            def scatter(it):
                lists = list_dram[bass.ds(it * CAP - CAP, CAP), :].rearrange("(t b) a -> t (b a)", b=NB)
                for g in range(CG):
                    pool.dma_start(slot[TB * g:TB * (g + 1), :], lists).then_inc(slot_landed, 16)
                pool.wait_ge(slot_landed, 16 * CG * it)
                own_wait()
                nc.gpsimd.tensor_scalar(slot[:], slot[:], float(CG), quarter[:, 0:1], ALU.mult, ALU.add).then_inc(slot_ready, 1)
                pool.wait_ge(slot_ready, it)
                pool.wait_ge(y_ready, it + 1)
                own_wait()
                for b in range(NB):
                    pool.indirect_dma_start(out=y_quarters, out_offset=bass.IndirectOffsetOnAxis(ap=slot[:, b:b + 1], axis=0),
                                            in_=yS[:, b, :], in_offset=None,
                                            bounds_check=S * TOPK * CG - 1, oob_is_err=False).then_inc(y_stored, 16)
                pool.wait_ge(y_stored, 16 * NB * it)
                own_wait()

            pool.wait_ge(iter_ready, 1)
            gather(0)
            gather(1)
            n_it = pool.snap(pool.value_load(more_iter[0:1, 0:1], min_val=0, max_val=(ROUNDS - 1) * E) + E)
            with pool.Fori(1, n_it) as it:
                gather(it + 1)
                scatter(it)
            scatter(n_it)

        @block.scalar
        def _(act):
            n_step = [0]

            def step(ins):
                n_step[0] += 1
                ins.then_inc(act_step, 1)
                act.wait_ge(act_step, n_step[0])

            act.dma_start(chan_rows[0:TAPS * MC, :], A["conv_w"][0].rearrange("t (c p) -> (t c) p", p=P)).then_inc(small_landed, 16)
            r0 = TAPS * MC
            for name, n in (("conv_b", MC), ("mh_gain", MC), ("b_pool", PG), ("ls_pool", PG)):
                act.dma_start(chan_rows[r0:r0 + n, :], A[name][0].rearrange("(c p) -> c p", p=P)).then_inc(small_landed, 16)
                r0 += n
            for j in range(2):
                act.dma_start(gate_b[0:H, j:j + 1], A["b_if"][0, H * j:H * (j + 1)].rearrange("(h a) -> h a", a=1)).then_inc(small_landed, 16)
            act.dma_start(wrv, A["w_router"][0].rearrange("(k p) e -> p k e", p=P)).then_inc(router_landed, 16)
            act.dma_start(br[:], A["b_router"][0:1, :].broadcast_to([P, E])).then_inc(router_landed, 16)

            def rstd(n):
                s0 = 16 * (n % 4)
                act.wait_ge(var_ready, n + 1)
                step(act.activation(stat[:, s0 + 14:s0 + 15], stat[:, s0 + 13:s0 + 14], ACT.Ln))
                act.activation(stat[:, s0 + 14:s0 + 15], stat[:, s0 + 14:s0 + 15], ACT.Exp, scale=-0.5).then_inc(rstd_ready, 1)

            rstd(NORM0)
            rstd(NORM0 + 1)
            act.wait_ge(chan_tr, 1)
            act.activation(chan[:, 0:56], ps[:, 3, 0:56], ACT.Copy).then_inc(chan_ready, 1)
            for i in range(NT):
                if i + 2 < NT:
                    rstd(NORM0 + i + 2)
                act.wait_ge(h0_tr, i + 1)
                b = 4 + 2 * (i % 2)
                act.activation(h0T[:, :, P * i:P * (i + 1)], ps[:, b:b + 2, :].rearrange("p b (c t) -> p (b c) t", t=P), ACT.Copy).then_inc(h0T_ready, 1)

            def take(n, dst, func=ACT.Copy, scale=1.0):
                act.wait_ge(gemm_done, n + 1)
                act.activation(dst, ps[:, n % 2, 0:dst_cols(dst)], func, scale=scale).then_inc(gemm_out, 1)

            def dst_cols(dst):
                return dst.shape[-1]

            act.wait_ge(if_done, 2)
            act.wait_ge(small_landed, 16 * 7)
            step(act.activation(t0_row, ps[0:H, 3, :], ACT.Abs, bias=gate_b[0:H, 1:2]))
            step(act.activation(t0_row, t0_row, ACT.Exp, scale=-1.0))
            act.activation(t0_row, t0_row, ACT.Ln, bias=1.0).then_inc(log_ready, 1)
            act.wait_ge(pads_made, 3)
            for g in range(PG):
                take(g, pT[:, g, PAD:PST])
            act.wait_ge(tot_ready, 1)
            act.activation(em_row, em_row, ACT.Exp, scale=-1.0).then_inc(em_ready, 1)
            for c in range(MC):
                take(PG + c, uT[:, c, CPAD:CPAD + S])
            for h in range(H):
                for i in range(NT):
                    take(N_PU + NT * h + i, v_sb[:, i, h, 0:DH])
            for c in range(MC):
                act.wait_ge(conv_ready, c + 1)
                act.activation(ucT[:, c, :], ucT[:, c, :], ACT.Silu).then_inc(silu_ready, 1)

            def head_qk(h):
                n = gemm_at_qk(h)
                for e in range(EC):
                    take(n + e, qT[:, e, :], scale=float(DH) ** -0.5)
                for e in range(EC):
                    take(n + EC + e, kT[:, e, :])

            def head_exp(h):
                for j in range(NT):
                    act.wait_ge(arg_ready, NT * h + j + 1)
                    w = wtmp[:, W_AT[j]:W_AT[j] + S - P * j]
                    act.activation(w, w, ACT.Exp, scale=-1.0).then_inc(w_ready, 1)

            act.wait_ge(pooled_ready, PG)
            act.wait_ge(mix_done, PG)
            head_qk(0)
            head_exp(0)
            for h in range(H):
                if h + 1 < H:
                    head_qk(h + 1)
                    head_exp(h + 1)
                for i in range(NT):
                    rstd(NORM_H + NT * h + i)
                for c in range(EC):
                    take(gemm_at_tr(h) + c, hnT[:, EC * h + c, 0:S])
            for m in range(MC):
                if m >= 2:
                    act.wait_ge(hout_ready, m - 1)
                take(GEMM_O + m, sig[:, m % 2, 0:S], ACT.Sigmoid)
            for m in range(KD):
                act.wait_ge(gate_done, m + 1)
                if m < 2:
                    act.wait_ge(hout_ready, MC)
                else:
                    act.wait_ge(merged_ready, m - 1)
                b = 2 if m % 2 == 0 else 6
                act.activation(sig[:, m % 2, :], ps[:, b:b + 2, :].rearrange("p b t -> p (b t)"), ACT.Sigmoid).then_inc(gate_ready, 1)
            for i in range(NT):
                rstd(NORM1 + i)
                act.wait_ge(x1_ready, i + 1)
                act.dma_start(x1_dram[P * i:P * (i + 1), :], X0v[:, i, :]).then_inc(x1_stored, 16)
                act.wait_ge(x1_tr, i + 1)
                act.activation(x1Tv[:, :, P * i:P * (i + 1)], ps[:, 0:2, :].rearrange("p b (c t) -> p (b c) t", t=P), ACT.Copy).then_inc(x1T_ready, 1)
            act.wait_ge(dist_ready, 1)
            act.activation(gatew[:], gatew[:], ACT.Exp).then_inc(router_exp, 1)

            act.wait_ge(iter_ready, 1)
            act.dma_start(gain[:], A["ln2_g"].broadcast_to([P, D])).then_inc(ln2_landed, 16)
            act.dma_start(bias[:], A["ln2_b"].broadcast_to([P, D])).then_inc(ln2_landed, 16)
            n_it = act.snap(act.value_load(more_iter[0:1, 0:1], min_val=0, max_val=(ROUNDS - 1) * E) + E)

            def take_xT(it1):
                act.wait_ge(x_tr, it1)
                act.activation(xT.rearrange("p c (b t) -> p c t b", b=NB), ps[:, 6:8, :].rearrange("p a (c t b) -> p (a c) t b", t=TB, b=NB), ACT.Copy).then_inc(xT_ready, 1)

            def take_actT(it):
                act.wait_ge(act_tr, it)
                act.activation(rest[:, 8960:9984], ps[:, 6:8, :].rearrange("p b t -> p (b t)"), ACT.Copy).then_inc(actT_ready, 1)

            def glu_sigmoid(it1):
                act.wait_ge(swiglu_step, it1 * 2 - 1)
                act.activation(sS, gS, ACT.Sigmoid, scale=GLU_ALPHA).then_inc(sig_ready, 1)

            take_xT(1)
            take_xT(2)
            glu_sigmoid(1)
            with act.Fori(1, n_it) as it:
                take_actT(it)
                take_xT(it + 2)
                glu_sigmoid(it + 1)
            take_actT(n_it)
            act.wait_ge(w2_used, n_it * (KF // 2))
            act.wait_ge(y_stored, n_it * (16 * NB))
            for i in range(NT):
                act.dma_start(yg[:, i], y_dram[P * i:P * (i + 1)]).then_inc(yg_landed[i], 16)
            for i in range(NT):
                rstd(NORM2 + i)

        @block.vector
        def _(dve):
            n_step = [0]

            def step(ins):
                n_step[0] += 1
                ins.then_inc(dve_step, 1)
                dve.wait_ge(dve_step, n_step[0])

            n_norm = [0]

            def statistics(n, src, width):
                s0 = 16 * (n % 4)
                pieces = max(1, width // BANK)
                w = width // pieces
                for a in range(pieces):
                    step(nc.vector.bn_stats(stat[:, s0 + 6 * a:s0 + 6 * a + 6], src[:, w * a:w * (a + 1)]))
                step(nc.vector.bn_aggr(stat[:, s0 + 12:s0 + 14], stat[:, s0:s0 + 6 * pieces]))
                nc.vector.tensor_scalar(stat[:, s0 + 13:s0 + 14], stat[:, s0 + 13:s0 + 14], LN_EPS, None, ALU.add).then_inc(var_ready, 1)

            def apply(n, t):
                s0 = 16 * (n % 4)
                var, y, q = stat[:, s0 + 13:s0 + 14], stat[:, s0 + 14:s0 + 15], stat[:, s0 + 15:s0 + 16]
                dve.wait_ge(rstd_ready, n + 1)
                step(nc.vector.scalar_tensor_tensor(out=q, in0=y, scalar=var, in1=y, op0=ALU.mult, op1=ALU.mult))
                step(nc.vector.tensor_scalar(q, q, -0.5, 1.5, ALU.mult, ALU.add))
                step(nc.vector.tensor_tensor(y, y, q, ALU.mult))
                return nc.vector.tensor_scalar(t, t, stat[:, s0 + 12:s0 + 13], stat[:, s0 + 14:s0 + 15], ALU.subtract, ALU.mult)

            def layer_norm_tail(n, t, done):
                step(apply(n, t))
                step(nc.vector.tensor_tensor(t, t, gain[:], ALU.mult))
                nc.vector.tensor_tensor(t, t, bias[:], ALU.add).then_inc(done, 1)

            for i in range(NT):
                dve.wait_ge(x_landed[i], 16)
                t = X0v[:, i, :]
                statistics(NORM0 + i, t, D)
                if i == 0:
                    dve.wait_ge(ln_landed, 32)
                if i >= 1:
                    layer_norm_tail(NORM0 + i - 1, X0v[:, i - 1, :], h0_ready)
            layer_norm_tail(NORM0 + NT - 1, X0v[:, NT - 1, :], h0_ready)

            dve.wait_ge(if_done, 2)
            dve.wait_ge(small_landed, 16 * 7)
            dve.wait_ge(log_ready, 1)
            step(nc.vector.tensor_scalar(t1_row, ps[0:H, 3, :], gate_b[0:H, 1:2], 0.0, ALU.add, ALU.min))
            step(nc.vector.tensor_tensor(t1_row, t1_row, t0_row, ALU.subtract))
            dve.wait_ge(consts_made, 2)
            step(nc.vector.tensor_tensor_scan(f_row, ones[0:H, 0:S], t1_row, 0.0, ALU.mult, ALU.add))
            step(nc.vector.scalar_tensor_tensor(out=a_row, in0=ps[0:H, 2, :], scalar=gate_b[0:H, 0:1], in1=f_row, op0=ALU.add, op1=ALU.subtract))
            step(nc.vector.tensor_tensor_scan(m_row, ones[0:H, 0:S], a_row, 0.0, ALU.mult, ALU.max))
            nc.vector.tensor_tensor(em_row, f_row, m_row, ALU.add).then_inc(tot_ready, 1)

            dve.wait_ge(chan_ready, 1)
            r_b, r_g, r_bp, r_ls = TAPS * MC, (TAPS + 1) * MC, (TAPS + 2) * MC, (TAPS + 2) * MC + PG
            for c in range(MC):
                dve.wait_ge(gemm_out, PG + c + 1)
                for j in range(TAPS):
                    src = uT[:, c, j:j + S]
                    tap = chan[:, MC * j + c:MC * j + c + 1]
                    if j == 0:
                        step(nc.vector.tensor_scalar(ucT[:, c, :], src, tap, chan[:, r_b + c:r_b + c + 1], ALU.mult, ALU.add))
                        continue
                    ins = nc.vector.scalar_tensor_tensor(out=ucT[:, c, :], in0=src, scalar=tap, in1=ucT[:, c, :], op0=ALU.mult, op1=ALU.add)
                    if j == TAPS - 1:
                        ins.then_inc(conv_ready, 1)
                    else:
                        step(ins)
            dve.wait_ge(rows_tr, 1)
            nc.vector.tensor_copy(cols[:], ps[:, 2, 0:NT * 2 * H]).then_inc(cols_ready, 1)
            for g in range(PG):
                dve.wait_ge(mix_done, g + 1)
                nc.vector.tensor_scalar(mixT[:, g, :], ps[:, 4 + g % 2, :], chan[:, r_bp + g:r_bp + g + 1], chan[:, r_ls + g:r_ls + g + 1],
                                        ALU.add, ALU.mult).then_inc(mixT_ready, 1)

            dve.wait_ge(cols_ready, 1)

            def head_args(h):
                dve.wait_ge(mb_done, h + 1)
                for j in range(NT):
                    if h >= 1:
                        dve.wait_ge(p_ready, NT * (h - 1) + j + 1)
                    nc.vector.tensor_scalar(wtmp[:, W_AT[j]:W_AT[j] + S - P * j], ps[:, 5, P * j:S], colv[:, j, h:h + 1], 0.0,
                                            ALU.subtract, ALU.max).then_inc(arg_ready, 1)

            def head_p(h):
                if h >= 2:
                    dve.wait_ge(pv_done, NT * (h - 1))
                dve.wait_ge(sc_done, h + 1)
                for j in range(NT):
                    dve.wait_ge(w_ready, NT * h + j + 1)
                    w = wtmp[:, W_AT[j]:W_AT[j] + S - P * j]
                    step(nc.vector.tensor_tensor(w[:, 0:P], w[:, 0:P], tri[:], ALU.mult))
                    b, c0 = S_AT[j]
                    nc.vector.tensor_tensor(Pm[h % 2][:, j, P * j:S], ps[:, b, c0:c0 + S - P * j], w, ALU.mult).then_inc(p_ready, 1)

            def head_norm(h):
                for i in range(NT):
                    n = NT * h + i
                    dve.wait_ge(pv_done, n + 1)
                    acc_ps = ps[:, 6 + n % 2, 0:VW]
                    step(nc.vector.tensor_scalar(stat[:, 64:65], acc_ps[:, DH:VW], -1.0, colv[:, i, H + h:H + h + 1], ALU.mult, ALU.max))
                    step(nc.vector.tensor_tensor(stat[:, 64:65], acc_ps[:, DH:VW], stat[:, 64:65], ALU.max))
                    step(nc.vector.reciprocal(stat[:, 65:66], stat[:, 64:65]))
                    if h >= 1 and i == 0:
                        dve.wait_ge(gemm_done, gemm_at_tr(h - 1) + EC)
                    nc.vector.tensor_scalar(hnv[:, i, :], acc_ps[:, 0:DH], stat[:, 65:66], None, ALU.mult).then_inc(num_read, 1)
                    dve.wait_ge(num_read, n + 1)
                    statistics(NORM_H + n, hnv[:, i, :], DH)
                    if i >= 1:
                        apply(NORM_H + n - 1, hnv[:, i - 1, :]).then_inc(hn_ready, 1)
                apply(NORM_H + NT * h + NT - 1, hnv[:, NT - 1, :]).then_inc(hn_ready, 1)

            head_args(0)
            head_p(0)
            for h in range(H):
                if h + 1 < H:
                    head_args(h + 1)
                    head_p(h + 1)
                head_norm(h)
            for m in range(MC):
                dve.wait_ge(gemm_out, GEMM_O + m + 1)
                nc.vector.scalar_tensor_tensor(out=hnT[:, m, 0:S], in0=hnT[:, m, 0:S], scalar=chan[:, r_g + m:r_g + m + 1],
                                               in1=sig[:, m % 2, 0:S], op0=ALU.mult, op1=ALU.mult).then_inc(hout_ready, 1)

            for m in range(KD):
                dve.wait_ge(gate_ready, m + 1)
                dve.wait_ge(y_done, m + 1)
                b = 4 if m % 2 == 0 else 0
                g = sig[:, m % 2, :]
                step(nc.vector.tensor_tensor(g, g, ps[:, b:b + 2, :].rearrange("p b t -> p (b t)"), ALU.mult))
                nc.vector.tensor_tensor(mergedT[:, m, :], g[:, 0:S], g[:, BANK:BANK + S], ALU.add).then_inc(merged_ready, 1)

            dve.wait_ge(ln1_landed, 32)
            for i in range(NT):
                dve.wait_ge(wo_done, i + 1)
                b = 2 + 2 * (i % 3)
                t = X0v[:, i, :]
                nc.vector.scalar_tensor_tensor(out=t, in0=t, scalar=DEEP_ALPHA, in1=ps[:, b:b + 2, :].rearrange("p b t -> p (b t)"),
                                               op0=ALU.mult, op1=ALU.add).then_inc(wo_read, 1)
                dve.wait_ge(wo_read, i + 1)
                statistics(NORM1 + i, t, D)
                layer_norm_tail(NORM1 + i, t, x1_ready)

            dve.wait_ge(router_landed, 32)
            dve.wait_ge(logits_done, 1)
            lg = cut(logits, 0, NT, E)
            step(nc.vector.tensor_tensor(lg, ps[:, 4, 0:NT * E].rearrange("p (i e) -> p i e", e=E),
                                         br[:].rearrange("p (a e) -> p a e", a=1).broadcast_to([P, NT, E]), ALU.add))
            topv = cut(top, 0, NT, 8)
            topiv = cut(topi, 0, NT, 8)
            for i in range(NT):
                step(nc.vector.max(topv[:, i, :], lg[:, i, :]))
                step(nc.vector.max_index(topiv[:, i, :], topv[:, i, :], lg[:, i, :]))
            gw = cut(gatew, 0, NT, TOPK)
            nc.vector.tensor_tensor(gw, topv[:, :, 0:TOPK], topv[:, :, 0:1].broadcast_to([P, NT, TOPK]), ALU.subtract).then_inc(dist_ready, 1)
            tf = cut(topf, 0, NT, TOPK)
            step(nc.vector.tensor_copy(tf, topiv[:, :, 0:TOPK]))
            oh = cut(onehot, 0, TOPK, NT, E)
            experts = iota_e[:].rearrange("p (a e) -> p a e", a=1).broadcast_to([P, NT, E])
            for k in range(TOPK):
                step(nc.vector.tensor_tensor(oh[:, k], experts, tf[:, :, k:k + 1].broadcast_to([P, NT, E]), ALU.is_equal))
            mk = cut(mask, 0, NT, E)
            step(nc.vector.tensor_tensor(mk, oh[:, 0], oh[:, 1], ALU.add))
            step(nc.vector.tensor_tensor(mk, mk, oh[:, 2], ALU.add))
            nc.vector.tensor_tensor(mk, mk, oh[:, 3], ALU.add).then_inc(mask_ready, 1)
            dve.wait_ge(router_exp, 1)
            gs = cut(gsum, 0, NT, 1)
            step(nc.vector.tensor_reduce(gs, gw, X_AXIS, ALU.add))
            step(nc.vector.reciprocal(gs, gs))
            step(nc.vector.tensor_tensor(gw, gw, gs.broadcast_to([P, NT, TOPK]), ALU.mult))

            dve.wait_ge(rank_done, 1)
            rk, rt, ri = cut(rank, 0, NT, E), cut(rtmp, 0, NT, E), cut(rint, 0, NT, E)
            rp = ps[:, 5, 0:NT * E].rearrange("p (i e) -> p i e", e=E)
            step(nc.vector.scalar_tensor_tensor(out=rk, in0=rp, scalar=float(NB), in1=iota_pos[:].rearrange("p (a e) -> p a e", a=1).broadcast_to([P, NT, E]),
                                                op0=ALU.mult, op1=ALU.add))
            for unit, weight in ((TB, 1 - NB * TB), (CAP, CAP * E - NB)):
                step(nc.vector.tensor_scalar(ri, rp, 1.0 / unit, 0.5 / unit - 0.5, ALU.mult, ALU.add))
                step(nc.vector.tensor_copy(rt, ri))
                step(nc.vector.scalar_tensor_tensor(out=rk, in0=rt, scalar=float(weight), in1=rk, op0=ALU.mult, op1=ALU.add))
            pv = cut(pos, 0, TOPK, NT, 1)
            for k in range(TOPK):
                step(nc.vector.tensor_tensor(rt, oh[:, k], rk, ALU.mult))
                step(nc.vector.tensor_reduce(pv[:, k], rt, X_AXIS, ALU.add))
            nc.vector.tensor_copy(posu[:], pos[:]).then_inc(pos_ready, 1)
            step(nc.vector.tensor_reduce(cnt[:, E:E + 1], ps[:, 5, NT * E:NT * E + E], X_AXIS, ALU.max))
            step(nc.vector.memset(cnt[:, E + 1:E + 2], 0.0))
            for r in range(1, ROUNDS):
                step(nc.vector.tensor_scalar(cnt[:, E + 2:E + 3], cnt[:, E:E + 1], float(CAP * r), float(E), ALU.is_gt, ALU.mult))
                step(nc.vector.tensor_tensor(cnt[:, E + 1:E + 2], cnt[:, E + 1:E + 2], cnt[:, E + 2:E + 3], ALU.add))
            nc.vector.tensor_copy(more_iter[0:1, :], cnt[0:1, E + 1:E + 2]).then_inc(iter_ready, 1)
            dve.wait_ge(iter_ready, 1)
            n_it = dve.snap(dve.value_load(more_iter[0:1, 0:1], min_val=0, max_val=(ROUNDS - 1) * E) + E)

            def swiglu(it1, first=False):
                dve.wait_ge(w1_used, it1 * KD)
                dve.wait_ge(b1_landed, 16 * CG * it1)
                nc.vector.tensor_tensor(hS, ps[:, 0:NB, :], b1t.rearrange("p (a n) -> p a n", a=1).broadcast_to([P, NB, HW_]), ALU.add).then_inc(h_read, 1)
                dve.wait_ge(h_read, it1)
                pair = hS.rearrange("p b (n two) -> p b n two", two=2)
                nc.vector.tensor_scalar(gS, pair[:, :, :, 0], GLU_LIMIT, None, ALU.min).then_inc(swiglu_step, 1)
                nc.vector.tensor_scalar(lS, pair[:, :, :, 1], GLU_LIMIT, -GLU_LIMIT, ALU.min, ALU.max).then_inc(swiglu_step, 1)
                dve.wait_ge(swiglu_step, 2 * it1)
                nc.vector.scalar_tensor_tensor(out=lS, in0=lS, scalar=1.0, in1=gS, op0=ALU.add, op1=ALU.mult).then_inc(lin_ready, 1)
                dve.wait_ge(lin_ready, it1)
                dve.wait_ge(sig_ready, it1)
                if not first:
                    dve.wait_ge(act_tr, it1 - 1)
                nc.vector.tensor_tensor(aS.rearrange("p b a n -> p b (a n)"), lS, sS, ALU.mult).then_inc(act_ready, 1)

            def take_y(it, first=False):
                dve.wait_ge(w2_used, it * (KF // 2))
                dve.wait_ge(b2_landed, 16 * CG * it)
                if not first:
                    dve.wait_ge(y_stored, 16 * NB * it - 16 * NB)
                nc.vector.tensor_tensor(yS, ps[:, 4:6, :].rearrange("p b (a n) -> p (b a) n", a=2),
                                        b2t.rearrange("p (a n) -> p a n", a=1).broadcast_to([P, NB, YW]), ALU.add).then_inc(y_ready, 1)

            nc.vector.memset(stat[:, 66:67], 0.0).then_inc(y_ready, 1)
            swiglu(1, first=True)
            swiglu(2)
            take_y(1, first=True)
            with dve.Fori(2, n_it) as it:
                swiglu(it + 1)
                take_y(it)
            take_y(n_it)

            dve.wait_ge(ln2_landed, 32)
            for i in range(NT):
                t = X0v[:, i, :]
                dve.wait_ge(yg_landed[i], 16)
                step(nc.vector.tensor_scalar(t, t, DEEP_ALPHA, None, ALU.mult))
                for k in range(TOPK):
                    step(nc.vector.scalar_tensor_tensor(out=t, in0=yg[:, i, k, :], scalar=gw[:, i, k:k + 1], in1=t, op0=ALU.mult, op1=ALU.add))
                statistics(NORM2 + i, t, D)
                layer_norm_tail(NORM2 + i, t, out_ready)

        @block.tensor
        def _(pe):
            mm = nc.tensor.matmul
            pe.wait_ge(consts_made, 2)
            pe.wait_ge(small_landed, 16 * 7)
            nc.tensor.transpose(ps[:, 3, 0:56], chan_rows[0:56, :], ident[0:56, 0:56]).then_inc(chan_tr, 1)
            for i in range(NT):
                pe.wait_ge(h0_ready, i + 1)
                if i >= 2:
                    pe.wait_ge(h0T_ready, i - 1)
                b = 4 + 2 * (i % 2)
                for k in range(KD):
                    last = nc.tensor.transpose(ps[:, b + k // 4, P * (k % 4):P * (k % 4 + 1)], X0v[:, i, P * k:P * (k + 1)], ident[:])
                last.then_inc(h0_tr, 1)
            pe.wait_ge(h0T_ready, NT)
            pe.wait_ge(wif_landed, 16)
            pe.wait_ge(chan_ready, 1)
            wifv = cut(wif, 0, KD, 2 * H)
            for j in range(2):
                for k in range(KD):
                    last = mm(ps[0:H, 2 + j, :], wifv[:, k, H * j:H * (j + 1)], h0T[:, k, :], start=(k == 0), stop=(k == KD - 1))
                last.then_inc(if_done, 1)

            def bank_for(n):
                if n >= 2:
                    pe.wait_ge(gemm_out, n - 1)
                return n % 2

            n_out = 0
            for n, (kind, _, _) in enumerate(PANELS[:PW // PANEL + MW // PANEL + H]):
                pe.wait_ge(ring_landed[n % RING], 16 * (n // RING + 1))
                slot = ring[:, n % RING]
                if kind == "v":
                    for i in range(NT):
                        b = bank_for(n_out)
                        for k in range(KD):
                            last = mm(ps[:, b, 0:DH], h0T[:, k, P * i:P * (i + 1)], slot[:, k, :], start=(k == 0), stop=(k == KD - 1))
                        last.then_inc(gemm_done, 1)
                        n_out += 1
                else:
                    for c in range(2):
                        b = bank_for(n_out)
                        for k in range(KD):
                            last = mm(ps[:, b, :], slot[:, k, P * c:P * (c + 1)], h0T[:, k, :], start=(k == 0), stop=(k == KD - 1))
                        last.then_inc(gemm_done, 1)
                        n_out += 1
                if n == PW // PANEL + MW // PANEL - 1:
                    pe.wait_ge(tot_ready, 1)
                    pe.wait_ge(em_ready, 1)
                    for i in range(NT):
                        for j, r in enumerate((a_row, em_row)):
                            last = nc.tensor.transpose(ps[:, 2, 2 * H * i + H * j:2 * H * i + H * (j + 1)], r[:, P * i:P * (i + 1)], ident[0:H, 0:H])
                    last.then_inc(rows_tr, 1)
                    pe.wait_ge(wpool_landed, 16)
                    wpv = cut(wpool, 0, PG, PGD)
                    for g in range(PG):
                        pe.wait_ge(pooled_ready, g + 1)
                        if g >= 2:
                            pe.wait_ge(mixT_ready, g - 1)
                        mm(ps[:, 4 + g % 2, :], wpv[:, g, :], pool_w[:, g, :], start=True, stop=True).then_inc(mix_done, 1)

            def head_qk(h):
                if h == 0:
                    pe.wait_ge(wqk_landed, 16 * 2 * H)
                pe.wait_ge(silu_ready, EC * (h + 1))
                n = gemm_at_qk(h)
                for j in range(2):
                    for e in range(EC):
                        b = bank_for(n)
                        for c in range(EC):
                            last = mm(ps[:, b, :], wqk[:, 2 * h + j, c, P * e:P * (e + 1)], ucT[:, EC * h + c, :], start=(c == 0), stop=(c == EC - 1))
                        last.then_inc(gemm_done, 1)
                        n += 1
                if h >= 1:
                    pe.wait_ge(arg_ready, NT * h)
                else:
                    pe.wait_ge(mixT_ready, PG)
                mm(ps[:, 5, :], cut(head_sel, 0, H, P)[0:H, h, :], m_row, start=True, stop=True).then_inc(mb_done, 1)
                pe.wait_ge(gemm_out, n)
                if h >= 1:
                    pe.wait_ge(p_ready, NT * h)
                else:
                    pe.wait_ge(cols_ready, 1)
                for j in range(NT):
                    b, c0 = S_AT[j]
                    for e in range(EC):
                        last = mm(ps[:, b, c0:c0 + S - P * j], kT[:, e, P * j:P * (j + 1)], qT[:, e, P * j:S], start=(e == 0), stop=(e == EC - 1))
                last.then_inc(sc_done, 1)

            def head_pv(h):
                for i in range(NT):
                    n = NT * h + i
                    pe.wait_ge(p_ready, n + 1)
                    if n >= 2:
                        pe.wait_ge(num_read, n - 1)
                    for j in range(i + 1):
                        last = mm(ps[:, 6 + n % 2, 0:VW], Pm[h % 2][:, j, P * i:P * (i + 1)], v_sb[:, j, h, :], start=(j == 0), stop=(j == i))
                    last.then_inc(pv_done, 1)

            def head_tr(h):
                pe.wait_ge(hn_ready, NT * (h + 1))
                for c in range(EC):
                    b = bank_for(gemm_at_tr(h) + c)
                    for i in range(NT):
                        last = nc.tensor.transpose(ps[:, b, P * i:P * (i + 1)], hnv[:, i, P * c:P * (c + 1)], ident[:])
                    last.then_inc(gemm_done, 1)

            head_qk(0)
            for h in range(H):
                if h + 1 < H:
                    head_qk(h + 1)
                head_pv(h)
                head_tr(h)
            for m in range(MC):
                n = PW // PANEL + MW // PANEL + H + m // 2
                if m % 2 == 0:
                    pe.wait_ge(ring_landed[n % RING], 16 * (n // RING + 1))
                b = bank_for(GEMM_O + m)
                for k in range(KD):
                    last = mm(ps[:, b, :], ring[:, n % RING][:, k, P * (m % 2):P * (m % 2 + 1)], h0T[:, k, :], start=(k == 0), stop=(k == KD - 1))
                last.then_inc(gemm_done, 1)

            for m in range(KD):
                w = merge_w[m % 2]
                gb, yb = (2, 4) if m % 2 == 0 else (6, 0)
                pe.wait_ge(merge_landed[m % 2], 64 * (m // 2 + 1))
                if m >= 2:
                    pe.wait_ge(merged_ready, m - 1)
                if m == 1:
                    pe.wait_ge(gemm_out, GEMM_O + MC)
                for j in range(2):
                    for k in range(KD):
                        last = mm(ps[:, gb + j, :], w[:, KD * j + k, :], h0T[:, k, :], start=(k == 0), stop=(k == KD - 1))
                last.then_inc(gate_done, 1)
                if m == 0:
                    pe.wait_ge(hout_ready, MC)
                    pe.wait_ge(mixT_ready, PG)
                for k in range(PG):
                    mm(ps[:, yb, :], w[:, 2 * KD + k, :], mixT[:, k, :], start=(k == 0), stop=(k == PG - 1))
                for k in range(MC):
                    last = mm(ps[:, yb + 1, :], w[:, 2 * KD + PG + k, :], hnT[:, k, 0:S], start=(k == 0), stop=(k == MC - 1))
                last.then_inc(y_done, 1)

            pe.wait_ge(wout_landed, 16)
            for i in range(NT):
                b = 2 + 2 * (i % 3)
                if i == 0:
                    pe.wait_ge(merged_ready, KD)
                if i == 3:
                    pe.wait_ge(wo_read, 1)
                for n in range(D // BANK):
                    for k in range(KD):
                        last = mm(ps[:, b + n, :], mergedT[:, k, P * i:P * (i + 1)], wout[:, k, BANK * n:BANK * (n + 1)], start=(k == 0), stop=(k == KD - 1))
                last.then_inc(wo_done, 1)
            for i in range(NT):
                pe.wait_ge(x1_ready, i + 1)
                if i >= 1:
                    pe.wait_ge(x1T_ready, i)
                for k in range(KD):
                    last = nc.tensor.transpose(ps[:, k // 4, P * (k % 4):P * (k % 4 + 1)], X0v[:, i, P * k:P * (k + 1)], ident[:])
                last.then_inc(x1_tr, 1)
            pe.wait_ge(router_landed, 32)
            pe.wait_ge(x1T_ready, NT)
            for i in range(NT):
                for k in range(KD):
                    last = mm(ps[:, 4, E * i:E * (i + 1)], x1Tv[:, k, P * i:P * (i + 1)], wrv[:, k, :], start=(k == 0), stop=(k == KD - 1))
            last.then_inc(logits_done, 1)
            pe.wait_ge(mask_ready, 1)
            mk = cut(mask, 0, NT, E)
            for i in range(NT):
                for j in range(i + 1):
                    mm(ps[:, 5, E * i:E * (i + 1)], tri_strict[:] if j == i else ones[:, 0:P], mk[:, j, :], start=(j == 0), stop=(j == i))
            for j in range(NT):
                last = mm(ps[:, 5, E * NT:E * (NT + 1)], ones[:, 0:P], mk[:, j, :], start=(j == 0), stop=(j == NT - 1))
            last.then_inc(rank_done, 1)

            def x_transposes(it1):
                pe.wait_ge(xg_landed, 16 * it1)
                for k in range(KD):
                    last = nc.tensor.transpose(ps[:, 6 + k // 4, P * (k % 4):P * (k % 4 + 1)], xg[:, P * k:P * (k + 1)], ident[:])
                last.then_inc(x_tr, 1)

            def fc1(it1, ks):
                for k in ks:
                    pe.wait_ge(w1_landed[k], 16 * it1)
                    for b in range(NB):
                        for g in range(CG):
                            last = mm(ps[TB * g:TB * (g + 1), b, :], xT[:, k, TB * b:TB * (b + 1)], W1[:, k, HW_ * g:HW_ * (g + 1)],
                                      start=(k == 0), stop=(k == KD - 1))
                    last.then_inc(w1_used, 1)

            def act_transposes(it):
                pe.wait_ge(act_ready, it)
                for b in range(NB):
                    for a in range(2):
                        last = nc.tensor.transpose(ps[:, 6 + b // 2, P * (2 * (b % 2) + a):P * (2 * (b % 2) + a + 1)], aS[:, b, a, :], ident[:])
                last.then_inc(act_tr, 1)

            def fc2(it):
                pe.wait_ge(actT_ready, it)
                for kk in range(KF // 2):
                    pe.wait_ge(w2_landed[kk], 16 * it)
                    for a in range(2):
                        k = 2 * kk + a
                        for b in range(NB):
                            for g in range(CG):
                                last = mm(ps[TB * g:TB * (g + 1), 4 + b // 2, YW * (b % 2):YW * (b % 2 + 1)],
                                          aT[:, b, k % 2, TB * (k // 2):TB * (k // 2 + 1)], W2[:, kk, a, YW * g:YW * (g + 1)],
                                          start=(k == 0 and b % 2 == 0), stop=(k == KF - 1), skip_group_check=True)
                    last.then_inc(w2_used, 1)

            pe.wait_ge(iter_ready, 1)
            n_it = pe.snap(pe.value_load(more_iter[0:1, 0:1], min_val=0, max_val=(ROUNDS - 1) * E) + E)
            x_transposes(1)
            pe.wait_ge(xT_ready, 1)
            fc1(1, range(KD))
            x_transposes(2)
            with pe.Fori(1, n_it) as it:
                pe.wait_ge(xT_ready, it + 1)
                pe.wait_ge(h_read, it)
                fc1(it + 1, range(KD // 2))
                act_transposes(it)
                fc1(it + 1, range(KD // 2, KD))
                pe.wait_ge(actT_ready, it)
                x_transposes(it + 2)
                pe.wait_ge(y_ready, it)
                fc2(it)
            pe.wait_ge(xT_ready, n_it + 1)
            act_transposes(n_it)
            pe.wait_ge(y_ready, n_it)
            fc2(n_it)


NAMES = ["x", "ln0_g", "ln0_b", "w_in", "conv_w", "conv_b", "w_q", "w_k", "b_if", "mh_gain", "w_pool", "b_pool", "ls_pool",
         "w_branch_pool", "w_branch_mlstm", "w_out", "ln1_g", "ln1_b", "w_router", "b_router", "w_e1", "b_e1", "w_e2", "b_e2",
         "ln2_g", "ln2_b"]


def kernel(**inputs):
    import numpy as np
    import concourse.bacc as bacc
    from concourse.bass_utils import run_bass_kernel_spmd

    nc = bacc.Bacc("TRN2", target_bir_lowering=False, num_devices=1)
    arrays, aps = {}, {}
    for name in NAMES:
        a = np.ascontiguousarray(inputs[name])
        arrays[f"in_{name}"] = a
        aps[name] = nc.dram_tensor(f"in_{name}", a.shape, mybir.dt.from_np(a.dtype), kind="ExternalInput").ap()
    shape = inputs["x"].shape
    out = nc.dram_tensor("out_rows", shape, F32, kind="ExternalOutput").ap()
    build_program(nc, aps, out)
    r = run_bass_kernel_spmd(nc, [arrays], core_ids=[0])
    return r.results[0]["out_rows"]
```

```python
from contextlib import ExitStack

import concourse.bass as bass
from concourse import mybir

F32 = mybir.dt.float32
U32 = mybir.dt.uint32
I32 = mybir.dt.int32
ALU = mybir.AluOpType
ACT = mybir.ActivationFunctionType
X_AXIS = mybir.AxisListType.X

P = 128
BANK = 512


def build_program(nc, A, out):
    _, S, D = A["x"].shape
    NT = S // P
    KD = D // P
    _, TAPS, MW = A["conv_w"].shape
    _, H, DH, _ = A["w_q"].shape
    _, PG, PGD, _ = A["w_pool"].shape
    PW = PG * PGD
    _, _, E = A["w_router"].shape
    FF = A["w_e2"].shape[2]
    KF = FF // P
    MC = MW // P
    EC = DH // P
    TOPK = 4
    LN_EPS = 1e-5
    DEEP_ALPHA = 2.0 ** 0.25
    GLU_ALPHA = 1.702
    GLU_LIMIT = 7.0
    COL_P, COL_U, COL_V, COL_O = 0, PW, PW + MW, PW + 2 * MW
    COL_IF = PW + 3 * MW
    COL_G = COL_IF + 2 * H
    PANEL = 2 * P
    RING = 4
    WINDOWS = [2 ** (g + 1) for g in range(PG)]
    PAD = WINDOWS[-1]
    CPAD = TAPS - 1
    UST = S + CPAD + 1
    PST = S + PAD
    VW = DH + 1
    CAP = P
    ROUNDS = S // CAP
    ROUND_ROWS = E * CAP
    N_ITER = ROUNDS * E
    NO_TOKEN = 1 << 20
    CG = 4
    TB = P // CG
    NB = CAP // TB
    HW_ = 2 * FF // CG
    YW = D // CG
    assert DH == PANEL and HW_ == BANK and NT == 4 and KD == 8

    w_in = A["w_in"][0]
    w_in_k = w_in.rearrange("(k p) n -> p k n", p=P)
    x_rows = A["x"][0]
    out_rows = out[0]

    x1_dram = nc.dram_tensor("x1_rows", (S, D), F32, kind="Internal").ap()
    y_dram = nc.dram_tensor("expert_rows", (S, TOPK, D), F32, kind="Internal").ap()
    y_quarters = y_dram.rearrange("t k (g n) -> (t k g) n", g=CG)

    with ExitStack() as ctx:
        def sb(name, cols, dt=F32, parts=P):
            return ctx.enter_context(nc.sbuf_tensor(name, [parts, cols], dt))

        def sem(name):
            return ctx.enter_context(nc.semaphore(name))

        X0 = sb("X0", NT * D)
        gain = sb("ln_gain", D)
        bias = sb("ln_bias", D)
        W1_COLS, W2_COLS = KD * 2 * FF, KF * D
        big = sb("big", W1_COLS + W2_COLS + 128)
        rest = sb("rest", 12288)
        x1T = sb("x1T", KD * S)
        P1 = sb("P1", NT * S)
        hn = sb("hn", NT * DH)
        ident = sb("ident", P)
        tri = sb("tri", P)
        tri_strict = sb("tri_strict", P)
        ones = sb("ones", BANK)
        head_sel = sb("head_sel", H * P)
        chan_rows = sb("chan_rows", P)
        chan = sb("chan", 64)
        gate_b = sb("gate_b", 2)
        m_line = sb("m_line", S)
        cols = sb("gate_cols", NT * 2 * H)
        wif = sb("w_if", KD * 2 * H)
        inv_cnt = sb("inv_cnt", PAD)
        bias_sel = ctx.enter_context(nc.sbuf_tensor("bias_sel", [P, TB], F32))[:]
        stat = sb("stat", 96)
        wr = sb("w_router_sb", KD * E)
        br = sb("b_router_sb", E)
        top = sb("top", NT * 8)
        topi = sb("topi", NT * 8, U32)
        topf = sb("topf", NT * TOPK)
        gatew = sb("gatew", NT * TOPK)
        gsum = sb("gsum", 2 * NT)
        rint = chan_rows[:, 0:NT * E].bitcast(I32)
        iota_e = sb("iota_e", E)
        place = sb("place", TOPK * NT)
        itern = sb("itern", TOPK * NT)
        slot_id = sb("slot_id", TOPK * NT)
        slot = sb("slot", NB, U32)
        quarter = sb("quarter", 1)
        cnt = sb("cnt", E + 8)
        more_iter = sb("more_iter", 1, I32)
        idx = sb("idx", 1, U32)
        blocks = m_line[:, 0:ROUNDS * E].bitcast(I32)

        def cut(t, at, *shape):
            n = 1
            for s in shape:
                n *= s
            v = t[:, at:at + n]
            if len(shape) == 2:
                return v.rearrange("p (a b) -> p a b", a=shape[0])
            if len(shape) == 3:
                return v.rearrange("p (a b c) -> p a b c", a=shape[0], b=shape[1])
            return v

        X0v = cut(X0, 0, NT, D)
        h0T = cut(big, 0, KD, S)
        uT = cut(big, 4096, MC, UST)
        hnT = uT
        v_sb = cut(big, 8224, NT, H, VW)
        mixT = cut(big, 12336, PG, S)
        pT = cut(big, 14384, PG, PST)
        P0 = cut(big, 14384, NT, S)
        pool_w = cut(big, 16496, PG, S)
        qT = cut(big, 16496, EC, S)
        kT = cut(big, 17520, EC, S)
        wqk = cut(big, 18544, 2 * H, EC, DH)
        wtmp = cut(big, 22640, 1280)
        wout = cut(big, 14384, KD, D)
        sig = cut(big, 22640, 2, 2 * BANK)
        sig_o = [x1T[:, 3584:3584 + S], big[:, 23920:23920 + S]]
        ring = cut(rest, 0, RING, KD, PANEL)
        ucT = cut(rest, 8192, MC, S)
        mergedT = ucT
        MS = (2 * KD + PG + MC) * P
        merge_w = [cut(x1T, 0, 2 * KD + PG + MC, P), cut(rest, 0, 2 * KD + PG + MC, P)]
        x1Tv = cut(x1T, 0, KD, S)
        Pm = [P0, cut(P1, 0, NT, S)]
        hnv = cut(hn, 0, NT, DH)
        m_row = m_line[0:H, :]
        idx_table = P1[:, 0:N_ITER + 1].bitcast(U32)
        slot_table = P1[:, 130:130 + NB * N_ITER].bitcast(U32)
        slots_f = P1[:, 642:642 + N_ITER]
        spread = P1[:, 770:770 + NB * P]
        iota_row = P1[:, 1282:1282 + P]
        place_oh = cut(x1T, 0, TOPK * NT, P)
        iter_oh = cut(x1T, TOPK * NT * P, TOPK * NT, P)
        a_row, f_row, em_row, t0_row, t1_row = (x1T[0:H, S * n:S * (n + 1)] for n in range(5))
        wpool = big[:, 23920:23920 + PG * PGD]
        onehot = hn[:, 0:TOPK * NT * E]
        logits, mask, rank, rtmp = (hn[:, NT * E * n:NT * E * (n + 1)] for n in range(TOPK, TOPK + 4))
        colv = cut(cols, 0, NT, 2 * H)
        wrv = cut(wr, 0, KD, E)
        W1 = cut(big, 0, KD, 2 * FF)
        W2 = cut(big, W1_COLS, KF // 2, 2, D)
        xg = cut(rest, 0, D)
        xT = cut(rest, 1024, KD, NB, TB)
        b1_row = rest[:, 2048:4096]
        b2_row = rest[:, 4096:5120]
        gS = cut(rest, 5120, NB, HW_ // 2)
        lS = cut(rest, 6144, NB, HW_ // 2)
        sS = cut(rest, 7168, NB, HW_ // 2)
        aS = cut(rest, 8192, NB, 2, P)
        aT = cut(rest, 9216, NB, 2, P)
        yS = cut(rest, 10240, NB, YW)
        gate_diag = place_oh
        yg = big[:, 0:NT * TOPK * D].rearrange("p (i k n) -> p i k n", i=NT, k=TOPK)
        acc = cut(rest, 0, 2, D)

        ps = ctx.enter_context(nc.psum_tensor("ps", [P, 8, BANK], F32))

        x_landed = [sem(f"x_landed{i}") for i in range(NT)]
        ln_landed = sem("ln_landed")
        small_landed = sem("small_landed")
        wif_landed = sem("wif_landed")
        wpool_landed = sem("wpool_landed")
        wqk_landed = sem("wqk_landed")
        wout_landed = sem("wout_landed")
        router_landed = sem("router_landed")
        ring_landed = [sem(f"ring_landed{i}") for i in range(RING)]
        merge_landed = [sem(f"merge_landed{i}") for i in range(2)]
        pool_step = sem("pool_step")
        pool_mark = sem("pool_mark")
        consts_made = sem("consts_made")
        pads_made = sem("pads_made")
        dve_step = sem("dve_step")
        act_step = sem("act_step")
        h0_ready = sem("h0_ready")
        gained = sem("gained")
        var_ready = sem("var_ready")
        rstd_ready = sem("rstd_ready")
        h0_tr = sem("h0_tr")
        h0T_ready = sem("h0T_ready")
        chan_tr = sem("chan_tr")
        chan_ready = sem("chan_ready")
        if_done = sem("if_done")
        log_ready = sem("log_ready")
        tot_ready = sem("tot_ready")
        em_ready = sem("em_ready")
        rows_tr = sem("rows_tr")
        cols_ready = sem("cols_ready")
        gemm_done = sem("gemm_done")
        gemm_out = sem("gemm_out")
        pooled_ready = sem("pooled_ready")
        mix_done = sem("mix_done")
        mixT_ready = sem("mixT_ready")
        conv_ready = sem("conv_ready")
        silu_ready = sem("silu_ready")
        mb_done = sem("mb_done")
        arg_ready = sem("arg_ready")
        w_ready = sem("w_ready")
        sc_done = sem("sc_done")
        p_ready = sem("p_ready")
        pv_done = sem("pv_done")
        num_read = sem("num_read")
        hn_ready = sem("hn_ready")
        hout_ready = sem("hout_ready")
        gate_done = sem("gate_done")
        gate_ready = sem("gate_ready")
        y_done = sem("y_done")
        merged_ready = sem("merged_ready")
        wo_done = sem("wo_done")
        wo_read = sem("wo_read")
        x1_ready = sem("x1_ready")
        x1_stored = sem("x1_stored")
        x1_tr = sem("x1_tr")
        x1T_ready = sem("x1T_ready")
        logits_done = sem("logits_done")
        router_exp = sem("router_exp")
        dist_ready = sem("dist_ready")
        mask_ready = sem("mask_ready")
        rank_done = sem("rank_done")
        pos_ready = sem("pos_ready")
        dispatch_consts = sem("dispatch_consts")
        slots_done = sem("slots_done")
        diags_ready = sem("diags_ready")
        combined = sem("combined")
        combined_read = sem("combined_read")
        slots_read = sem("slots_read")
        spread_done = sem("spread_done")
        tables_ready = sem("tables_ready")
        bias_zeroed = sem("bias_zeroed")
        iter_ready = sem("iter_ready")
        idx_ready = sem("idx_ready")
        slot_ready = sem("slot_ready")
        xg_landed = sem("xg_landed")
        w1_landed = [sem(f"w1_landed{k}") for k in range(KD)]
        w2_landed = [sem(f"w2_landed{k}") for k in range(KF // 2)]
        b1_landed = sem("b1_landed")
        b2_landed = sem("b2_landed")
        w1_used = sem("w1_used")
        w2_used = sem("w2_used")
        x_tr = sem("x_tr")
        xT_ready = sem("xT_ready")
        h_read = sem("h_read")
        swiglu_step = sem("swiglu_step")
        sig_ready = sem("sig_ready")
        lin_ready = sem("lin_ready")
        act_ready = sem("act_ready")
        act_tr = sem("act_tr")
        actT_ready = sem("actT_ready")
        y_ready = sem("y_ready")
        y_stored = sem("y_stored")
        yg_landed = [sem(f"yg_landed{i}") for i in range(NT)]
        tail_act = sem("tail_act")
        ln2_landed = sem("ln2_landed")
        ln1_landed = sem("ln1_landed")
        out_ready = sem("out_ready")
        out_stored = sem("out_stored")

        PANELS = ([("p", COL_P + PANEL * n, n) for n in range(PW // PANEL)]
                  + [("u", COL_U + PANEL * n, n) for n in range(MW // PANEL)]
                  + [("v", COL_V + PANEL * n, n) for n in range(H)]
                  + [("o", COL_O + PANEL * n, n) for n in range(MW // PANEL)])
        order = [("p", n) for n in range(PG)] + [("u", n) for n in range(MC)] + [("v", n) for n in range(H * NT)]
        order += [("qk", n) for n in range(2 * EC)]
        for h in range(H):
            order += [("qk", 2 * EC * (h + 1) + n) for n in range(2 * EC) if h + 1 < H]
            order += [("o", EC * h + n) for n in range(EC)] + [("tr", EC * h + n) for n in range(EC)]
        at = {what: n for n, what in enumerate(order)}
        PANEL_LAST = ([("p", 2 * n + 1) for n in range(PW // PANEL)] + [("u", 2 * n + 1) for n in range(MW // PANEL)]
                      + [("v", NT * n + NT - 1) for n in range(H)] + [("o", 2 * n + 1) for n in range(MW // PANEL)])

        S_AT = [(2, 0), (3, 0), (4, 0), (4, 256)]
        NORM0, NORM_H = 0, NT
        NORM1 = NORM_H + H * NT
        NORM2 = NORM1 + NT
        W_AT = [0, 512, 896, 1152]

        block = ctx.enter_context(nc.Block())

        @block.sync
        def _(sp):
            for i in range(NT):
                sp.dma_start(X0v[:, i, :], x_rows[P * i:P * (i + 1), :]).then_inc(x_landed[i], 16)
                if i == 0:
                    sp.dma_start(gain[:], A["ln0_g"].rearrange("(a d) -> a d", a=1).broadcast_to([P, D])).then_inc(ln_landed, 16)
                    sp.dma_start(bias[:], A["ln0_b"].rearrange("(a d) -> a d", a=1).broadcast_to([P, D])).then_inc(ln_landed, 16)
            sp.dma_start(cut(wif, 0, KD, 2 * H), w_in_k[:, :, COL_IF:COL_IF + 2 * H]).then_inc(wif_landed, 16)
            for n, (_, c0, _) in enumerate(PANELS):
                if n >= RING:
                    sp.wait_ge(gemm_done, at[PANEL_LAST[n - RING]] + 1)
                sp.dma_start(ring[:, n % RING], w_in_k[:, :, c0:c0 + PANEL]).then_inc(ring_landed[n % RING], 16)
                if n == 3:
                    sp.wait_ge(h0_ready, NT)
                    sp.dma_start(gain[:], A["ln1_g"].broadcast_to([P, D])).then_inc(ln1_landed, 16)
                    sp.dma_start(bias[:], A["ln1_b"].broadcast_to([P, D])).then_inc(ln1_landed, 16)
                if n == 5:
                    sp.dma_start(cut(wpool, 0, PG, PGD), A["w_pool"][0].rearrange("g c d -> c g d")).then_inc(wpool_landed, 16)
                if n == 7:
                    for h in range(H):
                        for j, name in enumerate(("w_q", "w_k")):
                            sp.dma_start(wqk[:, 2 * h + j], A[name][0, h].rearrange("(c p) e -> p c e", p=P)).then_inc(wqk_landed, 16)
            w_bp = A["w_branch_pool"][0].rearrange("(k p) n -> p k n", p=P)
            w_bm = A["w_branch_mlstm"][0].rearrange("(k p) n -> p k n", p=P)
            for m in range(KD):
                s = m % 2
                if m == 0:
                    sp.wait_ge(cols_ready, 1)
                if m == 1:
                    sp.wait_ge(gemm_done, len(order))
                    sp.wait_ge(hn_ready, H * NT)
                    sp.dma_start(wout, A["w_out"][0].rearrange("(k p) n -> p k n", p=P)).then_inc(wout_landed, 16)
                if m >= 2:
                    sp.wait_ge(y_done, m - 1)
                t = merge_w[s]
                for k0, src in ((0, w_in_k[:, :, COL_G + P * m:COL_G + P * (m + 1)]),
                                (KD, w_in_k[:, :, COL_G + D + P * m:COL_G + D + P * (m + 1)]),
                                (2 * KD, w_bp[:, :, P * m:P * (m + 1)]),
                                (2 * KD + PG, w_bm[:, :, P * m:P * (m + 1)])):
                    nk = src.shape[1]
                    sp.dma_start(t[:, k0:k0 + nk, :], src).then_inc(merge_landed[s], 16)
            sp.wait_ge(merged_ready, KD)

            def load_w1(it, e, first=False):
                for k in range(KD):
                    if not first:
                        sp.wait_ge(w1_used, KD * it - KD + k + 1)
                    elif k == KD - 1:
                        sp.wait_ge(wo_done, NT)
                    sp.dma_start(W1[:, k, :], A["w_e1"][0, e, P * k:P * (k + 1), :]).then_inc(w1_landed[k], 16)

            def load_w2(it, e, first=False):
                for k in range(KF // 2):
                    if not first:
                        sp.wait_ge(w2_used, (KF // 2) * it - KF // 2 + k + 1)
                    sp.dma_start(W2[:, k], A["w_e2"][0, e, 2 * P * k:2 * P * (k + 1), :].rearrange("(a p) n -> p a n", p=P)).then_inc(w2_landed[k], 16)

            load_w1(0, 0, first=True)
            load_w2(0, 0, first=True)
            load_w1(1, 1)
            sp.wait_ge(iter_ready, 1)
            n_it = sp.snap(sp.value_load(more_iter[0:1, 0:1], min_val=0, max_val=(ROUNDS - 1) * E) + E)
            with sp.Fori(1, n_it - 1) as it:
                load_w1(it + 1, sp.snap((it + 1) % E))
                load_w2(it, sp.snap(it % E))
            load_w2(n_it - 1, E - 1)

            for i in range(NT):
                sp.wait_ge(out_ready, i + 1)
                sp.dma_start(out_rows[P * i:P * (i + 1), :], X0v[:, i, :]).then_inc(out_stored, 16)
            sp.wait_ge(out_stored, 16 * NT)

        @block.gpsimd
        def _(pool):
            n_step = [0]

            def step(ins):
                n_step[0] += 1
                ins.then_inc(pool_step, 1)
                pool.wait_ge(pool_step, n_step[0])

            step(nc.gpsimd.memset(ident[:], 0.0))
            step(nc.gpsimd.affine_select(out=ident[:], in_=ident[:], compare_op=ALU.not_equal, fill=1.0, base=0,
                                         pattern=[[-1, P]], channel_multiplier=1))
            nc.gpsimd.memset(ones[:], 1.0).then_inc(consts_made, 1)
            nc.gpsimd.memset(uT[:, :, 0:CPAD], 0.0).then_inc(pads_made, 1)
            nc.gpsimd.memset(pT[:, :, 0:PAD], 0.0).then_inc(pads_made, 1)
            nc.gpsimd.memset(v_sb[:, :, :, DH:VW], 1.0).then_inc(pads_made, 1)
            step(nc.gpsimd.memset(tri[:], 1.0))
            step(nc.gpsimd.memset(tri_strict[:], 1.0))
            step(nc.gpsimd.affine_select(out=tri[:], in_=tri[:], compare_op=ALU.is_ge, fill=0.0, base=0,
                                         pattern=[[1, P]], channel_multiplier=-1))
            step(nc.gpsimd.affine_select(out=tri_strict[:], in_=tri_strict[:], compare_op=ALU.is_gt, fill=0.0, base=0,
                                         pattern=[[1, P]], channel_multiplier=-1))
            step(nc.gpsimd.memset(head_sel[:], 1.0))
            hs = cut(head_sel, 0, H, P)
            step(nc.gpsimd.affine_select(out=hs, in_=hs, compare_op=ALU.is_equal, fill=0.0, base=0,
                                         pattern=[[-1, H], [0, P]], channel_multiplier=1))
            step(nc.gpsimd.memset(bias_sel, 0.0))
            step(nc.gpsimd.memset(bias_sel[0:1, :], 1.0))
            for t in range(PAD):
                nc.gpsimd.memset(inv_cnt[:, t:t + 1], 1.0 / (t + 1))
            step(nc.gpsimd.iota(iota_e[:], pattern=[[1, E]], base=0, channel_multiplier=0, allow_small_or_imprecise_dtypes=True))
            step(nc.gpsimd.iota(slot_id[:], pattern=[[1, TOPK], [TOPK * P, NT]], base=-NO_TOKEN, channel_multiplier=TOPK, allow_small_or_imprecise_dtypes=True))
            for g in range(CG):
                step(nc.gpsimd.memset(quarter[TB * g:TB * (g + 1), :], float(g)))
            nc.gpsimd.memset(stat[:, 67:68], 0.0).then_inc(consts_made, 1)

            def add_bias(n, i, done):
                pool.wait_ge(gained, n + 1)
                nc.gpsimd.tensor_tensor(X0v[:, i, :], X0v[:, i, :], bias[:], ALU.add).then_inc(done, 1)

            for i in range(NT):
                add_bias(i, i, h0_ready)

            for g in range(PG):
                pool.wait_ge(gemm_out, g + 1)
                src = pT[:, g, :]
                for lvl in range(g + 1):
                    sh = 1 << lvl
                    if lvl == g:
                        step(nc.gpsimd.tensor_tensor(pool_w[:, g, :], src[:, PAD:PST], src[:, PAD - sh:PST - sh], ALU.add))
                    else:
                        lo = 2 * sh - 1
                        d = cut(hn, 0, PST) if lvl % 2 == 0 else cut(P1, 0, PST)
                        step(nc.gpsimd.tensor_tensor(d[:, lo:PST], src[:, lo:PST], src[:, lo - sh:PST - sh], ALU.add))
                        src = d
                w = WINDOWS[g]
                step(nc.gpsimd.tensor_tensor(pool_w[:, g, 0:w], pool_w[:, g, 0:w], inv_cnt[:, 0:w], ALU.mult))
                step(nc.gpsimd.tensor_scalar(pool_w[:, g, w:S], pool_w[:, g, w:S], 1.0 / w, None, ALU.mult))
                nc.gpsimd.tensor_tensor(pool_w[:, g, :], pool_w[:, g, :], pT[:, g, PAD:PST], ALU.subtract).then_inc(pooled_ready, 1)

            pool.wait_ge(pv_done, H * NT)
            step(nc.gpsimd.iota(iota_row, pattern=[[1, P]], base=0, channel_multiplier=0, allow_small_or_imprecise_dtypes=True))
            step(nc.gpsimd.memset(idx_table[:, N_ITER:N_ITER + 1], NO_TOKEN))
            step(nc.gpsimd.memset(spread, 1.0))
            sv = spread.rearrange("p (b g t) -> p b g t", b=NB, g=CG)
            nc.gpsimd.affine_select(out=sv, in_=sv, compare_op=ALU.is_equal, fill=0.0, base=0,
                                    pattern=[[-1, NB], [0, CG], [-NB, TB]], channel_multiplier=1).then_inc(dispatch_consts, 1)
            for i in range(NT):
                add_bias(NT + i, i, x1_ready)
            pool.wait_ge(wo_done, NT)
            nc.gpsimd.memset(rest[:, 2048:5120], 0.0).then_inc(bias_zeroed, 1)
            step(nc.gpsimd.memset(xg, 0.0))
            pool.wait_ge(x1_stored, 16 * NT)
            pool.wait_ge(tables_ready, 2)

            def own_wait():
                pool.sem_inc(pool_mark, 1)

            def gather(it, first=False):
                if not first:
                    pool.wait_ge(x_tr, it)
                    own_wait()
                nc.gpsimd.tensor_copy(idx[:], idx_table[:, bass.ds(it, 1)]).then_inc(idx_ready, 1)
                pool.wait_ge(idx_ready, it + 1)
                own_wait()
                pool.indirect_dma_start(out=xg, out_offset=None, in_=x1_dram,
                                        in_offset=bass.IndirectOffsetOnAxis(ap=idx[:, 0:1], axis=0),
                                        bounds_check=S - 1, oob_is_err=False).then_inc(xg_landed, 16)

            def scatter(it):
                pool.wait_ge(y_ready, it + 1)
                own_wait()
                nc.gpsimd.tensor_copy(slot[:], slot_table[:, bass.ds(it * NB - NB, NB)]).then_inc(slot_ready, 1)
                pool.wait_ge(slot_ready, it)
                own_wait()
                for b in range(NB):
                    pool.indirect_dma_start(out=y_quarters, out_offset=bass.IndirectOffsetOnAxis(ap=slot[:, b:b + 1], axis=0),
                                            in_=yS[:, b, :], in_offset=None,
                                            bounds_check=S * TOPK * CG - 1, oob_is_err=False).then_inc(y_stored, 16)

            gather(0, first=True)
            pool.wait_ge(x_tr, 1)
            gather(1)
            n_it = pool.snap(pool.value_load(more_iter[0:1, 0:1], min_val=0, max_val=(ROUNDS - 1) * E) + E)
            with pool.Fori(1, n_it) as it:
                gather(it + 1)
                scatter(it)
            scatter(n_it)
            pool.wait_ge(ln2_landed, 32)
            for i in range(NT):
                add_bias(2 * NT + i, i, out_ready)

        @block.scalar
        def _(act):
            n_step = [0]

            def step(ins):
                n_step[0] += 1
                ins.then_inc(act_step, 1)
                act.wait_ge(act_step, n_step[0])

            act.dma_start(chan_rows[0:TAPS * MC, :], A["conv_w"][0].rearrange("t (c p) -> (t c) p", p=P)).then_inc(small_landed, 16)
            r0 = TAPS * MC
            for name, n in (("conv_b", MC), ("mh_gain", MC), ("b_pool", PG), ("ls_pool", PG)):
                act.dma_start(chan_rows[r0:r0 + n, :], A[name][0].rearrange("(c p) -> c p", p=P)).then_inc(small_landed, 16)
                r0 += n
            for j in range(2):
                act.dma_start(gate_b[0:H, j:j + 1], A["b_if"][0, H * j:H * (j + 1)].rearrange("(h a) -> h a", a=1)).then_inc(small_landed, 16)
            act.dma_start(wrv, A["w_router"][0].rearrange("(k p) e -> p k e", p=P)).then_inc(router_landed, 16)
            act.dma_start(br[:], A["b_router"][0:1, :].broadcast_to([P, E])).then_inc(router_landed, 16)

            def rstd(n):
                s0 = 16 * (n % 4)
                act.wait_ge(var_ready, n + 1)
                step(act.activation(stat[:, s0 + 14:s0 + 15], stat[:, s0 + 13:s0 + 14], ACT.Ln))
                act.activation(stat[:, s0 + 14:s0 + 15], stat[:, s0 + 14:s0 + 15], ACT.Exp, scale=-0.5).then_inc(rstd_ready, 1)

            rstd(NORM0)
            rstd(NORM0 + 1)
            act.wait_ge(chan_tr, 1)
            act.activation(chan[:, 0:56], ps[:, 3, 0:56], ACT.Copy).then_inc(chan_ready, 1)
            for i in range(NT):
                if i + 2 < NT:
                    rstd(NORM0 + i + 2)
                act.wait_ge(h0_tr, i + 1)
                b = 4 + 2 * (i % 2)
                act.activation(h0T[:, :, P * i:P * (i + 1)], ps[:, b:b + 2, :].rearrange("p b (c t) -> p (b c) t", t=P), ACT.Copy).then_inc(h0T_ready, 1)

            def take(what, dst, func=ACT.Copy, scale=1.0):
                n = at[what]
                act.wait_ge(gemm_done, n + 1)
                act.activation(dst, ps[:, n % 2, 0:dst_cols(dst)], func, scale=scale).then_inc(gemm_out, 1)

            def dst_cols(dst):
                return dst.shape[-1]

            act.wait_ge(if_done, 2)
            act.wait_ge(small_landed, 16 * 7)
            step(act.activation(t0_row, ps[0:H, 3, :], ACT.Abs, bias=gate_b[0:H, 1:2]))
            step(act.activation(t0_row, t0_row, ACT.Exp, scale=-1.0))
            act.activation(t0_row, t0_row, ACT.Ln, bias=1.0).then_inc(log_ready, 1)
            act.wait_ge(pads_made, 3)
            for g in range(PG):
                take(("p", g), pT[:, g, PAD:PST])
            act.wait_ge(tot_ready, 1)
            act.activation(em_row, em_row, ACT.Exp, scale=-1.0).then_inc(em_ready, 1)
            for c in range(MC):
                take(("u", c), uT[:, c, CPAD:CPAD + S])
            for h in range(H):
                for i in range(NT):
                    take(("v", NT * h + i), v_sb[:, i, h, 0:DH])
            for c in range(MC):
                act.wait_ge(conv_ready, c + 1)
                act.activation(ucT[:, c, :], ucT[:, c, :], ACT.Silu).then_inc(silu_ready, 1)

            def head_qk(h):
                for e in range(EC):
                    take(("qk", 2 * EC * h + e), qT[:, e, :], scale=float(DH) ** -0.5)
                for e in range(EC):
                    take(("qk", 2 * EC * h + EC + e), kT[:, e, :])

            def head_exp(h):
                for j in range(NT):
                    act.wait_ge(arg_ready, NT * h + j + 1)
                    w = wtmp[:, W_AT[j]:W_AT[j] + S - P * j]
                    act.activation(w, w, ACT.Exp, scale=-1.0).then_inc(w_ready, 1)

            act.wait_ge(pooled_ready, PG)
            act.wait_ge(mix_done, PG)
            head_qk(0)
            head_exp(0)
            for h in range(H):
                if h + 1 < H:
                    head_qk(h + 1)
                    head_exp(h + 1)
                for c in range(EC):
                    if h >= 1:
                        act.wait_ge(hout_ready, EC * (h - 1) + c + 1)
                    take(("o", EC * h + c), sig_o[c], ACT.Sigmoid)
                for i in range(NT):
                    rstd(NORM_H + NT * h + i)
                for c in range(EC):
                    take(("tr", EC * h + c), hnT[:, EC * h + c, 0:S])
            for m in range(KD):
                act.wait_ge(gate_done, m + 1)
                if m < 2:
                    act.wait_ge(hout_ready, MC)
                else:
                    act.wait_ge(merged_ready, m - 1)
                b = 2 if m % 2 == 0 else 6
                act.activation(sig[:, m % 2, :], ps[:, b:b + 2, :].rearrange("p b t -> p (b t)"), ACT.Sigmoid).then_inc(gate_ready, 1)
            for i in range(NT):
                rstd(NORM1 + i)
                act.wait_ge(x1_ready, i + 1)
                act.dma_start(x1_dram[P * i:P * (i + 1), :], X0v[:, i, :]).then_inc(x1_stored, 16)
                act.wait_ge(x1_tr, i + 1)
                act.activation(x1Tv[:, :, P * i:P * (i + 1)], ps[:, 0:2, :].rearrange("p b (c t) -> p (b c) t", t=P), ACT.Copy).then_inc(x1T_ready, 1)
            act.wait_ge(dist_ready, 1)
            act.activation(gatew[:], gatew[:], ACT.Exp).then_inc(router_exp, 1)

            act.wait_ge(iter_ready, 1)
            act.dma_start(gain[:], A["ln2_g"].broadcast_to([P, D])).then_inc(ln2_landed, 16)
            act.dma_start(bias[:], A["ln2_b"].broadcast_to([P, D])).then_inc(ln2_landed, 16)
            n_it = act.snap(act.value_load(more_iter[0:1, 0:1], min_val=0, max_val=(ROUNDS - 1) * E) + E)

            def take_xT(it1):
                act.wait_ge(x_tr, it1)
                act.activation(xT.rearrange("p c b t -> p c t b"), ps[:, 6:8, :].rearrange("p a (c t b) -> p (a c) t b", t=TB, b=NB), ACT.Copy).then_inc(xT_ready, 1)

            def take_actT(it):
                act.wait_ge(act_tr, it)
                act.activation(rest[:, 9216:10240], ps[:, 6:8, :].rearrange("p b t -> p (b t)"), ACT.Copy).then_inc(actT_ready, 1)

            def glu_sigmoid(it1):
                act.wait_ge(swiglu_step, it1)
                act.activation(sS, gS, ACT.Sigmoid, scale=GLU_ALPHA).then_inc(sig_ready, 1)

            def load_b1(e):
                act.dma_start(b1_row[0:1, :], A["b_e1"][0, bass.ds(e, 1), :]).then_inc(b1_landed, 16)

            def load_b2(e):
                act.dma_start(b2_row[0:1, :], A["b_e2"][0, bass.ds(e, 1), :]).then_inc(b2_landed, 16)

            act.wait_ge(bias_zeroed, 1)
            load_b1(0)
            take_xT(1)
            take_xT(2)
            glu_sigmoid(1)
            load_b1(1)
            take_actT(1)
            with act.Fori(1, n_it) as it:
                act.wait_ge(y_ready, it)
                load_b2(act.snap((it - 1) % E))
                take_xT(it + 2)
                glu_sigmoid(it + 1)
                load_b1(act.snap((it + 1) % E))
                take_actT(it + 1)
            act.wait_ge(y_ready, n_it)
            load_b2(E - 1)
            act.wait_ge(b1_landed, n_it * 16 + 16)
            act.wait_ge(w2_used, n_it * (KF // 2))
            act.wait_ge(y_stored, n_it * (16 * NB))
            for i in range(NT):
                act.dma_start(yg[:, i], y_dram[P * i:P * (i + 1)]).then_inc(yg_landed[i], 16)
            for i in range(NT):
                rstd(NORM2 + i)

        @block.vector
        def _(dve):
            n_step = [0]

            def step(ins):
                n_step[0] += 1
                ins.then_inc(dve_step, 1)
                dve.wait_ge(dve_step, n_step[0])

            n_norm = [0]

            def statistics(n, src, width):
                s0 = 16 * (n % 4)
                pieces = max(1, width // BANK)
                w = width // pieces
                for a in range(pieces):
                    step(nc.vector.bn_stats(stat[:, s0 + 6 * a:s0 + 6 * a + 6], src[:, w * a:w * (a + 1)]))
                step(nc.vector.bn_aggr(stat[:, s0 + 12:s0 + 14], stat[:, s0:s0 + 6 * pieces]))
                nc.vector.tensor_scalar(stat[:, s0 + 13:s0 + 14], stat[:, s0 + 13:s0 + 14], LN_EPS, None, ALU.add).then_inc(var_ready, 1)

            def apply(n, t):
                s0 = 16 * (n % 4)
                var, y, q = stat[:, s0 + 13:s0 + 14], stat[:, s0 + 14:s0 + 15], stat[:, s0 + 15:s0 + 16]
                dve.wait_ge(rstd_ready, n + 1)
                step(nc.vector.scalar_tensor_tensor(out=q, in0=y, scalar=var, in1=y, op0=ALU.mult, op1=ALU.mult))
                step(nc.vector.tensor_scalar(q, q, -0.5, 1.5, ALU.mult, ALU.add))
                step(nc.vector.tensor_tensor(y, y, q, ALU.mult))
                return nc.vector.tensor_scalar(t, t, stat[:, s0 + 12:s0 + 13], stat[:, s0 + 14:s0 + 15], ALU.subtract, ALU.mult)

            def layer_norm_tail(n, t):
                step(apply(n, t))
                nc.vector.tensor_tensor(t, t, gain[:], ALU.mult).then_inc(gained, 1)

            for i in range(NT):
                dve.wait_ge(x_landed[i], 16)
                t = X0v[:, i, :]
                statistics(NORM0 + i, t, D)
                if i == 0:
                    dve.wait_ge(ln_landed, 32)
                if i >= 1:
                    layer_norm_tail(NORM0 + i - 1, X0v[:, i - 1, :])
            layer_norm_tail(NORM0 + NT - 1, X0v[:, NT - 1, :])

            dve.wait_ge(if_done, 2)
            dve.wait_ge(small_landed, 16 * 7)
            dve.wait_ge(log_ready, 1)
            step(nc.vector.tensor_scalar(t1_row, ps[0:H, 3, :], gate_b[0:H, 1:2], 0.0, ALU.add, ALU.min))
            step(nc.vector.tensor_tensor(t1_row, t1_row, t0_row, ALU.subtract))
            dve.wait_ge(consts_made, 2)
            step(nc.vector.tensor_tensor_scan(f_row, ones[0:H, 0:S], t1_row, 0.0, ALU.mult, ALU.add))
            step(nc.vector.scalar_tensor_tensor(out=a_row, in0=ps[0:H, 2, :], scalar=gate_b[0:H, 0:1], in1=f_row, op0=ALU.add, op1=ALU.subtract))
            step(nc.vector.tensor_tensor_scan(m_row, ones[0:H, 0:S], a_row, 0.0, ALU.mult, ALU.max))
            nc.vector.tensor_tensor(em_row, f_row, m_row, ALU.add).then_inc(tot_ready, 1)

            dve.wait_ge(chan_ready, 1)
            r_b, r_g, r_bp, r_ls = TAPS * MC, (TAPS + 1) * MC, (TAPS + 2) * MC, (TAPS + 2) * MC + PG
            for c in range(MC):
                dve.wait_ge(gemm_out, PG + c + 1)
                for j in range(TAPS):
                    src = uT[:, c, j:j + S]
                    tap = chan[:, MC * j + c:MC * j + c + 1]
                    if j == 0:
                        step(nc.vector.tensor_scalar(ucT[:, c, :], src, tap, chan[:, r_b + c:r_b + c + 1], ALU.mult, ALU.add))
                        continue
                    ins = nc.vector.scalar_tensor_tensor(out=ucT[:, c, :], in0=src, scalar=tap, in1=ucT[:, c, :], op0=ALU.mult, op1=ALU.add)
                    if j == TAPS - 1:
                        ins.then_inc(conv_ready, 1)
                    else:
                        step(ins)
            dve.wait_ge(rows_tr, 1)
            nc.vector.tensor_copy(cols[:], ps[:, 2, 0:NT * 2 * H]).then_inc(cols_ready, 1)
            for g in range(PG):
                dve.wait_ge(mix_done, g + 1)
                nc.vector.tensor_scalar(mixT[:, g, :], ps[:, 4 + g % 2, :], chan[:, r_bp + g:r_bp + g + 1], chan[:, r_ls + g:r_ls + g + 1],
                                        ALU.add, ALU.mult).then_inc(mixT_ready, 1)

            dve.wait_ge(cols_ready, 1)

            def head_args(h):
                dve.wait_ge(mb_done, h + 1)
                for j in range(NT):
                    if h >= 1:
                        dve.wait_ge(p_ready, NT * (h - 1) + j + 1)
                    nc.vector.tensor_scalar(wtmp[:, W_AT[j]:W_AT[j] + S - P * j], ps[:, 5, P * j:S], colv[:, j, h:h + 1], 0.0,
                                            ALU.subtract, ALU.max).then_inc(arg_ready, 1)

            def head_p(h):
                if h >= 2:
                    dve.wait_ge(pv_done, NT * (h - 1))
                dve.wait_ge(sc_done, h + 1)
                for j in range(NT):
                    dve.wait_ge(w_ready, NT * h + j + 1)
                    w = wtmp[:, W_AT[j]:W_AT[j] + S - P * j]
                    step(nc.vector.tensor_tensor(w[:, 0:P], w[:, 0:P], tri[:], ALU.mult))
                    b, c0 = S_AT[j]
                    nc.vector.tensor_tensor(Pm[h % 2][:, j, P * j:S], ps[:, b, c0:c0 + S - P * j], w, ALU.mult).then_inc(p_ready, 1)

            def head_norm(h):
                for i in range(NT):
                    n = NT * h + i
                    dve.wait_ge(pv_done, n + 1)
                    acc_ps = ps[:, 6 + n % 2, 0:VW]
                    step(nc.vector.tensor_scalar(stat[:, 64:65], acc_ps[:, DH:VW], -1.0, colv[:, i, H + h:H + h + 1], ALU.mult, ALU.max))
                    step(nc.vector.tensor_tensor(stat[:, 64:65], acc_ps[:, DH:VW], stat[:, 64:65], ALU.max))
                    step(nc.vector.reciprocal(stat[:, 65:66], stat[:, 64:65]))
                    if h >= 1 and i == 0:
                        dve.wait_ge(gemm_done, at[("tr", EC * h - 1)] + 1)
                    nc.vector.tensor_scalar(hnv[:, i, :], acc_ps[:, 0:DH], stat[:, 65:66], None, ALU.mult).then_inc(num_read, 1)
                    dve.wait_ge(num_read, n + 1)
                    statistics(NORM_H + n, hnv[:, i, :], DH)
                    if i >= 1:
                        apply(NORM_H + n - 1, hnv[:, i - 1, :]).then_inc(hn_ready, 1)
                apply(NORM_H + NT * h + NT - 1, hnv[:, NT - 1, :]).then_inc(hn_ready, 1)

            head_args(0)
            head_p(0)
            for h in range(H):
                if h + 1 < H:
                    head_args(h + 1)
                    head_p(h + 1)
                head_norm(h)
                for c in range(EC):
                    m = EC * h + c
                    dve.wait_ge(gemm_out, at[("tr", m)] + 1)
                    nc.vector.scalar_tensor_tensor(out=hnT[:, m, 0:S], in0=hnT[:, m, 0:S], scalar=chan[:, r_g + m:r_g + m + 1],
                                                   in1=sig_o[c], op0=ALU.mult, op1=ALU.mult).then_inc(hout_ready, 1)

            for m in range(KD):
                dve.wait_ge(gate_ready, m + 1)
                dve.wait_ge(y_done, m + 1)
                b = 4 if m % 2 == 0 else 0
                g = sig[:, m % 2, :]
                step(nc.vector.tensor_tensor(g, g, ps[:, b:b + 2, :].rearrange("p b t -> p (b t)"), ALU.mult))
                nc.vector.tensor_tensor(mergedT[:, m, :], g[:, 0:S], g[:, BANK:BANK + S], ALU.add).then_inc(merged_ready, 1)

            dve.wait_ge(ln1_landed, 32)
            for i in range(NT):
                dve.wait_ge(wo_done, i + 1)
                b = 2 + 2 * (i % 3)
                t = X0v[:, i, :]
                nc.vector.scalar_tensor_tensor(out=t, in0=t, scalar=DEEP_ALPHA, in1=ps[:, b:b + 2, :].rearrange("p b t -> p (b t)"),
                                               op0=ALU.mult, op1=ALU.add).then_inc(wo_read, 1)
                dve.wait_ge(wo_read, i + 1)
                statistics(NORM1 + i, t, D)
                layer_norm_tail(NORM1 + i, t)

            dve.wait_ge(router_landed, 32)
            dve.wait_ge(logits_done, 1)
            lg = cut(logits, 0, NT, E)
            step(nc.vector.tensor_tensor(lg, ps[:, 4, 0:NT * E].rearrange("p (i e) -> p i e", e=E),
                                         br[:].rearrange("p (a e) -> p a e", a=1).broadcast_to([P, NT, E]), ALU.add))
            topv = cut(top, 0, NT, 8)
            topiv = cut(topi, 0, NT, 8)
            for i in range(NT):
                step(nc.vector.max(topv[:, i, :], lg[:, i, :]))
                step(nc.vector.max_index(topiv[:, i, :], topv[:, i, :], lg[:, i, :]))
            gw = cut(gatew, 0, NT, TOPK)
            nc.vector.tensor_tensor(gw, topv[:, :, 0:TOPK], topv[:, :, 0:1].broadcast_to([P, NT, TOPK]), ALU.subtract).then_inc(dist_ready, 1)
            tf = cut(topf, 0, NT, TOPK)
            step(nc.vector.tensor_copy(tf, topiv[:, :, 0:TOPK]))
            oh = cut(onehot, 0, TOPK, NT, E)
            experts = iota_e[:].rearrange("p (a e) -> p a e", a=1).broadcast_to([P, NT, E])
            for k in range(TOPK):
                step(nc.vector.tensor_tensor(oh[:, k], experts, tf[:, :, k:k + 1].broadcast_to([P, NT, E]), ALU.is_equal))
            mk = cut(mask, 0, NT, E)
            step(nc.vector.tensor_tensor(mk, oh[:, 0], oh[:, 1], ALU.add))
            step(nc.vector.tensor_tensor(mk, mk, oh[:, 2], ALU.add))
            nc.vector.tensor_tensor(mk, mk, oh[:, 3], ALU.add).then_inc(mask_ready, 1)
            dve.wait_ge(router_exp, 1)
            gs = cut(gsum, 0, NT, 1)
            step(nc.vector.tensor_reduce(gs, gw, X_AXIS, ALU.add))
            step(nc.vector.reciprocal(gs, gs))
            step(nc.vector.tensor_tensor(gw, gw, gs.broadcast_to([P, NT, TOPK]), ALU.mult))

            dve.wait_ge(rank_done, 1)
            rk, rt, ri = cut(rank, 0, NT, E), cut(rtmp, 0, NT, E), cut(rint, 0, NT, E)
            rp = ps[:, 5, 0:NT * E].rearrange("p (i e) -> p i e", e=E)
            step(nc.vector.tensor_scalar(ri, rp, 1.0 / TB, 0.5 / TB - 0.5, ALU.mult, ALU.add))
            step(nc.vector.tensor_scalar(rt, ri, float(1 - NB * TB), None, ALU.mult))
            step(nc.vector.scalar_tensor_tensor(out=rk, in0=rp, scalar=float(NB), in1=rt, op0=ALU.mult, op1=ALU.add))
            step(nc.vector.tensor_scalar(ri, rp, 1.0 / CAP, 0.5 / CAP - 0.5, ALU.mult, ALU.add))
            step(nc.vector.tensor_copy(rt, ri))
            step(nc.vector.scalar_tensor_tensor(out=rk, in0=rt, scalar=float(-NB), in1=rk, op0=ALU.mult, op1=ALU.add))
            step(nc.vector.scalar_tensor_tensor(out=rt, in0=rt, scalar=float(E), in1=experts, op0=ALU.mult, op1=ALU.add))
            plv, itv, tk = cut(place, 0, TOPK, NT, 1), cut(itern, 0, TOPK, NT, 1), cut(logits, 0, NT, E)
            for k in range(TOPK):
                step(nc.vector.tensor_tensor(tk, oh[:, k], rk, ALU.mult))
                step(nc.vector.tensor_reduce(plv[:, k], tk, X_AXIS, ALU.add))
                step(nc.vector.tensor_tensor(tk, oh[:, k], rt, ALU.mult))
                step(nc.vector.tensor_reduce(itv[:, k], tk, X_AXIS, ALU.add))
            dve.wait_ge(dispatch_consts, 1)
            for n in range(TOPK * NT):
                nc.vector.tensor_scalar(place_oh[:, n, :], iota_row, place[:, n:n + 1], None, ALU.is_equal).then_inc(pos_ready, 1)
                nc.vector.tensor_scalar(iter_oh[:, n, :], iota_row, itern[:, n:n + 1], slot_id[:, n:n + 1], ALU.is_equal, ALU.mult).then_inc(pos_ready, 1)
            step(nc.vector.tensor_reduce(cnt[:, E:E + 1], ps[:, 5, NT * E:NT * E + E], X_AXIS, ALU.max))
            step(nc.vector.memset(cnt[:, E + 1:E + 2], 0.0))
            for r in range(1, ROUNDS):
                step(nc.vector.tensor_scalar(cnt[:, E + 2:E + 3], cnt[:, E:E + 1], float(CAP * r), float(E), ALU.is_gt, ALU.mult))
                step(nc.vector.tensor_tensor(cnt[:, E + 1:E + 2], cnt[:, E + 1:E + 2], cnt[:, E + 2:E + 3], ALU.add))
            blocksv = cut(blocks, 0, ROUNDS, E)
            for r in range(ROUNDS):
                step(nc.vector.tensor_scalar(blocksv[0:1, r, :], ps[0:1, 5, NT * E:NT * E + E], 1.0 / TB, (0.5 * (TB - 1) - CAP * r) / TB, ALU.mult, ALU.add))
            step(nc.vector.tensor_scalar(blocks[0:1, :], blocks[0:1, :], 1.0, float(NB), ALU.max, ALU.min))
            nc.vector.tensor_copy(more_iter[0:1, :], cnt[0:1, E + 1:E + 2]).then_inc(iter_ready, 1)
            dve.wait_ge(slots_done, 1)
            nc.vector.tensor_scalar(slots_f, ps[:, 4, 0:N_ITER], float(NO_TOKEN), None, ALU.add).then_inc(slots_read, 1)
            dve.wait_ge(slots_read, 1)
            nc.vector.tensor_scalar(idx_table[:, 0:N_ITER], slots_f, 1.0 / TOPK, -0.375, ALU.mult, ALU.add).then_inc(tables_ready, 1)
            dve.wait_ge(spread_done, 1)
            nc.vector.tensor_scalar(slot_table.rearrange("p (n b) -> p b n", b=NB), ps[:, 3, :].rearrange("p (b n) -> p b n", b=NB),
                                    float(CG), quarter[:, 0:1], ALU.mult, ALU.add).then_inc(tables_ready, 1)
            dve.wait_ge(iter_ready, 1)
            n_it = dve.snap(dve.value_load(more_iter[0:1, 0:1], min_val=0, max_val=(ROUNDS - 1) * E) + E)

            def swiglu(it1, first=False):
                dve.wait_ge(w1_used, it1 * KD)
                pair = ps[:, 0:NB, :].rearrange("p b (n two) -> p b n two", two=2)
                nc.vector.tensor_scalar(gS, pair[:, :, :, 0], GLU_LIMIT, None, ALU.min).then_inc(swiglu_step, 1)
                nc.vector.tensor_scalar(lS, pair[:, :, :, 1], GLU_LIMIT, -GLU_LIMIT, ALU.min, ALU.max).then_inc(h_read, 1)
                dve.wait_ge(h_read, it1)
                nc.vector.scalar_tensor_tensor(out=lS, in0=lS, scalar=1.0, in1=gS, op0=ALU.add, op1=ALU.mult).then_inc(lin_ready, 1)
                dve.wait_ge(lin_ready, it1)
                dve.wait_ge(sig_ready, it1)
                if not first:
                    dve.wait_ge(act_tr, it1 - 1)
                nc.vector.tensor_tensor(aS.rearrange("p b a n -> p b (a n)"), lS, sS, ALU.mult).then_inc(act_ready, 1)

            def take_y(it, first=False):
                dve.wait_ge(w2_used, it * (KF // 2))
                if not first:
                    dve.wait_ge(y_stored, 16 * NB * it - 16 * NB)
                nc.vector.tensor_copy(rest[:, 10240:11264], ps[:, 4:6, :].rearrange("p a n -> p (a n)")).then_inc(y_ready, 1)

            nc.vector.memset(stat[:, 66:67], 0.0).then_inc(y_ready, 1)
            for n in range(TOPK * NT):
                k, i = n // NT, n % NT
                nc.vector.tensor_scalar(gate_diag[:, n, :], ident[:], gw[:, i, k:k + 1], None, ALU.mult).then_inc(diags_ready, 1)
            swiglu(1, first=True)
            swiglu(2)
            take_y(1, first=True)
            with dve.Fori(2, n_it) as it:
                swiglu(it + 1)
                take_y(it)
            take_y(n_it)

            dve.wait_ge(ln2_landed, 32)
            for i in range(NT):
                t = X0v[:, i, :]
                dve.wait_ge(combined, i + 1)
                b = 2 * (i % 2)
                nc.vector.scalar_tensor_tensor(out=t, in0=t, scalar=DEEP_ALPHA, in1=ps[:, b:b + 2, :].rearrange("p b t -> p (b t)"),
                                               op0=ALU.mult, op1=ALU.add).then_inc(combined_read, 1)
                dve.wait_ge(combined_read, i + 1)
                statistics(NORM2 + i, t, D)
                layer_norm_tail(NORM2 + i, t)

        @block.tensor
        def _(pe):
            mm = nc.tensor.matmul
            pe.wait_ge(consts_made, 2)
            pe.wait_ge(small_landed, 16 * 7)
            nc.tensor.transpose(ps[:, 3, 0:56], chan_rows[0:56, :], ident[0:56, 0:56]).then_inc(chan_tr, 1)
            for i in range(NT):
                pe.wait_ge(h0_ready, i + 1)
                if i >= 2:
                    pe.wait_ge(h0T_ready, i - 1)
                b = 4 + 2 * (i % 2)
                for k in range(KD):
                    last = nc.tensor.transpose(ps[:, b + k // 4, P * (k % 4):P * (k % 4 + 1)], X0v[:, i, P * k:P * (k + 1)], ident[:])
                last.then_inc(h0_tr, 1)
            pe.wait_ge(h0T_ready, NT)
            pe.wait_ge(wif_landed, 16)
            pe.wait_ge(chan_ready, 1)
            wifv = cut(wif, 0, KD, 2 * H)
            for j in range(2):
                for k in range(KD):
                    last = mm(ps[0:H, 2 + j, :], wifv[:, k, H * j:H * (j + 1)], h0T[:, k, :], start=(k == 0), stop=(k == KD - 1))
                last.then_inc(if_done, 1)

            def bank_for(n):
                if n >= 2:
                    pe.wait_ge(gemm_out, n - 1)
                return n % 2

            n_out = 0
            for n, (kind, _, _) in enumerate(PANELS[:PW // PANEL + MW // PANEL + H]):
                pe.wait_ge(ring_landed[n % RING], 16 * (n // RING + 1))
                slot = ring[:, n % RING]
                if kind == "v":
                    for i in range(NT):
                        b = bank_for(n_out)
                        for k in range(KD):
                            last = mm(ps[:, b, 0:DH], h0T[:, k, P * i:P * (i + 1)], slot[:, k, :], start=(k == 0), stop=(k == KD - 1))
                        last.then_inc(gemm_done, 1)
                        n_out += 1
                else:
                    for c in range(2):
                        b = bank_for(n_out)
                        for k in range(KD):
                            last = mm(ps[:, b, :], slot[:, k, P * c:P * (c + 1)], h0T[:, k, :], start=(k == 0), stop=(k == KD - 1))
                        last.then_inc(gemm_done, 1)
                        n_out += 1
                if n == PW // PANEL + MW // PANEL - 1:
                    pe.wait_ge(tot_ready, 1)
                    pe.wait_ge(em_ready, 1)
                    for i in range(NT):
                        for j, r in enumerate((a_row, em_row)):
                            last = nc.tensor.transpose(ps[:, 2, 2 * H * i + H * j:2 * H * i + H * (j + 1)], r[:, P * i:P * (i + 1)], ident[0:H, 0:H])
                    last.then_inc(rows_tr, 1)
                    pe.wait_ge(wpool_landed, 16)
                    wpv = cut(wpool, 0, PG, PGD)
                    for g in range(PG):
                        pe.wait_ge(pooled_ready, g + 1)
                        if g >= 2:
                            pe.wait_ge(mixT_ready, g - 1)
                        mm(ps[:, 4 + g % 2, :], wpv[:, g, :], pool_w[:, g, :], start=True, stop=True).then_inc(mix_done, 1)

            def head_qk(h):
                if h == 0:
                    pe.wait_ge(wqk_landed, 16 * 2 * H)
                pe.wait_ge(silu_ready, EC * (h + 1))
                n = at[("qk", 2 * EC * h)]
                for j in range(2):
                    for e in range(EC):
                        b = bank_for(n)
                        for c in range(EC):
                            last = mm(ps[:, b, :], wqk[:, 2 * h + j, c, P * e:P * (e + 1)], ucT[:, EC * h + c, :], start=(c == 0), stop=(c == EC - 1))
                        last.then_inc(gemm_done, 1)
                        n += 1
                if h >= 1:
                    pe.wait_ge(arg_ready, NT * h)
                else:
                    pe.wait_ge(mixT_ready, PG)
                mm(ps[:, 5, :], cut(head_sel, 0, H, P)[0:H, h, :], m_row, start=True, stop=True).then_inc(mb_done, 1)
                pe.wait_ge(gemm_out, n)
                if h >= 1:
                    pe.wait_ge(p_ready, NT * h)
                else:
                    pe.wait_ge(cols_ready, 1)
                for j in range(NT):
                    b, c0 = S_AT[j]
                    for e in range(EC):
                        last = mm(ps[:, b, c0:c0 + S - P * j], kT[:, e, P * j:P * (j + 1)], qT[:, e, P * j:S], start=(e == 0), stop=(e == EC - 1))
                last.then_inc(sc_done, 1)

            def head_pv(h):
                for i in range(NT):
                    n = NT * h + i
                    pe.wait_ge(p_ready, n + 1)
                    if n >= 2:
                        pe.wait_ge(num_read, n - 1)
                    for j in range(i + 1):
                        last = mm(ps[:, 6 + n % 2, 0:VW], Pm[h % 2][:, j, P * i:P * (i + 1)], v_sb[:, j, h, :], start=(j == 0), stop=(j == i))
                    last.then_inc(pv_done, 1)

            def head_tr(h):
                pe.wait_ge(hn_ready, NT * (h + 1))
                for c in range(EC):
                    b = bank_for(at[("tr", EC * h + c)])
                    for i in range(NT):
                        last = nc.tensor.transpose(ps[:, b, P * i:P * (i + 1)], hnv[:, i, P * c:P * (c + 1)], ident[:])
                    last.then_inc(gemm_done, 1)

            head_qk(0)
            for h in range(H):
                if h + 1 < H:
                    head_qk(h + 1)
                n = PW // PANEL + MW // PANEL + H + h
                pe.wait_ge(ring_landed[n % RING], 16 * (n // RING + 1))
                for c in range(EC):
                    b = bank_for(at[("o", EC * h + c)])
                    for k in range(KD):
                        last = mm(ps[:, b, :], ring[:, n % RING][:, k, P * c:P * (c + 1)], h0T[:, k, :], start=(k == 0), stop=(k == KD - 1))
                    last.then_inc(gemm_done, 1)
                head_pv(h)
                head_tr(h)

            for m in range(KD):
                w = merge_w[m % 2]
                gb, yb = (2, 4) if m % 2 == 0 else (6, 0)
                pe.wait_ge(merge_landed[m % 2], 64 * (m // 2 + 1))
                if m >= 2:
                    pe.wait_ge(merged_ready, m - 1)
                if m == 1:
                    pe.wait_ge(gemm_out, len(order))
                for j in range(2):
                    for k in range(KD):
                        last = mm(ps[:, gb + j, :], w[:, KD * j + k, :], h0T[:, k, :], start=(k == 0), stop=(k == KD - 1))
                last.then_inc(gate_done, 1)
                if m == 0:
                    pe.wait_ge(hout_ready, MC)
                    pe.wait_ge(mixT_ready, PG)
                for k in range(PG):
                    mm(ps[:, yb, :], w[:, 2 * KD + k, :], mixT[:, k, :], start=(k == 0), stop=(k == PG - 1))
                for k in range(MC):
                    last = mm(ps[:, yb + 1, :], w[:, 2 * KD + PG + k, :], hnT[:, k, 0:S], start=(k == 0), stop=(k == MC - 1))
                last.then_inc(y_done, 1)

            def x1_transposes(i):
                pe.wait_ge(x1_ready, i + 1)
                if i >= 1:
                    pe.wait_ge(x1T_ready, i)
                for k in range(KD):
                    last = nc.tensor.transpose(ps[:, k // 4, P * (k % 4):P * (k % 4 + 1)], X0v[:, i, P * k:P * (k + 1)], ident[:])
                last.then_inc(x1_tr, 1)

            pe.wait_ge(wout_landed, 16)
            for i in range(NT):
                b = 2 + 2 * (i % 3)
                if i == 0:
                    pe.wait_ge(merged_ready, KD)
                if i == 3:
                    pe.wait_ge(wo_read, 1)
                for n in range(D // BANK):
                    for k in range(KD):
                        last = mm(ps[:, b + n, :], mergedT[:, k, P * i:P * (i + 1)], wout[:, k, BANK * n:BANK * (n + 1)], start=(k == 0), stop=(k == KD - 1))
                last.then_inc(wo_done, 1)
                if i >= 1:
                    x1_transposes(i - 1)
            x1_transposes(NT - 1)
            pe.wait_ge(router_landed, 32)
            pe.wait_ge(x1T_ready, NT)
            for i in range(NT):
                for k in range(KD):
                    last = mm(ps[:, 4, E * i:E * (i + 1)], x1Tv[:, k, P * i:P * (i + 1)], wrv[:, k, :], start=(k == 0), stop=(k == KD - 1))
            last.then_inc(logits_done, 1)
            pe.wait_ge(mask_ready, 1)
            mk = cut(mask, 0, NT, E)
            for i in range(NT):
                for j in range(i + 1):
                    mm(ps[:, 5, E * i:E * (i + 1)], tri_strict[:] if j == i else ones[:, 0:P], mk[:, j, :], start=(j == 0), stop=(j == i))
            for j in range(NT):
                last = mm(ps[:, 5, E * NT:E * (NT + 1)], ones[:, 0:P], mk[:, j, :], start=(j == 0), stop=(j == NT - 1))
            last.then_inc(rank_done, 1)

            for n in range(TOPK * NT):
                pe.wait_ge(pos_ready, 2 * n + 2)
                last = mm(ps[:, 4, 0:N_ITER], place_oh[:, n, :], iter_oh[:, n, :], start=(n == 0), stop=(n == TOPK * NT - 1))
            last.then_inc(slots_done, 1)
            pe.wait_ge(slots_read, 1)
            sv = cut(P1, 770, NB, P)
            for b in range(NB):
                last = mm(ps[:, 3, N_ITER * b:N_ITER * (b + 1)], sv[:, b, :], slots_f, start=True, stop=True)
            last.then_inc(spread_done, 1)

            def x_transposes(it1):
                pe.wait_ge(xg_landed, 16 * it1)
                for k in range(KD):
                    last = nc.tensor.transpose(ps[:, 6 + k // 4, P * (k % 4):P * (k % 4 + 1)], xg[:, P * k:P * (k + 1)], ident[:])
                last.then_inc(x_tr, 1)

            def fc1(it1, nb):
                pe.wait_ge(b1_landed, 16 * it1)
                for b in range(nb):
                    for g in range(CG):
                        mm(ps[TB * g:TB * (g + 1), b, :], bias_sel, b1_row[:, HW_ * g:HW_ * (g + 1)], start=True, stop=False)
                for k in range(KD):
                    pe.wait_ge(w1_landed[k], 16 * it1)
                    for b in range(nb):
                        for g in range(CG):
                            last = mm(ps[TB * g:TB * (g + 1), b, :], xT[:, k, b, :], W1[:, k, HW_ * g:HW_ * (g + 1)],
                                      start=False, stop=(k == KD - 1))
                    last.then_inc(w1_used, 1)

            def act_transposes(it):
                pe.wait_ge(act_ready, it)
                for b in range(NB):
                    for a in range(2):
                        last = nc.tensor.transpose(ps[:, 6 + b // 2, P * (2 * (b % 2) + a):P * (2 * (b % 2) + a + 1)], aS[:, b, a, :], ident[:])
                last.then_inc(act_tr, 1)

            def fc2(it, nb):
                pe.wait_ge(b2_landed, 16 * it)
                for b in range(nb):
                    for g in range(CG):
                        mm(ps[TB * g:TB * (g + 1), 4 + b // 2, YW * (b % 2):YW * (b % 2 + 1)], bias_sel, b2_row[:, YW * g:YW * (g + 1)],
                           start=(b % 2 == 0), stop=False, skip_group_check=True)
                for kk in range(KF // 2):
                    pe.wait_ge(w2_landed[kk], 16 * it)
                    for a in range(2):
                        k = 2 * kk + a
                        for b in range(nb):
                            for g in range(CG):
                                last = mm(ps[TB * g:TB * (g + 1), 4 + b // 2, YW * (b % 2):YW * (b % 2 + 1)],
                                          aT[:, b, k % 2, TB * (k // 2):TB * (k // 2 + 1)], W2[:, kk, a, YW * g:YW * (g + 1)],
                                          start=False, stop=(k == KF - 1), skip_group_check=True)
                    last.then_inc(w2_used, 1)

            def by_blocks(product, it, blocks):
                with pe.If(blocks < 3):
                    with pe.If(blocks < 2):
                        product(it, 1)
                    with pe.Else():
                        product(it, 2)
                with pe.Else():
                    with pe.If(blocks < 4):
                        product(it, 3)
                    with pe.Else():
                        product(it, 4)

            def blocks_of(n):
                return pe.value_load(blocks[0:1, bass.ds(n, 1)], min_val=1, max_val=NB)

            pe.wait_ge(iter_ready, 1)
            n_it = pe.snap(pe.value_load(more_iter[0:1, 0:1], min_val=0, max_val=(ROUNDS - 1) * E) + E)
            x_transposes(1)
            pe.wait_ge(xT_ready, 1)
            by_blocks(fc1, 1, blocks_of(0))
            x_transposes(2)
            pe.wait_ge(xT_ready, 2)
            act_transposes(1)
            with pe.Fori(1, n_it) as it:
                pe.wait_ge(h_read, it)
                by_blocks(fc1, it + 1, blocks_of(it))
                pe.wait_ge(actT_ready, it)
                x_transposes(it + 2)
                pe.wait_ge(y_ready, it)
                by_blocks(fc2, it, blocks_of(it - 1))
                pe.wait_ge(xT_ready, it + 2)
                act_transposes(it + 1)
            pe.wait_ge(actT_ready, n_it)
            pe.wait_ge(y_ready, n_it)
            by_blocks(fc2, n_it, blocks_of(n_it - 1))
            pe.wait_ge(diags_ready, TOPK * NT)
            pe.wait_ge(act_ready, n_it)
            for i in range(NT):
                pe.wait_ge(yg_landed[i], 16)
                if i >= 2:
                    pe.wait_ge(combined_read, i - 1)
                for n in range(D // BANK):
                    for k in range(TOPK):
                        last = mm(ps[:, 2 * (i % 2) + n, :], gate_diag[:, k * NT + i, :], yg[:, i, k, BANK * n:BANK * (n + 1)],
                                  start=(k == 0), stop=(k == TOPK - 1))
                last.then_inc(combined, 1)


NAMES = ["x", "ln0_g", "ln0_b", "w_in", "conv_w", "conv_b", "w_q", "w_k", "b_if", "mh_gain", "w_pool", "b_pool", "ls_pool",
         "w_branch_pool", "w_branch_mlstm", "w_out", "ln1_g", "ln1_b", "w_router", "b_router", "w_e1", "b_e1", "w_e2", "b_e2",
         "ln2_g", "ln2_b"]


def kernel(**inputs):
    import numpy as np
    import concourse.bacc as bacc
    from concourse.bass_utils import run_bass_kernel_spmd

    nc = bacc.Bacc("TRN2", target_bir_lowering=False, num_devices=1)
    arrays, aps = {}, {}
    for name in NAMES:
        a = np.ascontiguousarray(inputs[name])
        arrays[f"in_{name}"] = a
        aps[name] = nc.dram_tensor(f"in_{name}", a.shape, mybir.dt.from_np(a.dtype), kind="ExternalInput").ap()
    shape = inputs["x"].shape
    out = nc.dram_tensor("out_rows", shape, F32, kind="ExternalOutput").ap()
    build_program(nc, aps, out)
    r = run_bass_kernel_spmd(nc, [arrays], core_ids=[0])
    return r.results[0]["out_rows"]
```

```python
from contextlib import ExitStack

import concourse.bass as bass
from concourse import mybir

F32 = mybir.dt.float32
U32 = mybir.dt.uint32
I32 = mybir.dt.int32
ALU = mybir.AluOpType
ACT = mybir.ActivationFunctionType
X_AXIS = mybir.AxisListType.X

P = 128
BANK = 512


def build_program(nc, A, out):
    _, S, D = A["x"].shape
    NT = S // P
    KD = D // P
    _, TAPS, MW = A["conv_w"].shape
    _, H, DH, _ = A["w_q"].shape
    _, PG, PGD, _ = A["w_pool"].shape
    PW = PG * PGD
    _, _, E = A["w_router"].shape
    FF = A["w_e2"].shape[2]
    KF = FF // P
    MC = MW // P
    CHANNEL_ROWS = (TAPS + 2) * MC + 2 * PG
    EC = DH // P
    TOPK = 4
    LN_EPS = 1e-5
    DEEP_ALPHA = 2.0 ** 0.25
    GLU_ALPHA = 1.702
    GLU_LIMIT = 7.0
    COL_P, COL_U, COL_V, COL_O = 0, PW, PW + MW, PW + 2 * MW
    COL_IF = PW + 3 * MW
    COL_G = COL_IF + 2 * H
    PANEL = 2 * P
    RING = 4
    WINDOWS = [2 ** (g + 1) for g in range(PG)]
    PAD = WINDOWS[-1]
    CPAD = TAPS - 1
    UST = S + CPAD + 1
    PST = S + PAD
    VW = DH + 1
    W_COLS = NT * S - P * NT * (NT - 1) // 2
    CAP = P
    ROUNDS = S // CAP
    N_ITER = ROUNDS * E
    NO_TOKEN = 1 << 20
    CG = 4
    TB = P // CG
    NB = CAP // TB
    HW_ = 2 * FF // CG
    YW = D // CG
    assert DH == PANEL and HW_ == BANK and NT == 4 and KD == 8

    w_in = A["w_in"][0]
    w_in_k = w_in.rearrange("(k p) n -> p k n", p=P)
    x_rows = A["x"][0]
    out_rows = out[0]

    x1_dram = nc.dram_tensor("x1_rows", (S, D), F32, kind="Internal").ap()
    y_dram = nc.dram_tensor("expert_rows", (S, TOPK, D), F32, kind="Internal").ap()
    y_quarters = y_dram.rearrange("t k (g n) -> (t k g) n", g=CG)

    with ExitStack() as ctx:
        def sb(name, cols, dt=F32, parts=P):
            return ctx.enter_context(nc.sbuf_tensor(name, [parts, cols], dt))

        def sem(name):
            return ctx.enter_context(nc.semaphore(name))

        X0 = sb("X0", NT * D)
        gain = sb("ln_gain", D)
        bias = sb("ln_bias", D)
        W1_COLS, W2_COLS = KD * 2 * FF, KF * D
        XT_AT = D
        B1_AT = XT_AT + KD * CAP
        B2_AT = B1_AT + 2 * FF
        HID_AT = B2_AT + D
        HID_COLS = NB * HW_ // 2
        Y_AT = HID_AT + 5 * HID_COLS
        REST_COLS = max(Y_AT + NB * YW, RING * KD * PANEL + MC * S)
        big = sb("big", W1_COLS + W2_COLS + P)
        rest = sb("rest", REST_COLS)
        gate_area = sb("gate_area", KD * S)
        P1 = sb("P1", NT * S)
        hn = sb("hn", NT * DH)
        ident = sb("ident", P)
        tri = sb("tri", P)
        tri_strict = sb("tri_strict", P)
        ones = sb("ones", BANK)
        head_sel = sb("head_sel", H * P)
        chan_rows = sb("chan_rows", P)
        chan = sb("chan", 64)
        gate_b = sb("gate_b", 2)
        m_line = sb("m_line", S)
        cols = sb("gate_cols", NT * 2 * H)
        wif = sb("w_if", KD * 2 * H)
        inv_cnt = sb("inv_cnt", PAD)
        bias_sel = ctx.enter_context(nc.sbuf_tensor("bias_sel", [P, TB], F32))[:]
        stat = sb("stat", 96)
        wr = sb("w_router_sb", KD * E)
        br = sb("b_router_sb", E)
        top = sb("top", NT * 8)
        topi = sb("topi", NT * 8, U32)
        topf = sb("topf", NT * TOPK)
        gatew = sb("gatew", NT * TOPK)
        gsum = sb("gsum", 2 * NT)
        rint = chan_rows[:, 0:NT * E].bitcast(I32)
        iota_e = sb("iota_e", E)
        place = sb("place", TOPK * NT)
        itern = sb("itern", TOPK * NT)
        slot_id = sb("slot_id", TOPK * NT)
        slot = sb("slot", NB, U32)
        quarter = sb("quarter", 1)
        cnt = sb("cnt", E + 8)
        more_iter = sb("more_iter", 1, I32)
        idx = sb("idx", 1, U32)
        blocks = m_line[:, 0:ROUNDS * E].bitcast(I32)

        def cut(t, at, *shape):
            n = 1
            for s in shape:
                n *= s
            v = t[:, at:at + n]
            if len(shape) == 2:
                return v.rearrange("p (a b) -> p a b", a=shape[0])
            if len(shape) == 3:
                return v.rearrange("p (a b c) -> p a b c", a=shape[0], b=shape[1])
            return v

        U_AT = KD * S
        V_AT = U_AT + MC * UST
        MIX_AT = V_AT + NT * H * VW
        P_AT = MIX_AT + PG * S
        Q_AT = P_AT + PG * PST
        K_AT = Q_AT + EC * S
        QK_AT = Q_AT + PG * S
        TMP_AT = QK_AT + 2 * H * EC * DH
        SIG_O_AT = TMP_AT + W_COLS
        assert SIG_O_AT + S <= W1_COLS + W2_COLS + P and P_AT + KD * D <= TMP_AT
        UC_AT = RING * KD * PANEL
        MERGE_ROWS = 2 * KD + PG + MC
        X0v = cut(X0, 0, NT, D)
        h0T = cut(big, 0, KD, S)
        uT = cut(big, U_AT, MC, UST)
        hnT = uT
        v_sb = cut(big, V_AT, NT, H, VW)
        mixT = cut(big, MIX_AT, PG, S)
        pT = cut(big, P_AT, PG, PST)
        P0 = cut(big, P_AT, NT, S)
        pool_w = cut(big, Q_AT, PG, S)
        qT = cut(big, Q_AT, EC, S)
        kT = cut(big, K_AT, EC, S)
        wqk = cut(big, QK_AT, 2 * H, EC, DH)
        wtmp = cut(big, TMP_AT, W_COLS)
        wout = cut(big, P_AT, KD, D)
        sig = cut(big, TMP_AT, 2, 2 * BANK)
        sig_o = [gate_area[:, MERGE_ROWS * P:MERGE_ROWS * P + S], big[:, SIG_O_AT:SIG_O_AT + S]]
        ring = cut(rest, 0, RING, KD, PANEL)
        ucT = cut(rest, UC_AT, MC, S)
        mergedT = ucT
        merge_w = [cut(gate_area, 0, MERGE_ROWS, P), cut(rest, 0, MERGE_ROWS, P)]
        x1T = [cut(rest, HID_AT + KD * P * b, KD, P) for b in range(2)]
        Pm = [P0, cut(P1, 0, NT, S)]
        hnv = cut(hn, 0, NT, DH)
        m_row = m_line[0:H, :]
        tile_stats = cut(stat, 0, NT, 16)
        var_all, rstd_all, newton_all = (tile_stats[:, :, c:c + 1] for c in (13, 14, 15))
        SLOTS_AT = N_ITER + 2
        FLOAT_AT = SLOTS_AT + NB * N_ITER
        SPREAD_AT = FLOAT_AT + N_ITER
        IOTA_AT = SPREAD_AT + NB * P
        idx_table = P1[:, 0:N_ITER + 1].bitcast(U32)
        slot_table = P1[:, SLOTS_AT:FLOAT_AT].bitcast(U32)
        slots_f = P1[:, FLOAT_AT:SPREAD_AT]
        spread = P1[:, SPREAD_AT:IOTA_AT]
        iota_row = P1[:, IOTA_AT:IOTA_AT + P]
        chosen = cut(P1, IOTA_AT + P, TOPK, E)
        place_oh = cut(gate_area, 0, NT * TOPK, P)
        iter_oh = cut(gate_area, NT * TOPK * P, NT * TOPK, P)
        a_row, f_row, em_row = (gate_area[0:H, S * n:S * (n + 1)] for n in range(3))
        F_AT = 32
        t0_row, t1_row = (gate_area[F_AT:F_AT + H, S * n:S * (n + 1)] for n in range(3, 5))
        wpool = big[:, SIG_O_AT:SIG_O_AT + PG * PGD]
        onehot = hn[:, 0:TOPK * NT * E]
        logits, mask, rank, rtmp = (hn[:, NT * E * n:NT * E * (n + 1)] for n in range(TOPK, TOPK + 4))
        colv = cut(cols, 0, NT, 2 * H)
        wrv = cut(wr, 0, KD, E)
        W1 = cut(big, 0, KD, 2 * FF)
        W2 = cut(big, W1_COLS, KF // 2, 2, D)
        xg = cut(rest, 0, D)
        xT = cut(rest, XT_AT, KD, NB, TB)
        b1_row = rest[:, B1_AT:B2_AT]
        b2_row = rest[:, B2_AT:HID_AT]
        gS = cut(rest, HID_AT, NB, HW_ // 2)
        lS = cut(rest, HID_AT + HID_COLS, NB, HW_ // 2)
        sS = cut(rest, HID_AT + 2 * HID_COLS, NB, HW_ // 2)
        aS = cut(rest, HID_AT + 3 * HID_COLS, NB, 2, P)
        aT = cut(rest, HID_AT + 4 * HID_COLS, NB, 2, P)
        yS = cut(rest, Y_AT, NB, YW)
        gate_diag = place_oh
        yg = big[:, 0:NT * TOPK * D].rearrange("p (i k n) -> p i k n", i=NT, k=TOPK)

        ps = ctx.enter_context(nc.psum_tensor("ps", [P, 8, BANK], F32))

        x_landed = [sem(f"x_landed{i}") for i in range(NT)]
        ln_landed = sem("ln_landed")
        small_landed = sem("small_landed")
        wif_landed = sem("wif_landed")
        wpool_landed = sem("wpool_landed")
        wqk_landed = sem("wqk_landed")
        wout_landed = sem("wout_landed")
        router_landed = sem("router_landed")
        ring_landed = [sem(f"ring_landed{i}") for i in range(RING)]
        merge_landed = [sem(f"merge_landed{i}") for i in range(2)]
        pool_step = sem("pool_step")
        pool_mark = sem("pool_mark")
        consts_made = sem("consts_made")
        pads_made = sem("pads_made")
        dve_step = sem("dve_step")
        act_step = sem("act_step")
        h0_ready = sem("h0_ready")
        var_ready = sem("var_ready")
        rstd_ready = sem("rstd_ready")
        h0_tr = sem("h0_tr")
        h0T_ready = sem("h0T_ready")
        chan_tr = sem("chan_tr")
        chan_ready = sem("chan_ready")
        if_done = sem("if_done")
        log_ready = sem("log_ready")
        tot_ready = sem("tot_ready")
        em_ready = sem("em_ready")
        rows_tr = sem("rows_tr")
        cols_ready = sem("cols_ready")
        gemm_done = sem("gemm_done")
        gemm_out = sem("gemm_out")
        pooled_ready = sem("pooled_ready")
        mix_done = sem("mix_done")
        mixT_ready = sem("mixT_ready")
        conv_ready = sem("conv_ready")
        silu_ready = sem("silu_ready")
        mb_done = sem("mb_done")
        arg_ready = sem("arg_ready")
        w_ready = sem("w_ready")
        sc_done = sem("sc_done")
        p_ready = sem("p_ready")
        pv_done = sem("pv_done")
        num_read = sem("num_read")
        hn_ready = sem("hn_ready")
        hout_ready = sem("hout_ready")
        gate_done = sem("gate_done")
        gate_ready = sem("gate_ready")
        y_done = sem("y_done")
        merged_ready = sem("merged_ready")
        wo_done = sem("wo_done")
        wo_read = sem("wo_read")
        x1_ready = sem("x1_ready")
        x1_stored = sem("x1_stored")
        x1_tr = sem("x1_tr")
        x1T_ready = sem("x1T_ready")
        logits_done = sem("logits_done")
        router_exp = sem("router_exp")
        dist_ready = sem("dist_ready")
        mask_ready = sem("mask_ready")
        rank_done = sem("rank_done")
        rank_read = sem("rank_read")
        pos_ready = sem("pos_ready")
        dispatch_consts = sem("dispatch_consts")
        counted = sem("counted")
        slots_done = sem("slots_done")
        x1_scaled = sem("x1_scaled")
        fourth_added = sem("fourth_added")
        diags_ready = sem("diags_ready")
        combined = sem("combined")
        combined_read = sem("combined_read")
        slots_read = sem("slots_read")
        spread_done = sem("spread_done")
        tables_ready = sem("tables_ready")
        bias_zeroed = sem("bias_zeroed")
        iter_ready = sem("iter_ready")
        idx_ready = sem("idx_ready")
        slot_ready = sem("slot_ready")
        xg_landed = sem("xg_landed")
        w1_landed = [sem(f"w1_landed{k}") for k in range(KD)]
        w2_landed = [sem(f"w2_landed{k}") for k in range(KF // 2)]
        b1_landed = sem("b1_landed")
        b2_landed = sem("b2_landed")
        w1_used = sem("w1_used")
        w2_used = sem("w2_used")
        x_tr = sem("x_tr")
        xT_ready = sem("xT_ready")
        h_read = sem("h_read")
        glu_ready = sem("glu_ready")
        sig_ready = sem("sig_ready")
        lin_ready = sem("lin_ready")
        act_ready = sem("act_ready")
        act_tr = sem("act_tr")
        actT_ready = sem("actT_ready")
        y_ready = sem("y_ready")
        y_stored = sem("y_stored")
        yg_landed = [sem(f"yg_landed{i}") for i in range(NT)]
        ln2_landed = sem("ln2_landed")
        ln1_landed = sem("ln1_landed")
        out_ready = sem("out_ready")
        out_stored = sem("out_stored")

        PANELS = ([("v", COL_V + PANEL * n, n) for n in range(H)]
                  + [("p", COL_P + PANEL * n, n) for n in range(PW // PANEL)]
                  + [("u", COL_U + PANEL * n, n) for n in range(MW // PANEL)]
                  + [("o", COL_O + PANEL * n, n) for n in range(MW // PANEL)])
        V_ORDER = [NT * (h0 + h) + i for h0 in range(0, H, 2) for i in range(NT) for h in range(2)]
        order = [("v", n) for n in V_ORDER] + [("p", n) for n in range(PG)] + [("u", n) for n in range(MC)]
        order += [("qk", n) for n in range(2 * EC)]
        for h in range(H):
            order += [("qk", 2 * EC * (h + 1) + n) for n in range(2 * EC) if h + 1 < H]
            order += [("tr", EC * (h - 1) + n) for n in range(EC) if h >= 1]
            order += [("o", EC * h + n) for n in range(EC)]
        order += [("tr", EC * (H - 1) + n) for n in range(EC)]
        at = {what: n for n, what in enumerate(order)}
        PANEL_LAST = ([("v", NT * n + NT - 1) for n in range(H)] + [("p", 2 * n + 1) for n in range(PW // PANEL)]
                      + [("u", 2 * n + 1) for n in range(MW // PANEL)] + [("o", 2 * n + 1) for n in range(MW // PANEL)])

        S_AT = [(2, 0), (3, 0), (4, 0), (4, 256)]
        NORM0, NORM_H = 0, NT
        NORM1 = NORM_H + H
        NORM2 = NORM1 + NT
        W_AT = [S * j - P * j * (j - 1) // 2 for j in range(NT)]

        block = ctx.enter_context(nc.Block())

        @block.sync
        def _(sp):
            for i in range(NT):
                sp.dma_start(X0v[:, i, :], x_rows[P * i:P * (i + 1), :]).then_inc(x_landed[i], 16)
                if i == 0:
                    sp.dma_start(gain[:], A["ln0_g"].rearrange("(a d) -> a d", a=1).broadcast_to([P, D])).then_inc(ln_landed, 16)
                    sp.dma_start(bias[:], A["ln0_b"].rearrange("(a d) -> a d", a=1).broadcast_to([P, D])).then_inc(ln_landed, 16)
            for n, (_, c0, _) in enumerate(PANELS):
                if n >= RING:
                    sp.wait_ge(gemm_done, at[PANEL_LAST[n - RING]] + 1)
                sp.dma_start(ring[:, n % RING], w_in_k[:, :, c0:c0 + PANEL]).then_inc(ring_landed[n % RING], 16)
                if n == 1:
                    sp.dma_start(chan_rows[0:TAPS * MC, :], A["conv_w"][0].rearrange("t (c p) -> (t c) p", p=P)).then_inc(small_landed, 16)
                    r0 = TAPS * MC
                    for name, n in (("conv_b", MC), ("mh_gain", MC), ("b_pool", PG), ("ls_pool", PG)):
                        sp.dma_start(chan_rows[r0:r0 + n, :], A[name][0].rearrange("(c p) -> c p", p=P)).then_inc(small_landed, 16)
                        r0 += n
                    for j in range(2):
                        sp.dma_start(gate_b[F_AT * j:F_AT * j + H, j:j + 1], A["b_if"][0, H * j:H * (j + 1)].rearrange("(h a) -> h a", a=1)).then_inc(small_landed, 16)
                    sp.dma_start(wrv, A["w_router"][0].rearrange("(k p) e -> p k e", p=P)).then_inc(router_landed, 16)
                    sp.dma_start(br[:], A["b_router"][0:1, :].broadcast_to([P, E])).then_inc(router_landed, 16)
                    sp.dma_start(cut(wif, 0, KD, 2 * H), w_in_k[:, :, COL_IF:COL_IF + 2 * H]).then_inc(wif_landed, 16)
                if n == 3:
                    sp.wait_ge(h0_ready, NT)
                    sp.dma_start(gain[:], A["ln1_g"].broadcast_to([P, D])).then_inc(ln1_landed, 16)
                    sp.dma_start(bias[:], A["ln1_b"].broadcast_to([P, D])).then_inc(ln1_landed, 16)
                if n == 5:
                    sp.dma_start(cut(wpool, 0, PG, PGD), A["w_pool"][0].rearrange("g c d -> c g d")).then_inc(wpool_landed, 16)
                if n == 7:
                    for h in range(H):
                        for j, name in enumerate(("w_q", "w_k")):
                            sp.dma_start(wqk[:, 2 * h + j], A[name][0, h].rearrange("(c p) e -> p c e", p=P)).then_inc(wqk_landed, 16)
            w_bp = A["w_branch_pool"][0].rearrange("(k p) n -> p k n", p=P)
            w_bm = A["w_branch_mlstm"][0].rearrange("(k p) n -> p k n", p=P)
            for m in range(KD):
                s = m % 2
                if m == 0:
                    sp.wait_ge(cols_ready, 1)
                if m == 1:
                    sp.wait_ge(gemm_done, at[("o", MC - 1)] + 1)
                if m >= 2:
                    sp.wait_ge(y_done, m - 1)
                t = merge_w[s]
                for k0, src in ((0, w_in_k[:, :, COL_G + P * m:COL_G + P * (m + 1)]),
                                (KD, w_in_k[:, :, COL_G + D + P * m:COL_G + D + P * (m + 1)]),
                                (2 * KD, w_bp[:, :, P * m:P * (m + 1)]),
                                (2 * KD + PG, w_bm[:, :, P * m:P * (m + 1)])):
                    nk = src.shape[1]
                    sp.dma_start(t[:, k0:k0 + nk, :], src).then_inc(merge_landed[s], 16)
                if m == 1:
                    sp.wait_ge(gemm_done, len(order))
                    sp.dma_start(wout, A["w_out"][0].rearrange("(k p) n -> p k n", p=P)).then_inc(wout_landed, 16)
            sp.wait_ge(merged_ready, KD)

            def load_w1(it, e, first=False):
                for k in range(KD):
                    if not first:
                        sp.wait_ge(w1_used, KD * it - KD + k + 1)
                    elif k == KD - 1:
                        sp.wait_ge(wo_done, 2 * NT)
                    sp.dma_start(W1[:, k, :], A["w_e1"][0, e, P * k:P * (k + 1), :]).then_inc(w1_landed[k], 16)

            def load_w2(it, e, first=False):
                for k in range(KF // 2):
                    if not first:
                        sp.wait_ge(w2_used, (KF // 2) * it - KF // 2 + k + 1)
                    sp.dma_start(W2[:, k], A["w_e2"][0, e, 2 * P * k:2 * P * (k + 1), :].rearrange("(a p) n -> p a n", p=P)).then_inc(w2_landed[k], 16)

            load_w1(0, 0, first=True)
            load_w2(0, 0, first=True)
            load_w1(1, 1)
            sp.wait_ge(iter_ready, 1)
            n_it = sp.snap(sp.value_load(more_iter[0:1, 0:1], min_val=0, max_val=(ROUNDS - 1) * E) + E)
            with sp.Fori(1, n_it - 1) as it:
                load_w1(it + 1, sp.snap((it + 1) % E))
                load_w2(it, sp.snap(it % E))
            load_w2(n_it - 1, E - 1)

            for i in range(NT):
                sp.wait_ge(out_ready, i + 1)
                sp.dma_start(out_rows[P * i:P * (i + 1), :], X0v[:, i, :]).then_inc(out_stored, 16)
            sp.wait_ge(out_stored, 16 * NT)

        @block.gpsimd
        def _(pool):
            n_step = [0]

            def step(ins):
                n_step[0] += 1
                ins.then_inc(pool_step, 1)
                pool.wait_ge(pool_step, n_step[0])

            step(nc.gpsimd.memset(ident[:], 0.0))
            step(nc.gpsimd.affine_select(out=ident[:], in_=ident[:], compare_op=ALU.not_equal, fill=1.0, base=0,
                                         pattern=[[-1, P]], channel_multiplier=1))
            nc.gpsimd.memset(ones[:], 1.0).then_inc(consts_made, 1)
            nc.gpsimd.memset(uT[:, :, 0:CPAD], 0.0).then_inc(pads_made, 1)
            nc.gpsimd.memset(pT[:, :, 0:PAD], 0.0).then_inc(pads_made, 1)
            nc.gpsimd.memset(v_sb[:, :, :, DH:VW], 1.0).then_inc(pads_made, 1)
            step(nc.gpsimd.memset(tri[:], 1.0))
            step(nc.gpsimd.memset(tri_strict[:], 1.0))
            step(nc.gpsimd.affine_select(out=tri[:], in_=tri[:], compare_op=ALU.is_ge, fill=0.0, base=0,
                                         pattern=[[1, P]], channel_multiplier=-1))
            step(nc.gpsimd.affine_select(out=tri_strict[:], in_=tri_strict[:], compare_op=ALU.is_gt, fill=0.0, base=0,
                                         pattern=[[1, P]], channel_multiplier=-1))
            step(nc.gpsimd.memset(head_sel[:], 1.0))
            hs = cut(head_sel, 0, H, P)
            step(nc.gpsimd.affine_select(out=hs, in_=hs, compare_op=ALU.is_equal, fill=0.0, base=0,
                                         pattern=[[-1, H], [0, P]], channel_multiplier=1))
            step(nc.gpsimd.memset(bias_sel, 0.0))
            step(nc.gpsimd.memset(bias_sel[0:1, :], 1.0))
            for t in range(PAD):
                nc.gpsimd.memset(inv_cnt[:, t:t + 1], 1.0 / (t + 1))
            step(nc.gpsimd.iota(iota_e[:], pattern=[[1, E]], base=0, channel_multiplier=0, allow_small_or_imprecise_dtypes=True))
            step(nc.gpsimd.iota(slot_id[:], pattern=[[TOPK * P, NT], [1, TOPK]], base=-NO_TOKEN, channel_multiplier=TOPK, allow_small_or_imprecise_dtypes=True))
            for g in range(CG):
                step(nc.gpsimd.memset(quarter[TB * g:TB * (g + 1), :], float(g)))
            nc.gpsimd.memset(stat[:, 67:68], 0.0).then_inc(consts_made, 1)

            for g in range(PG):
                pool.wait_ge(gemm_out, at[("p", g)] + 1)
                src = pT[:, g, :]
                for lvl in range(g + 1):
                    sh = 1 << lvl
                    if lvl == g:
                        step(nc.gpsimd.tensor_tensor(pool_w[:, g, :], src[:, PAD:PST], src[:, PAD - sh:PST - sh], ALU.add))
                    else:
                        lo = 2 * sh - 1
                        d = cut(hn, 0, PST) if lvl % 2 == 0 else cut(P1, 0, PST)
                        step(nc.gpsimd.tensor_tensor(d[:, lo:PST], src[:, lo:PST], src[:, lo - sh:PST - sh], ALU.add))
                        src = d
                w = WINDOWS[g]
                step(nc.gpsimd.tensor_tensor(pool_w[:, g, 0:w], pool_w[:, g, 0:w], inv_cnt[:, 0:w], ALU.mult))
                step(nc.gpsimd.tensor_scalar(pool_w[:, g, w:S], pool_w[:, g, w:S], 1.0 / w, None, ALU.mult))
                nc.gpsimd.tensor_tensor(pool_w[:, g, :], pool_w[:, g, :], pT[:, g, PAD:PST], ALU.subtract).then_inc(pooled_ready, 1)

            pool.wait_ge(pv_done, H * NT)
            step(nc.gpsimd.iota(iota_row, pattern=[[1, P]], base=0, channel_multiplier=0, allow_small_or_imprecise_dtypes=True))
            step(nc.gpsimd.memset(idx_table[:, N_ITER:N_ITER + 1], NO_TOKEN))
            step(nc.gpsimd.memset(spread, 1.0))
            sv = spread.rearrange("p (b g t) -> p b g t", b=NB, g=CG)
            nc.gpsimd.affine_select(out=sv, in_=sv, compare_op=ALU.is_equal, fill=0.0, base=0,
                                    pattern=[[-1, NB], [0, CG], [-NB, TB]], channel_multiplier=1).then_inc(dispatch_consts, 1)
            pool.wait_ge(wo_done, 2 * NT)
            nc.gpsimd.memset(rest[:, B1_AT:HID_AT], 0.0).then_inc(bias_zeroed, 1)
            step(nc.gpsimd.memset(xg, 0.0))
            pool.wait_ge(x1_stored, 16 * NT)
            pool.wait_ge(tables_ready, 1)

            def own_wait():
                pool.sem_inc(pool_mark, 1)

            def gather(it, first=False):
                if not first:
                    pool.wait_ge(x_tr, it)
                    own_wait()
                nc.gpsimd.tensor_copy(idx[:], idx_table[:, bass.ds(it, 1)]).then_inc(idx_ready, 1)
                pool.wait_ge(idx_ready, it + 1)
                own_wait()
                pool.indirect_dma_start(out=xg, out_offset=None, in_=x1_dram,
                                        in_offset=bass.IndirectOffsetOnAxis(ap=idx[:, 0:1], axis=0),
                                        bounds_check=S - 1, oob_is_err=False).then_inc(xg_landed, 16)

            def scatter(it):
                pool.wait_ge(y_ready, it + 1)
                own_wait()
                nc.gpsimd.tensor_copy(slot[:], slot_table[:, bass.ds(it * NB - NB, NB)]).then_inc(slot_ready, 1)
                pool.wait_ge(slot_ready, it)
                own_wait()
                for b in range(NB):
                    pool.indirect_dma_start(out=y_quarters, out_offset=bass.IndirectOffsetOnAxis(ap=slot[:, b:b + 1], axis=0),
                                            in_=yS[:, b, :], in_offset=None,
                                            bounds_check=S * TOPK * CG - 1, oob_is_err=False).then_inc(y_stored, 16)

            gather(0, first=True)
            pool.wait_ge(x_tr, 1)
            gather(1)
            pool.wait_ge(tables_ready, 2)
            n_it = pool.snap(pool.value_load(more_iter[0:1, 0:1], min_val=0, max_val=(ROUNDS - 1) * E) + E)
            with pool.Fori(1, n_it) as it:
                gather(it + 1)
                scatter(it)
            scatter(n_it)
            pool.wait_ge(x1_scaled, 1)
            pool.wait_ge(diags_ready, TOPK * NT)
            for i in range(NT):
                pool.wait_ge(yg_landed[i], 16)
                row = yg[:, i, TOPK - 1, :]
                step(nc.gpsimd.tensor_scalar(row, row, gatew[:, TOPK * i + TOPK - 1:TOPK * (i + 1)], None, ALU.mult))
                nc.gpsimd.tensor_tensor(X0v[:, i, :], X0v[:, i, :], row, ALU.add).then_inc(fourth_added, 1)

        @block.scalar
        def _(act):
            n_step = [0]

            def step(ins):
                n_step[0] += 1
                ins.then_inc(act_step, 1)
                act.wait_ge(act_step, n_step[0])

            def rstd(n):
                s0 = 16 * (n % 4)
                act.wait_ge(var_ready, n + 1)
                step(act.activation(stat[:, s0 + 14:s0 + 15], stat[:, s0 + 13:s0 + 14], ACT.Ln))
                act.activation(stat[:, s0 + 14:s0 + 15], stat[:, s0 + 14:s0 + 15], ACT.Exp, scale=-0.5).then_inc(rstd_ready, 1)

            def take(what, dst, func=ACT.Copy, scale=1.0):
                n = at[what]
                act.wait_ge(gemm_done, n + 1)
                act.activation(dst, ps[:, n % 2, 0:dst_cols(dst)], func, scale=scale).then_inc(gemm_out, 1)

            def dst_cols(dst):
                return dst.shape[-1]

            def take_h0T(i):
                act.wait_ge(h0_tr, i + 1)
                b = 4 + 2 * (i % 2)
                act.activation(h0T[:, :, P * i:P * (i + 1)], ps[:, b:b + 2, :].rearrange("p b (c t) -> p (b c) t", t=P), ACT.Copy).then_inc(h0T_ready, 1)

            def take_v(n):
                take(("v", V_ORDER[n]), v_sb[:, V_ORDER[n] % NT, V_ORDER[n] // NT, 0:DH])

            rstd(NORM0)
            take_h0T(0)
            rstd(NORM0 + 1)
            act.wait_ge(pads_made, 3)
            for i in range(NT):
                take_v(2 * i)
                if i + 1 < NT:
                    if i + 2 < NT:
                        rstd(NORM0 + i + 2)
                    take_h0T(i + 1)
                else:
                    act.wait_ge(chan_tr, 1)
                    act.activation(chan[:, 0:CHANNEL_ROWS], ps[:, 3, 0:CHANNEL_ROWS], ACT.Copy).then_inc(chan_ready, 1)
                take_v(2 * i + 1)
            for n in range(2 * NT, H * NT):
                take_v(n)
            act.wait_ge(if_done, 2)
            act.wait_ge(small_landed, 16 * 7)
            step(act.activation(t0_row, ps[F_AT:F_AT + H, 3, :], ACT.Abs, bias=gate_b[F_AT:F_AT + H, 1:2]))
            step(act.activation(t0_row, t0_row, ACT.Exp, scale=-1.0))
            act.activation(t0_row, t0_row, ACT.Ln, bias=1.0).then_inc(log_ready, 1)
            for g in range(PG):
                take(("p", g), pT[:, g, PAD:PST])
            act.wait_ge(tot_ready, 1)
            act.activation(em_row, em_row, ACT.Exp, scale=-1.0).then_inc(em_ready, 1)

            def silu(c):
                act.wait_ge(conv_ready, c + 1)
                act.activation(ucT[:, c, :], ucT[:, c, :], ACT.Silu).then_inc(silu_ready, 1)

            for c in range(MC):
                take(("u", c), uT[:, c, CPAD:CPAD + S])
                if c >= 1:
                    silu(c - 1)
            silu(MC - 1)

            def head_qk(h):
                for e in range(EC):
                    take(("qk", 2 * EC * h + e), qT[:, e, :], scale=float(DH) ** -0.5)
                for e in range(EC):
                    take(("qk", 2 * EC * h + EC + e), kT[:, e, :])

            def head_exp(h):
                for j in range(NT):
                    act.wait_ge(arg_ready, NT * h + j + 1)
                    w = wtmp[:, W_AT[j]:W_AT[j] + S - P * j]
                    act.activation(w, w, ACT.Exp, scale=-1.0).then_inc(w_ready, 1)

            def take_tr(h):
                for c in range(EC):
                    take(("tr", EC * h + c), hnT[:, EC * h + c, 0:S])

            act.wait_ge(pooled_ready, PG)
            act.wait_ge(mix_done, PG)
            head_qk(0)
            head_exp(0)
            for h in range(H):
                if h + 1 < H:
                    head_qk(h + 1)
                    head_exp(h + 1)
                if h >= 1:
                    take_tr(h - 1)
                for c in range(EC):
                    if h >= 1:
                        act.wait_ge(hout_ready, EC * (h - 1) + c + 1)
                    take(("o", EC * h + c), sig_o[c], ACT.Sigmoid)
                act.wait_ge(var_ready, NORM_H + h + 1)
                step(act.activation(rstd_all, var_all, ACT.Ln))
                act.activation(rstd_all, rstd_all, ACT.Exp, scale=-0.5).then_inc(rstd_ready, 1)
            take_tr(H - 1)
            for m in range(KD):
                act.wait_ge(gate_done, m + 1)
                if m < 2:
                    act.wait_ge(hout_ready, MC)
                else:
                    act.wait_ge(merged_ready, m - 1)
                b = 2 if m % 2 == 0 else 6
                act.activation(sig[:, m % 2, :], ps[:, b:b + 2, :].rearrange("p b t -> p (b t)"), ACT.Sigmoid).then_inc(gate_ready, 1)
            for i in range(NT):
                rstd(NORM1 + i)
                act.wait_ge(x1_ready, i + 1)
                act.dma_start(x1_dram[P * i:P * (i + 1), :], X0v[:, i, :]).then_inc(x1_stored, 16)
                act.wait_ge(x1_tr, i + 1)
                if i >= 2:
                    act.wait_ge(logits_done, i - 1)
                act.activation(x1T[i % 2], ps[:, 0:2, :].rearrange("p b (c t) -> p (b c) t", t=P), ACT.Copy).then_inc(x1T_ready, 1)
            act.wait_ge(dist_ready, 1)
            act.activation(gatew[:], gatew[:], ACT.Exp).then_inc(router_exp, 1)

            act.wait_ge(iter_ready, 1)
            act.dma_start(gain[:], A["ln2_g"].broadcast_to([P, D])).then_inc(ln2_landed, 16)
            act.dma_start(bias[:], A["ln2_b"].broadcast_to([P, D])).then_inc(ln2_landed, 16)
            n_it = act.snap(act.value_load(more_iter[0:1, 0:1], min_val=0, max_val=(ROUNDS - 1) * E) + E)

            def take_xT(it1):
                act.wait_ge(x_tr, it1)
                act.activation(xT.rearrange("p c b t -> p c t b"), ps[:, 6:8, :].rearrange("p a (c t b) -> p (a c) t b", t=TB, b=NB), ACT.Copy).then_inc(xT_ready, 1)

            def take_actT(it):
                act.wait_ge(act_tr, it)
                act.activation(rest[:, HID_AT + 4 * HID_COLS:Y_AT], ps[:, 6:8, :].rearrange("p b t -> p (b t)"), ACT.Copy).then_inc(actT_ready, 1)

            def glu_sigmoid(it1):
                act.wait_ge(glu_ready, it1)
                act.activation(sS, gS, ACT.Sigmoid, scale=GLU_ALPHA).then_inc(sig_ready, 1)

            def load_b1(e):
                act.dma_start(b1_row[0:1, :], A["b_e1"][0, bass.ds(e, 1), :]).then_inc(b1_landed, 16)

            def load_b2(e):
                act.dma_start(b2_row[0:1, :], A["b_e2"][0, bass.ds(e, 1), :]).then_inc(b2_landed, 16)

            act.wait_ge(bias_zeroed, 1)
            load_b1(0)
            take_xT(1)
            act.wait_ge(w1_used, 1)
            load_b1(1)
            take_xT(2)
            glu_sigmoid(1)
            take_actT(1)
            act.wait_ge(x1_stored, 16 * NT)
            act.activation(X0[:], X0[:], ACT.Copy, scale=DEEP_ALPHA).then_inc(x1_scaled, 1)
            with act.Fori(1, n_it) as it:
                act.wait_ge(y_ready, it)
                load_b2(act.snap((it - 1) % E))
                take_xT(it + 2)
                glu_sigmoid(it + 1)
                load_b1(act.snap((it + 1) % E))
                take_actT(it + 1)
            act.wait_ge(y_ready, n_it)
            load_b2(E - 1)
            act.wait_ge(b1_landed, n_it * 16 + 16)
            act.wait_ge(w2_used, n_it * (KF // 2))
            act.wait_ge(y_stored, n_it * (16 * NB))
            for i in range(NT):
                act.dma_start(yg[:, i], y_dram[P * i:P * (i + 1)]).then_inc(yg_landed[i], 16)
            for i in range(NT):
                rstd(NORM2 + i)

        @block.vector
        def _(dve):
            n_step = [0]

            def step(ins):
                n_step[0] += 1
                ins.then_inc(dve_step, 1)
                dve.wait_ge(dve_step, n_step[0])

            n_norm = [0]

            def piece_statistics(n, a, src):
                s0 = 16 * (n % 4)
                step(nc.vector.bn_stats(stat[:, s0 + 6 * a:s0 + 6 * a + 6], src))

            def close_statistics(n, pieces):
                s0 = 16 * (n % 4)
                step(nc.vector.bn_aggr(stat[:, s0 + 12:s0 + 14], stat[:, s0:s0 + 6 * pieces]))
                nc.vector.tensor_scalar(stat[:, s0 + 13:s0 + 14], stat[:, s0 + 13:s0 + 14], LN_EPS, None, ALU.add).then_inc(var_ready, 1)

            def statistics(n, src, width):
                pieces = max(1, width // BANK)
                w = width // pieces
                for a in range(pieces):
                    piece_statistics(n, a, src[:, w * a:w * (a + 1)])
                close_statistics(n, pieces)

            def newton(n):
                s0 = 16 * (n % 4)
                var, y, q = stat[:, s0 + 13:s0 + 14], stat[:, s0 + 14:s0 + 15], stat[:, s0 + 15:s0 + 16]
                dve.wait_ge(rstd_ready, n + 1)
                step(nc.vector.scalar_tensor_tensor(out=q, in0=y, scalar=var, in1=y, op0=ALU.mult, op1=ALU.mult))
                step(nc.vector.tensor_scalar(q, q, -0.5, 1.5, ALU.mult, ALU.add))
                step(nc.vector.tensor_tensor(y, y, q, ALU.mult))
                return y

            def layer_norm_center(n, t):
                s0 = 16 * (n % 4)
                step(nc.vector.scalar_tensor_tensor(out=t, in0=t, scalar=stat[:, s0 + 12:s0 + 13], in1=gain[:], op0=ALU.subtract, op1=ALU.mult))

            def layer_norm_scale(n, t, done):
                y = newton(n)
                nc.vector.scalar_tensor_tensor(out=t, in0=t, scalar=y, in1=bias[:], op0=ALU.mult, op1=ALU.add).then_inc(done, 1)

            for i in range(NT):
                dve.wait_ge(x_landed[i], 16)
                t = X0v[:, i, :]
                statistics(NORM0 + i, t, D)
                if i == 0:
                    dve.wait_ge(ln_landed, 32)
                layer_norm_center(NORM0 + i, t)
                layer_norm_scale(NORM0 + i, t, h0_ready)

            dve.wait_ge(if_done, 2)
            dve.wait_ge(small_landed, 16 * 7)
            dve.wait_ge(log_ready, 1)
            step(nc.vector.tensor_scalar(t1_row, ps[F_AT:F_AT + H, 3, :], gate_b[F_AT:F_AT + H, 1:2], 0.0, ALU.add, ALU.min))
            step(nc.vector.tensor_tensor(t1_row, t1_row, t0_row, ALU.subtract))
            dve.wait_ge(consts_made, 2)
            step(nc.vector.tensor_tensor_scan(f_row, ones[F_AT:F_AT + H, 0:S], t1_row, 0.0, ALU.mult, ALU.add))
            step(nc.vector.scalar_tensor_tensor(out=a_row, in0=ps[0:H, 2, :], scalar=gate_b[0:H, 0:1], in1=f_row, op0=ALU.add, op1=ALU.subtract))
            step(nc.vector.tensor_tensor_scan(m_row, ones[0:H, 0:S], a_row, 0.0, ALU.mult, ALU.max))
            nc.vector.tensor_tensor(em_row, f_row, m_row, ALU.add).then_inc(tot_ready, 1)

            dve.wait_ge(chan_ready, 1)
            r_b, r_g, r_bp, r_ls = TAPS * MC, (TAPS + 1) * MC, (TAPS + 2) * MC, (TAPS + 2) * MC + PG
            for c in range(MC):
                dve.wait_ge(gemm_out, at[("u", c)] + 1)
                for j in range(TAPS):
                    src = uT[:, c, j:j + S]
                    tap = chan[:, MC * j + c:MC * j + c + 1]
                    if j == 0:
                        step(nc.vector.tensor_scalar(ucT[:, c, :], src, tap, chan[:, r_b + c:r_b + c + 1], ALU.mult, ALU.add))
                        continue
                    ins = nc.vector.scalar_tensor_tensor(out=ucT[:, c, :], in0=src, scalar=tap, in1=ucT[:, c, :], op0=ALU.mult, op1=ALU.add)
                    if j == TAPS - 1:
                        ins.then_inc(conv_ready, 1)
                    else:
                        step(ins)
            dve.wait_ge(rows_tr, 1)
            nc.vector.tensor_copy(cols[:], ps[:, 2, 0:NT * 2 * H]).then_inc(cols_ready, 1)
            for g in range(PG):
                dve.wait_ge(mix_done, g + 1)
                nc.vector.tensor_scalar(mixT[:, g, :], ps[:, 4 + g, :], chan[:, r_bp + g:r_bp + g + 1], chan[:, r_ls + g:r_ls + g + 1],
                                        ALU.add, ALU.mult).then_inc(mixT_ready, 1)

            dve.wait_ge(cols_ready, 1)

            def head_args(h):
                dve.wait_ge(mb_done, h + 1)
                for j in range(NT):
                    if h >= 1:
                        dve.wait_ge(p_ready, NT * (h - 1) + j + 1)
                    nc.vector.tensor_scalar(wtmp[:, W_AT[j]:W_AT[j] + S - P * j], ps[:, 5, P * j:S], colv[:, j, h:h + 1], 0.0,
                                            ALU.subtract, ALU.max).then_inc(arg_ready, 1)

            def head_p(h):
                if h >= 2:
                    dve.wait_ge(pv_done, NT * (h - 1))
                dve.wait_ge(sc_done, h + 1)
                for j in range(NT):
                    dve.wait_ge(w_ready, NT * h + j + 1)
                    w = wtmp[:, W_AT[j]:W_AT[j] + S - P * j]
                    step(nc.vector.tensor_tensor(w[:, 0:P], w[:, 0:P], tri[:], ALU.mult))
                    b, c0 = S_AT[j]
                    nc.vector.tensor_tensor(Pm[h % 2][:, j, P * j:S], ps[:, b, c0:c0 + S - P * j], w, ALU.mult).then_inc(p_ready, 1)

            def head_norm(h):
                for i in range(NT):
                    n = NT * h + i
                    dve.wait_ge(pv_done, n + 1)
                    acc_ps = ps[:, 6 + n % 2, 0:VW]
                    step(nc.vector.tensor_scalar(stat[:, 64:65], acc_ps[:, DH:VW], -1.0, colv[:, i, H + h:H + h + 1], ALU.mult, ALU.max))
                    step(nc.vector.tensor_tensor(stat[:, 64:65], acc_ps[:, DH:VW], stat[:, 64:65], ALU.max))
                    step(nc.vector.reciprocal(stat[:, 65:66], stat[:, 64:65]))
                    if h >= 1 and i == 0:
                        dve.wait_ge(gemm_done, at[("tr", EC * h - 1)] + 1)
                    nc.vector.tensor_scalar(hnv[:, i, :], acc_ps[:, 0:DH], stat[:, 65:66], None, ALU.mult).then_inc(num_read, 1)
                    dve.wait_ge(num_read, n + 1)
                    step(nc.vector.bn_stats(tile_stats[:, i, 0:6], hnv[:, i, :]))
                    step(nc.vector.bn_aggr(tile_stats[:, i, 12:14], tile_stats[:, i, 0:6]))
                nc.vector.tensor_scalar(var_all, var_all, LN_EPS, None, ALU.add).then_inc(var_ready, 1)
                dve.wait_ge(rstd_ready, NORM_H + h + 1)
                step(nc.vector.tensor_tensor(newton_all, rstd_all, rstd_all, ALU.mult))
                step(nc.vector.tensor_tensor(newton_all, newton_all, var_all, ALU.mult))
                step(nc.vector.tensor_scalar(newton_all, newton_all, -0.5, 1.5, ALU.mult, ALU.add))
                step(nc.vector.tensor_tensor(rstd_all, rstd_all, newton_all, ALU.mult))
                for i in range(NT):
                    nc.vector.tensor_scalar(hnv[:, i, :], hnv[:, i, :], tile_stats[:, i, 12:13], tile_stats[:, i, 14:15],
                                            ALU.subtract, ALU.mult).then_inc(hn_ready, 1)

            def head_out(h):
                for c in range(EC):
                    m = EC * h + c
                    dve.wait_ge(gemm_out, at[("tr", m)] + 1)
                    dve.wait_ge(gemm_out, at[("o", m)] + 1)
                    nc.vector.scalar_tensor_tensor(out=hnT[:, m, 0:S], in0=hnT[:, m, 0:S], scalar=chan[:, r_g + m:r_g + m + 1],
                                                   in1=sig_o[c], op0=ALU.mult, op1=ALU.mult).then_inc(hout_ready, 1)

            head_args(0)
            head_p(0)
            for h in range(H):
                if h + 1 < H:
                    head_args(h + 1)
                    head_p(h + 1)
                if h >= 1:
                    head_out(h - 1)
                head_norm(h)
            head_out(H - 1)

            for m in range(KD):
                dve.wait_ge(gate_ready, m + 1)
                dve.wait_ge(y_done, m + 1)
                b = 4 if m % 2 == 0 else 0
                g = sig[:, m % 2, :]
                step(nc.vector.tensor_tensor(g, g, ps[:, b:b + 2, :].rearrange("p b t -> p (b t)"), ALU.mult))
                nc.vector.tensor_tensor(mergedT[:, m, :], g[:, 0:S], g[:, BANK:BANK + S], ALU.add).then_inc(merged_ready, 1)

            topv, topiv, tf, gw = cut(top, 0, NT, 8), cut(topi, 0, NT, 8), cut(topf, 0, NT, TOPK), cut(gatew, 0, NT, TOPK)
            oh = cut(onehot, 0, NT, TOPK, E)
            experts = iota_e[:].rearrange("p (a e) -> p a e", a=1)

            def top_experts(i):
                lg = logits[:, E * i:E * (i + 1)]
                dve.wait_ge(logits_done, i + 1)
                step(nc.vector.tensor_tensor(lg, ps[:, 6, E * i:E * (i + 1)], br[:], ALU.add))
                step(nc.vector.max(topv[:, i, :], lg))
                step(nc.vector.max_index(topiv[:, i, :], topv[:, i, :], lg))
                step(nc.vector.tensor_copy(tf[:, i, :], topiv[:, i, 0:TOPK]))
                step(nc.vector.tensor_tensor(oh[:, i], experts.broadcast_to([P, TOPK, E]),
                                             tf[:, i, :].rearrange("p (k a) -> p k a", a=1).broadcast_to([P, TOPK, E]), ALU.is_equal))
                nc.vector.tensor_reduce(mask[:, E * i:E * (i + 1)].rearrange("p (e a) -> p e a", a=1), oh[:, i].rearrange("p k e -> p e k"),
                                        X_AXIS, ALU.add).then_inc(mask_ready, 1)

            def places(i):
                dve.wait_ge(rank_done, i + 1)
                rk, rt, ri = (v[:, E * i:E * (i + 1)] for v in (rank, rtmp, rint))
                rp = ps[:, 7, E * i:E * (i + 1)]
                step(nc.vector.tensor_scalar(ri, rp, 1.0 / TB, 0.5 / TB - 0.5, ALU.mult, ALU.add))
                step(nc.vector.tensor_scalar(rt, ri, float(1 - NB * TB), None, ALU.mult))
                step(nc.vector.scalar_tensor_tensor(out=rk, in0=rp, scalar=float(NB), in1=rt, op0=ALU.mult, op1=ALU.add))
                nc.vector.tensor_scalar(ri, rp, 1.0 / CAP, 0.5 / CAP - 0.5, ALU.mult, ALU.add).then_inc(rank_read, 1)
                dve.wait_ge(rank_read, i + 1)
                step(nc.vector.tensor_copy(rt, ri))
                step(nc.vector.scalar_tensor_tensor(out=rk, in0=rt, scalar=float(-NB), in1=rk, op0=ALU.mult, op1=ALU.add))
                step(nc.vector.scalar_tensor_tensor(out=rt, in0=rt, scalar=float(E), in1=iota_e[:], op0=ALU.mult, op1=ALU.add))
                for what, into in ((rk, place), (rt, itern)):
                    step(nc.vector.tensor_tensor(chosen, oh[:, i], what.rearrange("p (a e) -> p a e", a=1).broadcast_to([P, TOPK, E]), ALU.mult))
                    step(nc.vector.tensor_reduce(into[:, TOPK * i:TOPK * (i + 1)].rearrange("p (k a) -> p k a", a=1), chosen, X_AXIS, ALU.add))
                if i == 0:
                    dve.wait_ge(dispatch_consts, 1)
                for n in range(TOPK * i, TOPK * (i + 1)):
                    nc.vector.tensor_scalar(place_oh[:, n, :], iota_row, place[:, n:n + 1], None, ALU.is_equal).then_inc(pos_ready, 1)
                    nc.vector.tensor_scalar(iter_oh[:, n, :], iota_row, itern[:, n:n + 1], slot_id[:, n:n + 1], ALU.is_equal, ALU.mult).then_inc(pos_ready, 1)

            def layer_norm_1(i):
                t = X0v[:, i, :]
                for n in range(D // BANK):
                    dve.wait_ge(wo_done, 2 * i + n + 1)
                    half = t[:, BANK * n:BANK * (n + 1)]
                    nc.vector.scalar_tensor_tensor(out=half, in0=half, scalar=DEEP_ALPHA, in1=ps[:, 2 + 2 * (i % 2) + n, :],
                                                   op0=ALU.mult, op1=ALU.add).then_inc(wo_read, 1)
                    dve.wait_ge(wo_read, 2 * i + n + 1)
                    piece_statistics(NORM1 + i, n, half)
                    if n == 0 and i >= 1:
                        top_experts(i - 1)
                close_statistics(NORM1 + i, D // BANK)
                layer_norm_center(NORM1 + i, t)
                layer_norm_scale(NORM1 + i, t, x1_ready)

            dve.wait_ge(ln1_landed, 32)
            dve.wait_ge(router_landed, 32)
            for i in range(NT):
                layer_norm_1(i)
                if i >= 1:
                    places(i - 1)
            top_experts(NT - 1)
            places(NT - 1)
            dve.wait_ge(slots_done, 1)
            nc.vector.tensor_scalar(slots_f, ps[:, 2, 0:N_ITER], float(NO_TOKEN), None, ALU.add).then_inc(slots_read, 1)
            dve.wait_ge(slots_read, 1)
            nc.vector.tensor_scalar(idx_table[:, 0:N_ITER], slots_f, 1.0 / TOPK, -0.375, ALU.mult, ALU.add).then_inc(tables_ready, 1)
            dve.wait_ge(counted, 1)
            step(nc.vector.tensor_reduce(cnt[:, E:E + 1], ps[:, 3, 0:E], X_AXIS, ALU.max))
            step(nc.vector.memset(cnt[:, E + 1:E + 2], 0.0))
            for r in range(1, ROUNDS):
                step(nc.vector.tensor_scalar(cnt[:, E + 2:E + 3], cnt[:, E:E + 1], float(CAP * r), float(E), ALU.is_gt, ALU.mult))
                step(nc.vector.tensor_tensor(cnt[:, E + 1:E + 2], cnt[:, E + 1:E + 2], cnt[:, E + 2:E + 3], ALU.add))
            blocksv = cut(blocks, 0, ROUNDS, E)
            for r in range(ROUNDS):
                step(nc.vector.tensor_scalar(blocksv[0:1, r, :], ps[0:1, 3, 0:E], 1.0 / TB, (0.5 * (TB - 1) - CAP * r) / TB, ALU.mult, ALU.add))
            step(nc.vector.tensor_scalar(blocks[0:1, :], blocks[0:1, :], 1.0, float(NB), ALU.max, ALU.min))
            nc.vector.tensor_copy(more_iter[0:1, :], cnt[0:1, E + 1:E + 2]).then_inc(iter_ready, 1)
            dve.wait_ge(spread_done, 1)
            nc.vector.tensor_scalar(slot_table.rearrange("p (n b) -> p b n", b=NB), ps[:, 5, :].rearrange("p (b n) -> p b n", b=NB),
                                    float(CG), quarter[:, 0:1], ALU.mult, ALU.add).then_inc(tables_ready, 1)
            nc.vector.tensor_tensor(gw, topv[:, :, 0:TOPK], topv[:, :, 0:1].broadcast_to([P, NT, TOPK]), ALU.subtract).then_inc(dist_ready, 1)
            dve.wait_ge(router_exp, 1)
            gs = cut(gsum, 0, NT, 1)
            step(nc.vector.tensor_reduce(gs, gw, X_AXIS, ALU.add))
            step(nc.vector.reciprocal(gs, gs))
            step(nc.vector.tensor_tensor(gw, gw, gs.broadcast_to([P, NT, TOPK]), ALU.mult))
            dve.wait_ge(iter_ready, 1)
            n_it = dve.snap(dve.value_load(more_iter[0:1, 0:1], min_val=0, max_val=(ROUNDS - 1) * E) + E)

            def swiglu(it1, first=False):
                dve.wait_ge(w1_used, it1 * KD)
                pair = ps[:, 0:NB, :].rearrange("p b (n two) -> p b n two", two=2)
                nc.vector.tensor_scalar(gS, pair[:, :, :, 0], GLU_LIMIT, None, ALU.min).then_inc(glu_ready, 1)
                nc.vector.tensor_scalar(lS, pair[:, :, :, 1], GLU_LIMIT, -GLU_LIMIT, ALU.min, ALU.max).then_inc(h_read, 1)
                dve.wait_ge(h_read, it1)
                nc.vector.scalar_tensor_tensor(out=lS, in0=lS, scalar=1.0, in1=gS, op0=ALU.add, op1=ALU.mult).then_inc(lin_ready, 1)
                dve.wait_ge(lin_ready, it1)
                dve.wait_ge(sig_ready, it1)
                if not first:
                    dve.wait_ge(act_tr, it1 - 1)
                nc.vector.tensor_tensor(aS.rearrange("p b a n -> p b (a n)"), lS, sS, ALU.mult).then_inc(act_ready, 1)

            def take_y(it, first=False):
                dve.wait_ge(w2_used, it * (KF // 2))
                if not first:
                    dve.wait_ge(y_stored, 16 * NB * it - 16 * NB)
                nc.vector.tensor_copy(rest[:, Y_AT:Y_AT + NB * YW], ps[:, 4:6, :].rearrange("p a n -> p (a n)")).then_inc(y_ready, 1)

            nc.vector.memset(stat[:, 66:67], 0.0).then_inc(y_ready, 1)
            for n in range(TOPK * NT):
                i, k = n // TOPK, n % TOPK
                nc.vector.tensor_scalar(gate_diag[:, n, :], ident[:], gw[:, i, k:k + 1], None, ALU.mult).then_inc(diags_ready, 1)
            swiglu(1, first=True)
            swiglu(2)
            take_y(1, first=True)
            with dve.Fori(2, n_it) as it:
                swiglu(it + 1)
                take_y(it)
            take_y(n_it)

            dve.wait_ge(ln2_landed, 32)
            for i in range(NT):
                t = X0v[:, i, :]
                dve.wait_ge(fourth_added, i + 1)
                for n in range(D // BANK):
                    dve.wait_ge(combined, 2 * i + n + 1)
                    half = t[:, BANK * n:BANK * (n + 1)]
                    nc.vector.tensor_tensor(half, half, ps[:, 2 * (i % 2) + n, :], ALU.add).then_inc(combined_read, 1)
                    dve.wait_ge(combined_read, 2 * i + n + 1)
                    piece_statistics(NORM2 + i, n, half)
                close_statistics(NORM2 + i, D // BANK)
                if i >= 1:
                    layer_norm_scale(NORM2 + i - 1, X0v[:, i - 1, :], out_ready)
                layer_norm_center(NORM2 + i, t)
            layer_norm_scale(NORM2 + NT - 1, X0v[:, NT - 1, :], out_ready)

        @block.tensor
        def _(pe):
            mm = nc.tensor.matmul
            pe.wait_ge(consts_made, 2)
            def bank_for(n):
                if n >= 2:
                    pe.wait_ge(gemm_out, n - 1)
                return n % 2

            def h0_transposes(i):
                pe.wait_ge(h0_ready, i + 1)
                if i >= 2:
                    pe.wait_ge(h0T_ready, i - 1)
                b = 4 + 2 * (i % 2)
                for k in range(KD):
                    last = nc.tensor.transpose(ps[:, b + k // 4, P * (k % 4):P * (k % 4 + 1)], X0v[:, i, P * k:P * (k + 1)], ident[:])
                last.then_inc(h0_tr, 1)

            def v_product(n):
                i, h = V_ORDER[n] % NT, V_ORDER[n] // NT
                pe.wait_ge(ring_landed[h], 16)
                b = bank_for(n)
                for k in range(KD):
                    last = mm(ps[:, b, 0:DH], h0T[:, k, P * i:P * (i + 1)], ring[:, h, k, :], start=(k == 0), stop=(k == KD - 1))
                last.then_inc(gemm_done, 1)

            h0_transposes(0)
            for i in range(NT):
                pe.wait_ge(h0T_ready, i + 1)
                v_product(2 * i)
                if i + 1 < NT:
                    h0_transposes(i + 1)
                else:
                    pe.wait_ge(small_landed, 16 * 7)
                    nc.tensor.transpose(ps[:, 3, 0:CHANNEL_ROWS], chan_rows[0:CHANNEL_ROWS, :], ident[0:CHANNEL_ROWS, 0:CHANNEL_ROWS]).then_inc(chan_tr, 1)
                v_product(2 * i + 1)
            for n in range(2 * NT, H * NT):
                v_product(n)
            pe.wait_ge(wif_landed, 16)
            pe.wait_ge(chan_ready, 1)
            wifv = cut(wif, 0, KD, 2 * H)
            for k in range(KD):
                for j in range(2):
                    last = mm(ps[F_AT * j:F_AT * j + H, 2 + j, :], wifv[:, k, H * j:H * (j + 1)], h0T[:, k, :], start=(k == 0), stop=(k == KD - 1))
                    if k == KD - 1:
                        last.then_inc(if_done, 1)

            n_out = H * NT
            for n in range(H, H + PW // PANEL + MW // PANEL):
                pe.wait_ge(ring_landed[n % RING], 16 * (n // RING + 1))
                slot = ring[:, n % RING]
                for c in range(2):
                    b = bank_for(n_out)
                    for k in range(KD):
                        last = mm(ps[:, b, :], slot[:, k, P * c:P * (c + 1)], h0T[:, k, :], start=(k == 0), stop=(k == KD - 1))
                    last.then_inc(gemm_done, 1)
                    n_out += 1
                if n == H + PW // PANEL + MW // PANEL - 1:
                    pe.wait_ge(tot_ready, 1)
                    pe.wait_ge(em_ready, 1)
                    for i in range(NT):
                        for j, r in enumerate((a_row, em_row)):
                            last = nc.tensor.transpose(ps[:, 2, 2 * H * i + H * j:2 * H * i + H * (j + 1)], r[:, P * i:P * (i + 1)], ident[0:H, 0:H])
                    last.then_inc(rows_tr, 1)
                    pe.wait_ge(wpool_landed, 16)
                    wpv = cut(wpool, 0, PG, PGD)
                    for g in range(PG):
                        pe.wait_ge(pooled_ready, g + 1)
                        mm(ps[:, 4 + g, :], wpv[:, g, :], pool_w[:, g, :], start=True, stop=True).then_inc(mix_done, 1)

            def head_qk(h):
                if h == 0:
                    pe.wait_ge(wqk_landed, 16 * 2 * H)
                pe.wait_ge(silu_ready, EC * (h + 1))
                n = at[("qk", 2 * EC * h)]
                for j in range(2):
                    for e in range(EC):
                        b = bank_for(n)
                        for c in range(EC):
                            last = mm(ps[:, b, :], wqk[:, 2 * h + j, c, P * e:P * (e + 1)], ucT[:, EC * h + c, :], start=(c == 0), stop=(c == EC - 1))
                        last.then_inc(gemm_done, 1)
                        n += 1
                if h >= 1:
                    pe.wait_ge(arg_ready, NT * h)
                else:
                    pe.wait_ge(mixT_ready, PG)
                mm(ps[:, 5, :], cut(head_sel, 0, H, P)[0:H, h, :], m_row, start=True, stop=True).then_inc(mb_done, 1)
                pe.wait_ge(gemm_out, n)
                if h >= 1:
                    pe.wait_ge(p_ready, NT * h)
                else:
                    pe.wait_ge(cols_ready, 1)
                for j in range(NT):
                    b, c0 = S_AT[j]
                    for e in range(EC):
                        last = mm(ps[:, b, c0:c0 + S - P * j], kT[:, e, P * j:P * (j + 1)], qT[:, e, P * j:S], start=(e == 0), stop=(e == EC - 1))
                last.then_inc(sc_done, 1)

            def head_pv(h):
                for i in range(NT):
                    n = NT * h + i
                    pe.wait_ge(p_ready, n + 1)
                    if n >= 2:
                        pe.wait_ge(num_read, n - 1)
                    for j in range(i + 1):
                        last = mm(ps[:, 6 + n % 2, 0:VW], Pm[h % 2][:, j, P * i:P * (i + 1)], v_sb[:, j, h, :], start=(j == 0), stop=(j == i))
                    last.then_inc(pv_done, 1)

            def head_tr(h):
                pe.wait_ge(hn_ready, NT * (h + 1))
                for c in range(EC):
                    b = bank_for(at[("tr", EC * h + c)])
                    for i in range(NT):
                        last = nc.tensor.transpose(ps[:, b, P * i:P * (i + 1)], hnv[:, i, P * c:P * (c + 1)], ident[:])
                    last.then_inc(gemm_done, 1)

            def branch_gates(m):
                gb = 2 if m % 2 == 0 else 6
                pe.wait_ge(merge_landed[m % 2], 64 * (m // 2 + 1))
                if m >= 2:
                    pe.wait_ge(merged_ready, m - 1)
                if m == 1:
                    pe.wait_ge(num_read, H * NT)
                if m == 0:
                    pe.wait_ge(p_ready, H * NT)
                for j in range(2):
                    for k in range(KD):
                        last = mm(ps[:, gb + j, :], merge_w[m % 2][:, KD * j + k, :], h0T[:, k, :], start=(k == 0), stop=(k == KD - 1))
                last.then_inc(gate_done, 1)

            def pool_product(m):
                if m == 0:
                    pe.wait_ge(mixT_ready, PG)
                    pe.wait_ge(p_ready, H * NT)
                for k in range(PG):
                    mm(ps[:, 4 if m % 2 == 0 else 0, :], merge_w[m % 2][:, 2 * KD + k, :], mixT[:, k, :], start=(k == 0), stop=(k == PG - 1))

            def mlstm_product(m):
                if m == 0:
                    pe.wait_ge(hout_ready, MC)
                for k in range(MC):
                    last = mm(ps[:, 5 if m % 2 == 0 else 1, :], merge_w[m % 2][:, 2 * KD + PG + k, :], hnT[:, k, 0:S], start=(k == 0), stop=(k == MC - 1))
                last.then_inc(y_done, 1)

            head_qk(0)
            for h in range(H):
                if h + 1 < H:
                    head_qk(h + 1)
                else:
                    branch_gates(0)
                if h >= 1:
                    head_tr(h - 1)
                n = PW // PANEL + MW // PANEL + H + h
                pe.wait_ge(ring_landed[n % RING], 16 * (n // RING + 1))
                for c in range(EC):
                    b = bank_for(at[("o", EC * h + c)])
                    for k in range(KD):
                        last = mm(ps[:, b, :], ring[:, n % RING][:, k, P * c:P * (c + 1)], h0T[:, k, :], start=(k == 0), stop=(k == KD - 1))
                    last.then_inc(gemm_done, 1)
                head_pv(h)

            pool_product(0)
            branch_gates(1)
            head_tr(H - 1)
            mlstm_product(0)
            pe.wait_ge(gemm_out, len(order))
            pool_product(1)
            mlstm_product(1)
            for m in range(2, KD):
                branch_gates(m)
                pool_product(m)
                mlstm_product(m)

            mk = cut(mask, 0, NT, E)

            def w_out_product(i, n, logits_of=None):
                if i >= 2:
                    pe.wait_ge(wo_read, 2 * (i - 2) + n + 1)
                for k in range(KD):
                    if k == KD // 2 and logits_of is not None:
                        router_logits(logits_of)
                    if i == 0 and n == 0:
                        pe.wait_ge(merged_ready, k + 1)
                    last = mm(ps[:, 2 + 2 * (i % 2) + n, :], mergedT[:, k, P * i:P * (i + 1)], wout[:, k, BANK * n:BANK * (n + 1)], start=(k == 0), stop=(k == KD - 1))
                last.then_inc(wo_done, 1)

            def x1_transposes(i):
                pe.wait_ge(x1_ready, i + 1)
                if i >= 1:
                    pe.wait_ge(x1T_ready, i)
                for k in range(KD):
                    last = nc.tensor.transpose(ps[:, k // 4, P * (k % 4):P * (k % 4 + 1)], X0v[:, i, P * k:P * (k + 1)], ident[:])
                last.then_inc(x1_tr, 1)

            def router_logits(i):
                pe.wait_ge(x1T_ready, i + 1)
                if i >= 1:
                    pe.wait_ge(mask_ready, i)
                for k in range(KD):
                    last = mm(ps[:, 6, E * i:E * (i + 1)], x1T[i % 2][:, k, :], wrv[:, k, :], start=(k == 0), stop=(k == KD - 1))
                last.then_inc(logits_done, 1)

            def ranks(i):
                pe.wait_ge(mask_ready, i + 1)
                if i >= 1:
                    pe.wait_ge(rank_read, i)
                for j in range(i + 1):
                    last = mm(ps[:, 7, E * i:E * (i + 1)], tri_strict[:] if j == i else ones[:, 0:P], mk[:, j, :], start=(j == 0), stop=(j == i))
                last.then_inc(rank_done, 1)

            def slots(i):
                for n in range(TOPK * i, TOPK * (i + 1)):
                    pe.wait_ge(pos_ready, 2 * n + 2)
                    last = mm(ps[:, 2, 0:N_ITER], place_oh[:, n, :], iter_oh[:, n, :], start=(n == 0), stop=(n == TOPK * NT - 1))
                return last

            pe.wait_ge(wout_landed, 16)
            pe.wait_ge(router_landed, 32)
            pe.wait_ge(gate_ready, KD - 1)
            for i in range(NT):
                w_out_product(i, 0)
                if i >= 1:
                    x1_transposes(i - 1)
                w_out_product(i, 1, logits_of=i - 1 if i >= 1 else None)
                if i >= 1:
                    ranks(i - 1)
            for i in range(NT - 2):
                slots(i)
            x1_transposes(NT - 1)
            router_logits(NT - 1)
            ranks(NT - 1)
            slots(NT - 2)
            for j in range(NT):
                last = mm(ps[:, 3, 0:E], ones[:, 0:P], mk[:, j, :], start=(j == 0), stop=(j == NT - 1))
            last.then_inc(counted, 1)
            slots(NT - 1).then_inc(slots_done, 1)
            pe.wait_ge(slots_read, 1)
            sv = cut(P1, SPREAD_AT, NB, P)
            for b in range(NB):
                last = mm(ps[:, 5, N_ITER * b:N_ITER * (b + 1)], sv[:, b, :], slots_f, start=True, stop=True)
            last.then_inc(spread_done, 1)

            def x_transposes(it1):
                pe.wait_ge(xg_landed, 16 * it1)
                for k in range(KD):
                    last = nc.tensor.transpose(ps[:, 6 + k // 4, P * (k % 4):P * (k % 4 + 1)], xg[:, P * k:P * (k + 1)], ident[:])
                last.then_inc(x_tr, 1)

            def fc1(it1, nb):
                pe.wait_ge(b1_landed, 16 * it1)
                for b in range(nb):
                    for g in range(CG):
                        mm(ps[TB * g:TB * (g + 1), b, :], bias_sel, b1_row[:, HW_ * g:HW_ * (g + 1)], start=True, stop=False)
                for k in range(KD):
                    pe.wait_ge(w1_landed[k], 16 * it1)
                    for b in range(nb):
                        for g in range(CG):
                            last = mm(ps[TB * g:TB * (g + 1), b, :], xT[:, k, b, :], W1[:, k, HW_ * g:HW_ * (g + 1)],
                                      start=False, stop=(k == KD - 1))
                    last.then_inc(w1_used, 1)

            def act_transposes(it):
                pe.wait_ge(act_ready, it)
                for b in range(NB):
                    for a in range(2):
                        last = nc.tensor.transpose(ps[:, 6 + b // 2, P * (2 * (b % 2) + a):P * (2 * (b % 2) + a + 1)], aS[:, b, a, :], ident[:])
                last.then_inc(act_tr, 1)

            def fc2(it, nb):
                pe.wait_ge(b2_landed, 16 * it)
                for b in range(nb):
                    for g in range(CG):
                        mm(ps[TB * g:TB * (g + 1), 4 + b // 2, YW * (b % 2):YW * (b % 2 + 1)], bias_sel, b2_row[:, YW * g:YW * (g + 1)],
                           start=(b % 2 == 0), stop=False, skip_group_check=True)
                for kk in range(KF // 2):
                    pe.wait_ge(w2_landed[kk], 16 * it)
                    for a in range(2):
                        k = 2 * kk + a
                        for b in range(nb):
                            for g in range(CG):
                                last = mm(ps[TB * g:TB * (g + 1), 4 + b // 2, YW * (b % 2):YW * (b % 2 + 1)],
                                          aT[:, b, k % 2, TB * (k // 2):TB * (k // 2 + 1)], W2[:, kk, a, YW * g:YW * (g + 1)],
                                          start=False, stop=(k == KF - 1), skip_group_check=True)
                    last.then_inc(w2_used, 1)

            def by_blocks(product, it, blocks):
                with pe.If(blocks < 3):
                    with pe.If(blocks < 2):
                        product(it, 1)
                    with pe.Else():
                        product(it, 2)
                with pe.Else():
                    with pe.If(blocks < 4):
                        product(it, 3)
                    with pe.Else():
                        product(it, 4)

            def blocks_of(n):
                return pe.value_load(blocks[0:1, bass.ds(n, 1)], min_val=1, max_val=NB)

            pe.wait_ge(iter_ready, 1)
            n_it = pe.snap(pe.value_load(more_iter[0:1, 0:1], min_val=0, max_val=(ROUNDS - 1) * E) + E)
            x_transposes(1)
            pe.wait_ge(xT_ready, 1)
            by_blocks(fc1, 1, blocks_of(0))
            x_transposes(2)
            pe.wait_ge(xT_ready, 2)
            act_transposes(1)
            with pe.Fori(1, n_it) as it:
                pe.wait_ge(h_read, it)
                by_blocks(fc1, it + 1, blocks_of(it))
                pe.wait_ge(actT_ready, it)
                x_transposes(it + 2)
                pe.wait_ge(y_ready, it)
                by_blocks(fc2, it, blocks_of(it - 1))
                pe.wait_ge(xT_ready, it + 2)
                act_transposes(it + 1)
            pe.wait_ge(actT_ready, n_it)
            pe.wait_ge(y_ready, n_it)
            by_blocks(fc2, n_it, blocks_of(n_it - 1))
            pe.wait_ge(diags_ready, TOPK * NT)
            pe.wait_ge(act_ready, n_it)
            for i in range(NT):
                pe.wait_ge(yg_landed[i], 16)
                for n in range(D // BANK):
                    if i >= 2:
                        pe.wait_ge(combined_read, 2 * (i - 2) + n + 1)
                    for k in range(TOPK - 1):
                        last = mm(ps[:, 2 * (i % 2) + n, :], gate_diag[:, TOPK * i + k, :], yg[:, i, k, BANK * n:BANK * (n + 1)],
                                  start=(k == 0), stop=(k == TOPK - 2))
                    last.then_inc(combined, 1)


NAMES = ["x", "ln0_g", "ln0_b", "w_in", "conv_w", "conv_b", "w_q", "w_k", "b_if", "mh_gain", "w_pool", "b_pool", "ls_pool",
         "w_branch_pool", "w_branch_mlstm", "w_out", "ln1_g", "ln1_b", "w_router", "b_router", "w_e1", "b_e1", "w_e2", "b_e2",
         "ln2_g", "ln2_b"]


def kernel(**inputs):
    import numpy as np
    import concourse.bacc as bacc
    from concourse.bass_utils import run_bass_kernel_spmd

    nc = bacc.Bacc("TRN2", target_bir_lowering=False, num_devices=1)
    arrays, aps = {}, {}
    for name in NAMES:
        a = np.ascontiguousarray(inputs[name])
        arrays[f"in_{name}"] = a
        aps[name] = nc.dram_tensor(f"in_{name}", a.shape, mybir.dt.from_np(a.dtype), kind="ExternalInput").ap()
    shape = inputs["x"].shape
    out = nc.dram_tensor("out_rows", shape, F32, kind="ExternalOutput").ap()
    build_program(nc, aps, out)
    r = run_bass_kernel_spmd(nc, [arrays], core_ids=[0])
    return r.results[0]["out_rows"]
```
